# Optimizing a Trainium2 kernel written in Bass

```python
import math
import jax
import jax.numpy as jnp
from jax import lax
import numpy as np

D_MODEL = 1024
BATCH = 1
SEQ = 256
DEPTH = 2

GRID_W = 64
CTX_LEN = 256
NORM_EPS = 1e-6
ROPE_BASE = 10000.0
DEEPNORM_ALPHA = (2.0 * DEPTH) ** 0.25
DEEPNORM_BETA = (8.0 * DEPTH) ** -0.25

MLA_HEADS = 8
MLA_Q_LORA = 256
MLA_KV_LORA = 128
MLA_NOPE = 64
MLA_ROPE = 32
MLA_V = 64
MLA_SCALE = (MLA_NOPE + MLA_ROPE) ** -0.5

DN_HEADS = 8
DN_HEAD_DIM = 64
DN_WIDTH = DN_HEADS * DN_HEAD_DIM
DN_CONV = 5
DN_CHUNK = 64

GQA_HEADS = 8
GQA_KV_HEADS = 2
GQA_GROUP = GQA_HEADS // GQA_KV_HEADS
GQA_HEAD_DIM = 64
GQA_SCALE = GQA_HEAD_DIM ** -0.5
WINDOW = 128
Q_BLOCK = 128

N_EXPERTS = 64
TOP_K = 8
N_GROUPS = 8
TOPK_GROUPS = 4
EXPERT_DIM = 256
SHARED_DIM = 256
ROUTED_SCALE = 2.5
EXPERT_BLOCK = 128

IN_SIZES = (MLA_Q_LORA, MLA_KV_LORA, MLA_ROPE,
            3 * DN_WIDTH, 2 * DN_HEADS, 2 * DN_HEADS, DN_WIDTH,
            GQA_HEADS * GQA_HEAD_DIM, GQA_KV_HEADS * GQA_HEAD_DIM, GQA_KV_HEADS * GQA_HEAD_DIM,
            3 * D_MODEL)
D_IN = sum(IN_SIZES)

kernel_name = 'hybrid_mla_deltanet_swa_moe_trunk'

def _split(z, sizes):
    return jnp.split(z, np.cumsum(sizes)[:-1].tolist(), axis=-1)

def _layernorm(x, g, b):
    xf = x.astype(jnp.float32)
    mu = jnp.mean(xf, -1, keepdims=True)
    var = jnp.mean(jnp.square(xf - mu), -1, keepdims=True)
    y = (xf - mu) * lax.rsqrt(var + NORM_EPS) * g.astype(jnp.float32) + b.astype(jnp.float32)
    return y.astype(x.dtype)

def _rmsnorm(x, g):
    xf = x.astype(jnp.float32)
    y = xf * lax.rsqrt(jnp.mean(xf * xf, -1, keepdims=True) + NORM_EPS)
    return (y * g.astype(jnp.float32)).astype(x.dtype)

def _l2norm(x):
    xf = x.astype(jnp.float32)
    return xf * lax.rsqrt(jnp.sum(xf * xf, -1, keepdims=True) + 1e-6)

def _axial_angles(n_rows, dim):
    row = jnp.repeat(jnp.arange(n_rows, dtype=jnp.float32), GRID_W)
    col = jnp.tile(jnp.arange(GRID_W, dtype=jnp.float32), n_rows)
    n = dim // 4
    inv = ROPE_BASE ** (-jnp.arange(n, dtype=jnp.float32) / n)
    return jnp.concatenate([row[:, None] * inv, col[:, None] * inv], axis=-1)

def _rope(x, ang):
    shape = (ang.shape[0],) + (1,) * (x.ndim - 3) + (ang.shape[1],)
    cos = jnp.cos(ang).reshape(shape).astype(x.dtype)
    sin = jnp.sin(ang).reshape(shape).astype(x.dtype)
    x1, x2 = jnp.split(x, 2, axis=-1)
    return jnp.concatenate([x1 * cos - x2 * sin, x2 * cos + x1 * sin], axis=-1)

def _blocks(t):
    B, L = t.shape[:2]
    return jnp.moveaxis(t.reshape((B, L // Q_BLOCK, Q_BLOCK) + t.shape[2:]), 1, 0)

def _unblocks(t):
    t = jnp.moveaxis(t, 0, 1)
    return t.reshape((t.shape[0], t.shape[1] * t.shape[2]) + t.shape[3:])

def _mla_project(cq, ckv, kr, ang, q_norm, kv_norm, w_uq, w_ukv):
    B, L, _ = cq.shape
    q = (_rmsnorm(cq, q_norm) @ w_uq).reshape(B, L, MLA_HEADS, MLA_NOPE + MLA_ROPE)
    q_nope, q_rope = q[..., :MLA_NOPE], q[..., MLA_NOPE:]
    kv = (_rmsnorm(ckv, kv_norm) @ w_ukv).reshape(B, L, MLA_HEADS, MLA_NOPE + MLA_V)
    k_nope, v = kv[..., :MLA_NOPE], kv[..., MLA_NOPE:]
    if ang is not None:
        q_rope = _rope(q_rope, ang)
        kr = _rope(kr, ang)
    return q_nope, q_rope, k_nope, kr, v

def _mla_attend(q_nope, q_rope, k_nope, k_rope, v):
    s = (jnp.einsum('bqhd,bkhd->bhqk', q_nope, k_nope)
         + jnp.einsum('bqhr,bkr->bhqk', q_rope, k_rope))
    p = jax.nn.softmax(s.astype(jnp.float32) * MLA_SCALE, axis=-1).astype(v.dtype)
    return jnp.einsum('bhqk,bkhd->bqhd', p, v)

def _short_conv(x, w):
    ch = x.shape[-1]
    y = lax.conv_general_dilated(x, w[:, None, :].astype(x.dtype), window_strides=(1,),
                                 padding=[(DN_CONV // 2, DN_CONV // 2)],
                                 dimension_numbers=('NWC', 'WIO', 'NWC'), feature_group_count=ch)
    return jax.nn.silu(y)

def _dn_prepare(qkv, a, b, conv_w, a_log, dt_bias):
    B, L, _ = qkv.shape
    q, k, v = jnp.split(_short_conv(qkv, conv_w), 3, axis=-1)
    shp = (B, L, DN_HEADS, DN_HEAD_DIM)
    q = _l2norm(q.reshape(shp))
    k = _l2norm(k.reshape(shp))
    v = v.reshape(shp).astype(jnp.float32)
    a = a.astype(jnp.float32).reshape(B, L, 2, DN_HEADS)
    b = b.astype(jnp.float32).reshape(B, L, 2, DN_HEADS)
    g = -jnp.exp(a_log.astype(jnp.float32)) * jax.nn.softplus(a + dt_bias.astype(jnp.float32))
    return q, k, v, g, jax.nn.sigmoid(b)

def _to_chunks(t):
    B, L, H = t.shape[:3]
    t = t.reshape((B, L // DN_CHUNK, DN_CHUNK, H) + t.shape[3:])
    return jnp.moveaxis(t, (1, 3), (0, 2))

def _chunk_gated_delta(q, k, v, g, beta, s0):
    B, L, H, dk = q.shape
    dv = v.shape[-1]
    q, k, v, g, beta = (_to_chunks(t) for t in (q, k, v, g, beta))
    q = q * dk ** -0.5
    gc = jnp.cumsum(g, axis=-1)
    idx = jnp.arange(DN_CHUNK)
    incl = idx[:, None] >= idx[None, :]
    strict = idx[:, None] > idx[None, :]
    decay = jnp.exp(jnp.where(incl, gc[..., :, None] - gc[..., None, :], -jnp.inf))
    kb = k * beta[..., None]
    a_mat = jnp.where(strict, jnp.einsum('nbhid,nbhjd->nbhij', kb, k) * decay, 0.0)
    rhs = jnp.concatenate([v * beta[..., None], kb * jnp.exp(gc)[..., None]], axis=-1)
    sol = lax.linalg.triangular_solve(a_mat + jnp.eye(DN_CHUNK, dtype=a_mat.dtype), rhs,
                                      left_side=True, lower=True, unit_diagonal=True)
    u, w = sol[..., :dv], sol[..., dv:]
    qk = jnp.einsum('nbhid,nbhjd->nbhij', q, k) * decay
    qg = q * jnp.exp(gc)[..., None]
    kg = k * jnp.exp(gc[..., -1:] - gc)[..., None]
    g_last = jnp.exp(gc[..., -1])

    def step(S, xs):
        qg_i, kg_i, u_i, w_i, qk_i, gl_i = xs
        v_new = u_i - jnp.einsum('bhcd,bhde->bhce', w_i, S)
        o = jnp.einsum('bhcd,bhde->bhce', qg_i, S) + jnp.einsum('bhij,bhje->bhie', qk_i, v_new)
        S = S * gl_i[..., None, None] + jnp.einsum('bhcd,bhce->bhde', kg_i, v_new)
        return S, o

    s_fin, o = lax.scan(step, s0, (qg, kg, u, w, qk, g_last))
    o = jnp.moveaxis(o, (0, 2), (1, 3)).reshape(B, L, H, dv)
    return o, s_fin

def _dn_bidirectional(dc, dl):
    qc, kc, vc, gc, bc = dc
    ql, kl, vl, gl, bl = dl
    B, _, H, dk = qc.shape
    s0 = jnp.zeros((B, H, dk, vc.shape[-1]), jnp.float32)
    outs_c, outs_l = [], []
    for d in range(2):
        f = (lambda t: t) if d == 0 else (lambda t: jnp.flip(t, axis=1))
        oc, sc = _chunk_gated_delta(f(qc), f(kc), f(vc), f(gc[:, :, d]), f(bc[:, :, d]), s0)
        ol, _ = _chunk_gated_delta(f(ql), f(kl), f(vl), f(gl[:, :, d]), f(bl[:, :, d]), sc)
        outs_c.append(f(oc))
        outs_l.append(f(ol))
    return outs_c[0] + outs_c[1], outs_l[0] + outs_l[1]

def _dn_out(o, z, norm_w):
    B, L = o.shape[:2]
    zf = z.astype(jnp.float32).reshape(B, L, DN_HEADS, DN_HEAD_DIM)
    return (_rmsnorm(o, norm_w) * jax.nn.silu(zf)).reshape(B, L, DN_WIDTH).astype(z.dtype)

def _gqa_heads(q, k, v):
    B, L, _ = q.shape
    q = q.reshape(B, L, GQA_KV_HEADS, GQA_GROUP, GQA_HEAD_DIM)
    k = k.reshape(B, L, GQA_KV_HEADS, GQA_HEAD_DIM)
    v = v.reshape(B, L, GQA_KV_HEADS, GQA_HEAD_DIM)
    return q, k, v

def _gqa_ctx(q, k, v, sink):
    s = jnp.einsum('bqhgd,bkhd->bhgqk', q, k).astype(jnp.float32) * GQA_SCALE
    sk = jnp.broadcast_to(sink.astype(jnp.float32).reshape(GQA_KV_HEADS, GQA_GROUP)[None, :, :, None, None],
                          s.shape[:-1] + (1,))
    p = jax.nn.softmax(jnp.concatenate([s, sk], axis=-1), axis=-1)[..., :-1].astype(v.dtype)
    return jnp.einsum('bhgqk,bkhd->bqhgd', p, v)

def _gqa_latent(q, k, v, k_ctx, v_ctx, sink):
    B, L = q.shape[:2]
    C = k_ctx.shape[1]
    span = Q_BLOCK + 2 * WINDOW
    kp = jnp.pad(k, ((0, 0), (WINDOW, WINDOW), (0, 0), (0, 0)))
    vp = jnp.pad(v, ((0, 0), (WINDOW, WINDOW), (0, 0), (0, 0)))
    offs_q = jnp.arange(Q_BLOCK)
    offs_k = jnp.arange(span) - WINDOW
    sink_f = sink.astype(jnp.float32).reshape(GQA_KV_HEADS, GQA_GROUP)[None, :, :, None, None]

    def block(args):
        qb, start = args
        kb = lax.dynamic_slice_in_dim(kp, start, span, axis=1)
        vb = lax.dynamic_slice_in_dim(vp, start, span, axis=1)
        q_pos = start + offs_q
        k_pos = start + offs_k
        ok = ((jnp.abs(k_pos[None, :] - q_pos[:, None]) <= WINDOW)
              & (k_pos[None, :] >= 0) & (k_pos[None, :] < L))
        s_loc = jnp.einsum('bqhgd,bkhd->bhgqk', qb, kb).astype(jnp.float32) * GQA_SCALE
        s_loc = jnp.where(ok, s_loc, -jnp.inf)
        s_ctx = jnp.einsum('bqhgd,bkhd->bhgqk', qb, k_ctx).astype(jnp.float32) * GQA_SCALE
        sk = jnp.broadcast_to(sink_f, s_loc.shape[:-1] + (1,))
        p = jax.nn.softmax(jnp.concatenate([s_loc, s_ctx, sk], axis=-1), axis=-1).astype(v.dtype)
        return (jnp.einsum('bhgqk,bkhd->bqhgd', p[..., :span], vb)
                + jnp.einsum('bhgqk,bkhd->bqhgd', p[..., span:span + C], v_ctx))

    starts = jnp.arange(L // Q_BLOCK) * Q_BLOCK
    return _unblocks(lax.map(block, (_blocks(q), starts)))

def _merge(o_mla, o_dn, o_gqa, gates, w_o_mla, w_o_dn, w_o_gqa, w_out):
    g = jax.nn.sigmoid(gates.astype(jnp.float32)).astype(gates.dtype)
    g1, g2, g3 = jnp.split(g, 3, axis=-1)
    m = g1 * (o_mla @ w_o_mla) + g2 * (o_dn @ w_o_dn) + g3 * (o_gqa @ w_o_gqa)
    return m @ w_out

def _mixer(u_ctx, u_lat, ang_mla, ang_gqa, w_in, mla_q_norm, mla_kv_norm, w_uq, w_ukv,
           dn_conv, dn_a_log, dn_dt_bias, dn_norm, gqa_sink, w_o_mla, w_o_dn, w_o_gqa, w_out, need_ctx):
    B, C, _ = u_ctx.shape
    L = u_lat.shape[1]
    z = jnp.concatenate([u_ctx, u_lat], axis=1) @ w_in
    cq, ckv, kr, dqkv, da, db, dz, gq, gk, gv, gates = _split(z, IN_SIZES)
    cs = lambda t: t[:, :C]
    ls = lambda t: t[:, C:]
    mc = _mla_project(cs(cq), cs(ckv), cs(kr), None, mla_q_norm, mla_kv_norm, w_uq, w_ukv)
    ml = _mla_project(ls(cq), ls(ckv), ls(kr), ang_mla, mla_q_norm, mla_kv_norm, w_uq, w_ukv)
    kn_all = jnp.concatenate([mc[2], ml[2]], axis=1)
    kr_all = jnp.concatenate([mc[3], ml[3]], axis=1)
    v_all = jnp.concatenate([mc[4], ml[4]], axis=1)
    o_mla = _unblocks(lax.map(lambda qs: _mla_attend(qs[0], qs[1], kn_all, kr_all, v_all),
                              (_blocks(ml[0]), _blocks(ml[1]))))
    dc = _dn_prepare(cs(dqkv), cs(da), cs(db), dn_conv, dn_a_log, dn_dt_bias)
    dl = _dn_prepare(ls(dqkv), ls(da), ls(db), dn_conv, dn_a_log, dn_dt_bias)
    o_dn_c, o_dn_l = _dn_bidirectional(dc, dl)
    qc, kc, vc = _gqa_heads(cs(gq), cs(gk), cs(gv))
    ql, kl, vl = _gqa_heads(ls(gq), ls(gk), ls(gv))
    o_gqa = _gqa_latent(_rope(ql, ang_gqa), _rope(kl, ang_gqa), vl, kc, vc, gqa_sink)
    y_lat = _merge(o_mla.reshape(B, L, -1), _dn_out(o_dn_l, ls(dz), dn_norm), o_gqa.reshape(B, L, -1),
                   ls(gates), w_o_mla, w_o_dn, w_o_gqa, w_out)
    if not need_ctx:
        return None, y_lat
    y_ctx = _merge(_mla_attend(*mc).reshape(B, C, -1), _dn_out(o_dn_c, cs(dz), dn_norm),
                   _gqa_ctx(qc, kc, vc, gqa_sink).reshape(B, C, -1),
                   cs(gates), w_o_mla, w_o_dn, w_o_gqa, w_out)
    return y_ctx, y_lat

def _route(u, w_router, router_bias):
    scores = jax.nn.sigmoid((u @ w_router).astype(jnp.float32))
    sel = scores + router_bias.astype(jnp.float32)
    grp = sel.reshape(sel.shape[:-1] + (N_GROUPS, N_EXPERTS // N_GROUPS))
    grp_score = jnp.sum(lax.top_k(grp, 2)[0], axis=-1)
    _, gidx = lax.top_k(grp_score, TOPK_GROUPS)
    gmask = jnp.any(gidx[..., None] == jnp.arange(N_GROUPS), axis=-2)
    sel = jnp.where(jnp.repeat(gmask, N_EXPERTS // N_GROUPS, axis=-1), sel, -jnp.inf)
    _, eidx = lax.top_k(sel, TOP_K)
    w = jnp.take_along_axis(scores, eidx, axis=-1)
    return eidx, w / jnp.sum(w, axis=-1, keepdims=True) * ROUTED_SCALE

def _routed_experts(u, eidx, ew, w_gate, w_up, w_down):
    T = u.shape[0]
    A = T * TOP_K
    n_blocks = -(-(A + N_EXPERTS * (EXPERT_BLOCK - 1)) // EXPERT_BLOCK)
    rows = n_blocks * EXPERT_BLOCK
    flat_e = eidx.reshape(-1)
    order = jnp.argsort(flat_e)
    e_sorted = flat_e[order]
    counts = jnp.bincount(flat_e, length=N_EXPERTS)
    padded = (counts + EXPERT_BLOCK - 1) // EXPERT_BLOCK * EXPERT_BLOCK
    start_sorted = jnp.cumsum(counts) - counts
    pad_end = jnp.cumsum(padded)
    start_pad = pad_end - padded
    dest = start_pad[e_sorted] + jnp.arange(A) - start_sorted[e_sorted]
    row_tok = jnp.zeros((rows,), jnp.int32).at[dest].set((order // TOP_K).astype(jnp.int32))
    row_w = jnp.zeros((rows,), ew.dtype).at[dest].set(ew.reshape(-1)[order])
    block_e = jnp.minimum(jnp.searchsorted(pad_end, jnp.arange(n_blocks) * EXPERT_BLOCK, side='right'),
                          N_EXPERTS - 1)
    xb = u[row_tok].reshape(n_blocks, EXPERT_BLOCK, -1)

    def expert_block(args):
        xr, e = args
        hdn = jax.nn.silu(xr @ w_gate[e]) * (xr @ w_up[e])
        return hdn @ w_down[e]

    y = lax.map(expert_block, (xb, block_e)).reshape(rows, -1)
    return jnp.zeros_like(u).at[row_tok].add((y * row_w[:, None]).astype(u.dtype))

def _moe(u, w_router, router_bias, w_gate, w_up, w_down, w_sh_gate, w_sh_up, w_sh_down):
    eidx, ew = _route(u, w_router, router_bias)
    routed = lax.map(lambda a: _routed_experts(a[0], a[1], a[2], w_gate, w_up, w_down), (u, eidx, ew))
    shared = (jax.nn.silu(u @ w_sh_gate) * (u @ w_sh_up)) @ w_sh_down
    return shared + routed

def setup_inputs(seed: int = 0) -> dict:
    key = jax.random.key(seed)
    keys = iter(jax.random.split(key, 40))
    f32 = jnp.float32

    def normal(shape, std=1.0):
        return jax.random.normal(next(keys), shape, f32) * std

    D, NL = D_MODEL, DEPTH
    dt = jnp.exp(jax.random.uniform(next(keys), (NL, 2, DN_HEADS), f32, math.log(1e-3), math.log(1e-1)))
    a_log = jnp.log(jax.random.uniform(next(keys), (NL, 2, DN_HEADS), f32, 1.0, 16.0))
    return {
        'x': normal((BATCH, SEQ, D)),
        'c': normal((BATCH, D)),
        'ctx': normal((BATCH, CTX_LEN, D)),
        'c_ctx': normal((D,)),
        'w_ada': normal((NL, D, 6 * D), 0.5 * D ** -0.5),
        'b_ada': normal((NL, 6 * D), 0.02),
        'w_in': normal((NL, D, D_IN), D ** -0.5),
        'mla_q_norm': 1.0 + normal((NL, MLA_Q_LORA), 0.02),
        'mla_kv_norm': 1.0 + normal((NL, MLA_KV_LORA), 0.02),
        'w_uq': normal((NL, MLA_Q_LORA, MLA_HEADS * (MLA_NOPE + MLA_ROPE)), MLA_Q_LORA ** -0.5),
        'w_ukv': normal((NL, MLA_KV_LORA, MLA_HEADS * (MLA_NOPE + MLA_V)), MLA_KV_LORA ** -0.5),
        'dn_conv': normal((NL, DN_CONV, 3 * DN_WIDTH), DN_CONV ** -0.5),
        'dn_a_log': a_log,
        'dn_dt_bias': dt + jnp.log(-jnp.expm1(-dt)),
        'dn_norm': 1.0 + normal((NL, DN_HEAD_DIM), 0.02),
        'gqa_sink': normal((NL, GQA_HEADS), 0.5),
        'w_o_mla': normal((NL, MLA_HEADS * MLA_V, D), (MLA_HEADS * MLA_V) ** -0.5),
        'w_o_dn': normal((NL, DN_WIDTH, D), DN_WIDTH ** -0.5),
        'w_o_gqa': normal((NL, GQA_HEADS * GQA_HEAD_DIM, D), (GQA_HEADS * GQA_HEAD_DIM) ** -0.5),
        'w_out': normal((NL, D, D), DEEPNORM_BETA * D ** -0.5),
        'ln1_g': 1.0 + normal((NL, D), 0.02),
        'ln1_b': normal((NL, D), 0.02),
        'w_router': normal((NL, D, N_EXPERTS), D ** -0.5),
        'router_bias': normal((NL, N_EXPERTS), 0.01),
        'w_exp_gate': normal((NL, N_EXPERTS, D, EXPERT_DIM), D ** -0.5),
        'w_exp_up': normal((NL, N_EXPERTS, D, EXPERT_DIM), D ** -0.5),
        'w_exp_down': normal((NL, N_EXPERTS, EXPERT_DIM, D), DEEPNORM_BETA * EXPERT_DIM ** -0.5),
        'w_sh_gate': normal((NL, D, SHARED_DIM), D ** -0.5),
        'w_sh_up': normal((NL, D, SHARED_DIM), D ** -0.5),
        'w_sh_down': normal((NL, SHARED_DIM, D), DEEPNORM_BETA * SHARED_DIM ** -0.5),
        'ln2_g': 1.0 + normal((NL, D), 0.02),
        'ln2_b': normal((NL, D), 0.02),
    }

def reference(x, c, ctx, c_ctx, w_ada, b_ada, w_in, mla_q_norm, mla_kv_norm, w_uq, w_ukv,
              dn_conv, dn_a_log, dn_dt_bias, dn_norm, gqa_sink, w_o_mla, w_o_dn, w_o_gqa, w_out,
              ln1_g, ln1_b, w_router, router_bias, w_exp_gate, w_exp_up, w_exp_down,
              w_sh_gate, w_sh_up, w_sh_down, ln2_g, ln2_b):
    n_lat = x.shape[1]
    n_ctx = ctx.shape[1]
    n_rows = n_lat // GRID_W
    ang_mla = _axial_angles(n_rows, MLA_ROPE)
    ang_gqa = _axial_angles(n_rows, GQA_HEAD_DIM)
    h = ctx
    for l in range(DEPTH):
        need_ctx = l < DEPTH - 1
        mod = jax.nn.silu(c) @ w_ada[l] + b_ada[l]
        mod_c = jax.nn.silu(c_ctx) @ w_ada[l] + b_ada[l]
        sh_a, sc_a, g_a, sh_f, sc_f, g_f = jnp.split(mod[:, None, :], 6, axis=-1)
        csh_a, csc_a, cg_a, csh_f, csc_f, cg_f = jnp.split(mod_c, 6, axis=-1)
        y_ctx, y_lat = _mixer(h * (1.0 + csc_a) + csh_a, x * (1.0 + sc_a) + sh_a, ang_mla, ang_gqa,
                              w_in[l], mla_q_norm[l], mla_kv_norm[l], w_uq[l], w_ukv[l],
                              dn_conv[l], dn_a_log[l], dn_dt_bias[l], dn_norm[l], gqa_sink[l],
                              w_o_mla[l], w_o_dn[l], w_o_gqa[l], w_out[l], need_ctx)
        x = _layernorm(DEEPNORM_ALPHA * x + g_a * y_lat, ln1_g[l], ln1_b[l])
        moe_w = (w_router[l], router_bias[l], w_exp_gate[l], w_exp_up[l], w_exp_down[l],
                 w_sh_gate[l], w_sh_up[l], w_sh_down[l])
        if need_ctx:
            h = _layernorm(DEEPNORM_ALPHA * h + cg_a * y_ctx, ln1_g[l], ln1_b[l])
            f = _moe(jnp.concatenate([h * (1.0 + csc_f) + csh_f, x * (1.0 + sc_f) + sh_f], axis=1), *moe_w)
            h = _layernorm(DEEPNORM_ALPHA * h + cg_f * f[:, :n_ctx], ln2_g[l], ln2_b[l])
            x = _layernorm(DEEPNORM_ALPHA * x + g_f * f[:, n_ctx:], ln2_g[l], ln2_b[l])
        else:
            f = _moe(x * (1.0 + sc_f) + sh_f, *moe_w)
            x = _layernorm(DEEPNORM_ALPHA * x + g_f * f, ln2_g[l], ln2_b[l])
    return x


_drawn_inputs = setup_inputs


def setup_inputs(seed=0):
    import zlib

    import numpy as np

    out = dict(_drawn_inputs(seed))
    spreads = {}
    factors = {'ctx': 3.93,
     'c_ctx': 2.702,
     'b_ada': 2.693,
     'mla_q_norm': 8.0,
     'mla_kv_norm': 8.0,
     'w_uq': 5.574,
     'dn_a_log': 3.632,
     'dn_norm': 8.0,
     'gqa_sink': 64.0,
     'w_o_mla': 2.713}
    for name, (base, spread) in spreads.items():
        noise = np.random.default_rng([zlib.crc32(name.encode()), seed]).standard_normal(out[name].shape)
        drawn = base * np.exp(spread * noise) if base else spread * noise
        out[name] = jnp.asarray(drawn.astype(out[name].dtype))
    for name, factor in factors.items():
        out[name] = (out[name] * factor).astype(out[name].dtype)
    return out
```

```python
from contextlib import ExitStack

import numpy as np

import concourse.bass as bass
from concourse import mybir

F32 = mybir.dt.float32
I32 = mybir.dt.int32
ALU = mybir.AluOpType
ACT = mybir.ActivationFunctionType
AX = mybir.AxisListType

P = 128
D = 1024
KT = D // P
DEPTH = 2
SEG = 256
T = 2 * SEG
NT = T // P
EPS = 1e-6
ALPHA = (2.0 * DEPTH) ** 0.25
GRID_W = 64

Q_LORA, KV_LORA = 256, 128
H = 8
NOPE, ROPE, HD = 64, 32, 64
QK = NOPE + ROPE
MLA_SCALE = QK ** -0.5
GQA_SCALE = HD ** -0.5
KV_HEADS = 2
WINDOW = 128
CONV = 5
CH = 64
DW = H * HD

NE, TOPK, NG, TOPG = 64, 8, 8, 4
FE = 256
ROUTED_SCALE = 2.5
NBLK = T * TOPK // P + NE
FAR = 1 << 14
MASKED = -1e30

C_DQKV, C_AB, C_GATES = 416, 1952, 3264
ZCH = [(0, 0, 416), (1952, 416, 512), (2464, 928, 512), (2976, 1440, 288)]
ZW = 1728
Z_CQ, Z_CKV, Z_KR, Z_A, Z_B, Z_DZ, Z_GQ, Z_GK, Z_GV = 0, 256, 384, 416, 432, 448, 960, 1472, 1600

LEVELS = 6


def constants():
    i = np.arange(P)
    same = (i[:, None] // CH) == (i[None, :] // CH)
    parts = {}
    parts["ident"] = np.eye(P)
    parts["tri0"] = same & (i[:, None] <= i[None, :])
    parts["tri1"] = same & (i[:, None] >= i[None, :])
    parts["blk"] = same
    parts["sel0"] = np.repeat((i < CH)[:, None], P, 1)
    parts["sel1"] = np.repeat((i >= CH)[:, None], P, 1)
    for d in range(2):
        for s in range(LEVELS):
            b = 1 << s
            a, c = (i[:, None], i[None, :]) if d == 0 else (i[None, :], i[:, None])
            parts[f"lvl{d}{s}"] = (a // (2 * b) == c // (2 * b)) & (a // b % 2 == 1) & (c // b % 2 == 0)
    for t in range(2):
        q = t * P + i[:, None]
        k = np.arange(SEG)[None, :]
        ok = np.abs(q - k) <= WINDOW
        parts[f"win{t}"] = np.concatenate([np.zeros((P, SEG)), np.where(ok, 0.0, MASKED)], 1)
    for name, dim in (("m", ROPE), ("g", HD)):
        n = dim // 4
        inv = np.float32(10000.0) ** (-np.arange(n, dtype=np.float32) / np.float32(n))
        t = np.arange(SEG)
        ang = np.concatenate([(t // GRID_W).astype(np.float32)[:, None] * inv,
                              (t % GRID_W).astype(np.float32)[:, None] * inv], 1)
        for f, nm in ((np.cos, "cos"), (np.sin, "sin")):
            tab = f(ang.astype(np.float32)).reshape(2, P, 2 * n).transpose(1, 0, 2)
            parts[nm + name] = tab.reshape(P, 4 * n)
    parts["before"] = i[:, None] < i[None, :]
    parts["ones"] = np.ones((P, P))
    g = np.arange(NG)
    parts["glow"] = np.tile((g[None, :] < g[:, None]).reshape(1, -1), (P, 1))
    parts["rowid"] = i[:, None]
    parts["iota"] = np.tile(i[None, :], (P, 1))
    parts["blkbase"] = np.tile(P * i[None, :], (P, 1))
    parts["tokid"] = i[:, None] + P * np.arange(NT)[None, :]
    at, cols = {}, 0
    for n, v in parts.items():
        at[n] = (cols, v.shape[1])
        cols += v.shape[1]
    return np.concatenate([np.asarray(v, np.float32) for v in parts.values()], 1), at


CONST, CAT = constants()
NCONST = CONST.shape[1]


class Chain:

    def __init__(self, eng, sem):
        self.eng, self.sem, self.n = eng, sem, 0

    def add(self, ins):
        ins.then_inc(self.sem, 1)
        self.n += 1

    def sync(self):
        self.eng.wait_ge(self.sem, self.n)

    def run(self, ins):
        self.add(ins)
        self.sync()


def trunk(nc, a, out, depth=DEPTH):
    with ExitStack() as ctx:
        def sb(name, shape, dt=F32):
            return ctx.enter_context(nc.sbuf_tensor(name, shape, dt))

        shared = [ctx.enter_context(nc.semaphore(f"s_stage{i}")) for i in range(72)]
        taken = {}

        def sem(name):
            if name not in taken:
                taken[name] = shared[len(taken)]
            return taken[name]

        def own_sem(name):
            return ctx.enter_context(nc.semaphore(name))

        X = sb("X", [P, NT, D])
        UT = sb("UT", [P, KT, T])
        CB = sb("CB", [P, NCONST])
        RING = sb("RING", [P, 3, 8 * 512])
        AR = sb("AR", [P, 27392])
        SM = sb("SM", [P, 1040])
        EXPERT = sb("EXPERT", [1, P], I32)
        NPAIR = sb("NPAIR", [1, 1], I32)
        IXG = sb("IXG", [P, 2], I32)
        IXV = sb("IXV", [P, 2], I32)
        IXS = sb("IXS", [P, 2], I32)
        BEI = sb("BEI", [P, 1], I32)
        PS = ctx.enter_context(nc.psum_tensor("PS", [P, 8, 512], F32))

        mod_d = nc.dram_tensor("mod_d", [DEPTH, 2, 6 * D], F32).ap()
        u_d = nc.dram_tensor("u_d", [T, D], F32).ap()
        y_d = nc.dram_tensor("y_d", [TOPK * T, D], F32).ap()
        blk_d = nc.dram_tensor("blk_d", [P, 1], I32).ap()

        def cst(name):
            o, n = CAT[name]
            return CB[:, o:o + n]

        ident = cst("ident")

        def ar(off, *dims):
            n = int(np.prod(dims))
            v = AR[:, off:off + n]
            if len(dims) == 1:
                return v
            names = "abcde"[:len(dims)]
            return v.rearrange(f"p ({' '.join(names)}) -> p {' '.join(names)}", **{c: k for c, k in zip(names[1:], dims[1:])})

        def sm(off, *dims):
            n = int(np.prod(dims))
            v = SM[:, off:off + n]
            if len(dims) == 1:
                return v
            names = "abcde"[:len(dims)]
            return v.rearrange(f"p ({' '.join(names)}) -> p {' '.join(names)}", **{c: k for c, k in zip(names[1:], dims[1:])})

        s_bar = own_sem("s_bar")
        s_act = own_sem("s_act_chain")
        s_dve = own_sem("s_dve_chain")
        s_pool = own_sem("s_pool_chain")
        s_const = own_sem("s_const")
        s_slot = [own_sem(f"s_slot{i}") for i in range(3)]
        s_wfree = own_sem("s_wfree")

        plan, where = [], {}

        def use(key, moves):
            where[key] = len(plan)
            plan.append(moves)

        def by_k(w, n):
            return (w.rearrange("(k p) n -> p k n", p=P), w.shape[0] // P, n)

        for l in range(depth):
            for n in range(12):
                use(("ada", l, n), [(0, *by_k(a["w_ada"][l, :, n * 512:(n + 1) * 512], 512))])
        moe_after = {}
        for l in range(depth):
            for c, (src, _, n) in enumerate(ZCH):
                use(("z", l, c), [(0, *by_k(a["w_in"][l, :, src:src + n], n))])
            use(("uqkv", l), [(0, *by_k(a["w_uq"][l], 768)), (1536, *by_k(a["w_ukv"][l], 1024))])
            for c in range(3):
                use(("dqkv", l, c), [(0, *by_k(a["w_in"][l, :, C_DQKV + 512 * c:C_DQKV + 512 * (c + 1)], 512))])
            for b, nm in enumerate(("w_o_mla", "w_o_dn", "w_o_gqa")):
                for c in range(2):
                    g0 = C_GATES + b * D + c * 512
                    use(("gate", l, b, c), [(0, *by_k(a["w_in"][l, :, g0:g0 + 512], 512))])
                use(("o", l, b), [(0, *by_k(a[nm][l], D))])
            for c in range(2):
                use(("out", l, c), [(0, *by_k(a["w_out"][l, :, c * 512:(c + 1) * 512], 512))])
            use(("router", l), [(0, *by_k(a["w_router"][l], NE))])
            use(("shgu", l), [(0, *by_k(a["w_sh_gate"][l], FE)), (KT * FE, *by_k(a["w_sh_up"][l], FE))])
            use(("shd", l), [(0, *by_k(a["w_sh_down"][l], D))])
            moe_after[len(plan)] = l
        ready = []
        count = [0, 0, 0]
        for n, moves in enumerate(plan):
            count[n % 3] += 16 * len(moves)
            ready.append(count[n % 3])

        def slot(key, off=0, *dims):
            base = RING[:, where[key] % 3, off:off + int(np.prod(dims))]
            return base.rearrange("p (k n) -> p k n", k=dims[0])

        def landed(pe, key):
            n = where[key]
            pe.wait_ge(s_slot[n % 3], ready[n])

        phases = []
        MOE = ("wl", "oh", "ixp", "ixd", "tr", "xta", "xtd", "gu", "sg", "h", "ht", "hte", "y", "ye")
        moe_dma = [{k: [own_sem(f"s_moe{l}_{k}{q}") for q in range(2)] for k in ("xg", "sc")} for l in range(depth)]
        moe = {}

        def stage_mod():
            s_c, s_cs, s_ps, s_ev, s_st = (sem(f"s_mod_{x}") for x in ("c", "cs", "ps", "ev", "st"))
            cv = sm(0, KT, 2)
            cs = sm(16, KT, 2)
            row = AR[0:2, 0:depth * 6 * D].rearrange("p (l n) -> p l n", l=depth)

            def act(e, ch):
                e.dma_start(cv[:, :, 0], a["c_ctx"].rearrange("(k p) -> p k", p=P), allow_slow_non_contiguous=True).then_inc(s_c, 16)
                e.dma_start(cv[:, :, 1], a["c"][0].rearrange("(k p) -> p k", p=P), allow_slow_non_contiguous=True).then_inc(s_c, 16)
                for i in range(2):
                    e.dma_start(row[i:i + 1], a["b_ada"][0:depth].rearrange("(o l) n -> o l n", o=1)).then_inc(s_st, 16)
                e.wait_ge(s_c, 32)
                e.activation(cs, cv, ACT.Silu).then_inc(s_cs, 1)
                e.wait_ge(s_ev, 12 * depth)
                for i in range(2):
                    e.dma_start(mod_d[0:depth, i, :].rearrange("(o l) n -> o l n", o=1), row[i:i + 1]).then_inc(s_st, 16)
                e.wait_ge(s_st, 64)

            def pe(e):
                e.wait_ge(s_cs, 1)
                for i in range(12 * depth):
                    key = ("ada", i // 12, i % 12)
                    landed(e, key)
                    w = slot(key, 0, KT, 512)
                    if i >= 2:
                        e.wait_ge(s_ev, i - 1)
                    for k in range(KT):
                        m = e.matmul(PS[0:2, i % 2, :], cs[:, k, :], w[:, k, :], start=k == 0, stop=k == KT - 1)
                    m.then_inc(s_ps, 1)
                    e.wait_ge(s_ps, i + 1)
                    e.sem_inc(s_wfree, 1)

            def dve(e, ch):
                e.wait_ge(s_st, 32)
                for i in range(12 * depth):
                    e.wait_ge(s_ps, i + 1)
                    r = row[:, i // 12, (i % 12) * 512:(i % 12 + 1) * 512]
                    e.tensor_tensor(r, PS[0:2, i % 2, :], r, ALU.add).then_inc(s_ev, 1)
            return dict(act=act, pe=pe, dve=dve)

        def modulation(e, l, which, dst, s, segs):
            n = 0
            for i, w in enumerate(which):
                for g in segs:
                    e.dma_start(dst[:, g, i, :], mod_d[l, g:g + 1, w * D:(w + 1) * D].broadcast_to([P, D])).then_inc(s, 16)
                    n += 16
            return n

        def stage_u(l, ffn, t0):
            nm = f"s_u{int(ffn)}_"
            s_m, s_u, s_tp, s_te, s_ud0, s_ud1, s_t1 = (sem(nm + x) for x in ("m", "u", "tp", "te", "ud0", "ud1", "t1"))
            s_ud = (s_ud0, s_ud1)
            mb = ar(0, 2, 2, D)
            u = ar(4 * D, 2, D)
            tmp = ar(6 * D, 2, D)
            tiles = list(range(t0, NT))
            segs = range(t0 // 2, 2)

            def act(e, ch):
                modulation(e, l, (3, 4) if ffn else (0, 1), mb, s_m, segs)
                for i, t in enumerate(tiles):
                    if ffn:
                        e.wait_ge(s_u, i + 1)
                        e.dma_start(u_d[t * P:(t + 1) * P, :], u[:, i % 2, :]).then_inc(s_ud[i % 2], 16)
                    for g in range(2):
                        e.wait_ge(s_tp, 2 * i + g + 1)
                        e.activation(UT[:, 4 * g:4 * g + 4, t * P:(t + 1) * P],
                                     PS[:, (2 * i + g) % 4, :].rearrange("p (k q) -> p k q", k=4), ACT.Copy).then_inc(s_te, 1)
                if ffn:
                    for q in range(2):
                        e.wait_ge(s_ud[q], 8 * len(tiles))

            def pe(e):
                for i, t in enumerate(tiles):
                    e.wait_ge(s_u, i + 1)
                    for g in range(2):
                        n = 2 * i + g
                        if n >= 4:
                            e.wait_ge(s_te, n - 3)
                        for k in range(4):
                            m = e.transpose(PS[:, n % 4, k * P:(k + 1) * P], u[:, i % 2, (4 * g + k) * P:(4 * g + k + 1) * P], ident)
                        m.then_inc(s_tp, 1)

            def dve(e, ch):
                e.wait_ge(s_m, 64 if t0 == 0 else 32)
                for i, t in enumerate(tiles):
                    e.scalar_tensor_tensor(out=tmp[:, i % 2, :], in0=mb[:, t // 2, 1, :], scalar=1.0, in1=X[:, t, :],
                                           op0=ALU.add, op1=ALU.mult).then_inc(s_t1, 1)
                    e.wait_ge(s_t1, i + 1)
                    if i >= 2:
                        e.wait_ge(s_tp, 2 * (i - 1))
                        if ffn:
                            e.wait_ge(s_ud[i % 2], 16 * (i // 2))
                    e.tensor_tensor(u[:, i % 2, :], tmp[:, i % 2, :], mb[:, t // 2, 0, :], ALU.add).then_inc(s_u, 1)
            return dict(act=act, pe=pe, dve=dve)

        ZA = ar(0, NT, ZW)

        def stage_z(l, t0):
            s_ps, s_ea, s_ed = (sem(f"s_z_{x}") for x in ("ps", "ea", "ed"))
            items = []
            for c, (_, dst, n) in enumerate(ZCH):
                for t in range(NT):
                    width = n if t >= t0 or c in (0, 3) else (32 if c == 1 else 0)
                    if width:
                        items.append((c, t, dst, width))

            def evac(e, parity, s, fn):
                for i, (c, t, dst, n) in enumerate(items):
                    if i % 2 == parity:
                        e.wait_ge(s_ps, i + 1)
                        fn(ZA[:, t, dst:dst + n], PS[:, i % 4, 0:n]).then_inc(s, 1)

            def act(e, ch):
                evac(e, 0, s_ea, lambda o, i: e.activation(o, i, ACT.Copy))

            def dve(e, ch):
                evac(e, 1, s_ed, lambda o, i: e.tensor_copy(o, i))

            def pe(e):
                for i, (c, t, dst, n) in enumerate(items):
                    landed(e, ("z", l, c))
                    w = slot(("z", l, c), 0, KT, ZCH[c][2])
                    if i >= 4:
                        e.wait_ge(s_ea if i % 2 == 0 else s_ed, (i - 4) // 2 + 1)
                    for k in range(KT):
                        m = e.matmul(PS[:, i % 4, 0:n], UT[:, k, t * P:(t + 1) * P], w[:, k, 0:n], start=k == 0, stop=k == KT - 1)
                    m.then_inc(s_ps, 1)
                    if i + 1 == len(items) or items[i + 1][0] != c:
                        e.wait_ge(s_ps, i + 1)
                        e.sem_inc(s_wfree, 1)
            return dict(act=act, pe=pe, dve=dve)

        def rope(e, ch, x1, x2, cos, sin, tmp):
            ch.add(e.tensor_tensor(tmp[0], x1, cos, ALU.mult))
            ch.add(e.tensor_tensor(tmp[1], x2, sin, ALU.mult))
            ch.add(e.tensor_tensor(tmp[2], x2, cos, ALU.mult))
            ch.add(e.tensor_tensor(tmp[3], x1, sin, ALU.mult))
            ch.sync()
            ch.add(e.tensor_tensor(x1, tmp[0], tmp[1], ALU.subtract))
            ch.add(e.tensor_tensor(x2, tmp[2], tmp[3], ALU.add))
            ch.sync()

        OT = [ar(ZW * NT, 4, T), ar(ZW * NT + 2048, 4, T), ar(ZW * NT + 4096, 4, T)]
        O_MLA, O_GQA, _ = OT
        DZ = ar(ZW * NT + 4096, NT, DW)
        B0 = ZW * NT + 3 * 2048

        qT = ar(B0, H, T)
        kTm = ar(B0 + 4096, H, T)
        V = ar(B0 + 8192, NT, DW)
        PB = ar(B0 + 10240, 3, 512)
        C0 = B0 + 11776

        def stage_mla(l, t0):
            s_g, s_ms, s_rt, s_cn, s_tp, s_te, s_pj, s_pe_, s_rq, s_kk, s_hp, s_he = (
                sem(f"s_ml_{x}") for x in ("g", "ms", "rt", "cn", "tp", "te", "pj", "ev", "rq", "kk", "hp", "he"))
            gain = sm(0, 384)
            ss, rt = sm(384, 8), sm(392, 8)
            cT = ar(C0, 3, T)
            tile = ar(B0 + 10240, 2, 768)
            tmp = [ar(C0 + 1536 + 128 * i, H, 16) for i in range(4)]
            cosm = cst("cosm").rearrange("p (t n) -> p t n", t=2)
            sinm = cst("sinm").rearrange("p (t n) -> p t n", t=2)
            sqd = ar(B0 + 10240, 256)
            jobs = [("kv", t) for t in range(NT)] + [("q", t) for t in range(t0, NT)]

            def act(e, ch):
                e.dma_start(gain[:, 0:256], a["mla_q_norm"][l:l + 1, :].broadcast_to([P, 256])).then_inc(s_g, 16)
                e.dma_start(gain[:, 256:384], a["mla_kv_norm"][l:l + 1, :].broadcast_to([P, 128])).then_inc(s_g, 16)
                e.wait_ge(s_ms, 1)
                e.activation(rt, ss, ACT.Sqrt).then_inc(s_rt, 1)
                for t in range(NT):
                    e.wait_ge(s_tp, t + 1)
                    lo = 0 if t >= t0 else 2
                    e.activation(cT[:, lo:3, t * P:(t + 1) * P],
                                 PS[:, t % 2, lo * P:384].rearrange("p (k q) -> p k q", q=P), ACT.Copy).then_inc(s_te, 1)
                for i, (kind, t) in enumerate(jobs):
                    o = tile[:, i % 2, :].rearrange("p (h n) -> p h n", h=H)
                    if i >= 2:
                        e.wait_ge(s_hp, 2 * (i - 1))
                    for g in range(2):
                        e.wait_ge(s_pj, 2 * i + g + 1)
                        b = PS[:, 2 + g, :]
                        if kind == "q":
                            e.activation(o[:, 4 * g:4 * g + 4, :], b[:, 0:384].rearrange("p (h n) -> p h n", h=4), ACT.Copy).then_inc(s_pe_, 1)
                        else:
                            kv = b.rearrange("p (h n) -> p h n", h=4)
                            e.activation(o[:, 4 * g:4 * g + 4, 0:NOPE], kv[:, :, 0:NOPE], ACT.Copy)
                            e.activation(V[:, t, 256 * g:256 * (g + 1)].rearrange("p (h n) -> p h n", h=4), kv[:, :, NOPE:], ACT.Copy).then_inc(s_pe_, 1)
                    for g in range(2):
                        e.wait_ge(s_hp, 2 * i + g + 1)
                        dst = qT if kind == "q" else kTm
                        e.activation(dst[0:QK, 4 * g:4 * g + 4, t * P:(t + 1) * P],
                                     PS[0:QK, 4 + g, :].rearrange("p (h q) -> p h q", h=4), ACT.Copy).then_inc(s_he, 1)

            def dve(e, ch):
                cq = [ZA[:, t, Z_CQ:Z_CQ + 256] for t in range(NT)]
                ckv = [ZA[:, t, Z_CKV:Z_CKV + 128] for t in range(NT)]
                ch.run(e.memset(ss, 1.0))
                for t in range(NT):
                    if t >= t0:
                        ch.run(e.tensor_tensor_reduce(sqd, cq[t], cq[t], 1.0 / 256, EPS, ALU.mult, ALU.add, ss[:, t:t + 1]))
                    ch.run(e.tensor_tensor_reduce(sqd[:, 0:128], ckv[t], ckv[t], 1.0 / 128, EPS, ALU.mult, ALU.add, ss[:, 4 + t:5 + t]))
                e.sem_inc(s_ms, 1)
                e.wait_ge(s_rt, 1)
                ch.run(e.reciprocal(ss, rt))
                e.wait_ge(s_g, 32)
                for t in range(NT):
                    if t >= t0:
                        ch.add(e.scalar_tensor_tensor(out=cq[t], in0=cq[t], scalar=ss[:, t:t + 1], in1=gain[:, 0:256], op0=ALU.mult, op1=ALU.mult))
                    e.scalar_tensor_tensor(out=ckv[t], in0=ckv[t], scalar=ss[:, 4 + t:5 + t], in1=gain[:, 256:384],
                                           op0=ALU.mult, op1=ALU.mult).then_inc(s_cn, 1)
                kr = ZA[:, 2:4, Z_KR:Z_KR + ROPE]
                rope(e, ch, kr[:, :, 0:16], kr[:, :, 16:32], cosm, sinm, [x[:, 0:2, :] for x in tmp])
                for i, (kind, t) in enumerate(jobs):
                    o = tile[:, i % 2, :].rearrange("p (h n) -> p h n", h=H)
                    e.wait_ge(s_pe_, 2 * i + 2)
                    if kind == "q":
                        if t >= 2:
                            cb = cosm[:, t - 2:t - 1, :].broadcast_to([P, H, 16])
                            sn = sinm[:, t - 2:t - 1, :].broadcast_to([P, H, 16])
                            rope(e, ch, o[:, :, NOPE:NOPE + 16], o[:, :, NOPE + 16:QK], cb, sn, tmp)
                    else:
                        ch.run(e.tensor_copy(o[:, :, NOPE:QK], ZA[:, t:t + 1, Z_KR:Z_KR + ROPE].broadcast_to([P, H, ROPE])))
                    e.sem_inc(s_rq, 1)

            def pe(e):
                for t in range(NT):
                    e.wait_ge(s_cn, t + 1)
                    if t >= 2:
                        e.wait_ge(s_te, t - 1)
                    for k in range(3):
                        if k == 2 or t >= t0:
                            src = Z_CQ + k * P
                            m = e.transpose(PS[:, t % 2, k * P:(k + 1) * P], ZA[:, t, src:src + P], ident)
                    m.then_inc(s_tp, 1)
                e.wait_ge(s_te, NT)
                landed(e, ("uqkv", l))
                wq = slot(("uqkv", l), 0, 2, 768)
                wkv = slot(("uqkv", l), 1536, 1, D)
                for i in range(len(jobs) + 1):
                    if i < len(jobs):
                        kind, t = jobs[i]
                        for g in range(2):
                            if i >= 1:
                                e.wait_ge(s_pe_, 2 * (i - 1) + g + 1)
                            if kind == "q":
                                for k in range(2):
                                    m = e.matmul(PS[:, 2 + g, 0:384], cT[:, k, t * P:(t + 1) * P], wq[:, k, g * 384:(g + 1) * 384], start=k == 0, stop=k == 1)
                            else:
                                m = e.matmul(PS[:, 2 + g, :], cT[:, 2, t * P:(t + 1) * P], wkv[:, 0, g * 512:(g + 1) * 512], start=True, stop=True)
                            m.then_inc(s_pj, 1)
                    if i >= 1:
                        j = i - 1
                        o = tile[:, j % 2, :].rearrange("p (h n) -> p h n", h=H)
                        e.wait_ge(s_rq, j + 1)
                        for g in range(2):
                            if j >= 1:
                                e.wait_ge(s_he, 2 * (j - 1) + g + 1)
                            for h in range(4):
                                m = e.transpose(PS[0:QK, 4 + g, h * P:(h + 1) * P], o[:, 4 * g + h, :], ident)
                            m.then_inc(s_hp, 1)
                e.wait_ge(s_hp, 2 * len(jobs))
                e.sem_inc(s_wfree, 1)
            return dict(act=act, pe=pe, dve=dve)

        kT2 = ar(B0 + 4096, KV_HEADS, T)

        def stage_gqa(l, t0):
            s_k, s_sk, s_tp, s_te = (sem(f"s_gq_{x}") for x in ("k", "sk", "tp", "te"))
            kd = ar(B0 + 8192, NT, KV_HEADS, 2, HD)
            tmp = [ar(B0 + 9216 + 640 * i, 2, 10, 32) for i in range(4)]
            cosg = cst("cosg").rearrange("p (t n) -> p t n", t=2)
            sing = cst("sing").rearrange("p (t n) -> p t n", t=2)
            groups = [("k", t, 0) for t in range(NT)] + [("q", t, 0) for t in range(t0, NT)]

            def act(e, ch):
                e.dma_start(sm(0, H), a["gqa_sink"][l:l + 1, :].broadcast_to([P, H])).then_inc(s_sk, 16)
                for i, (kind, t, _) in enumerate(groups):
                    e.wait_ge(s_tp, i + 1)
                    if kind == "k":
                        e.activation(kT2[:, :, t * P:(t + 1) * P], PS[:, i % 4, 0:256].rearrange("p (g q) -> p g q", g=2), ACT.Copy).then_inc(s_te, 1)
                    else:
                        e.activation(qT[:, 0:4, t * P:(t + 1) * P], PS[:, i % 4, :].rearrange("p (g q) -> p g q", g=4), ACT.Copy).then_inc(s_te, 1)
                e.wait_ge(s_sk, 16)

            def dve(e, ch):
                for t in range(2):
                    qk = ZA[:, 2 + t, Z_GQ:Z_GV].rearrange("p (h n) -> p h n", n=HD)
                    cb = cosg[:, t:t + 1, :].broadcast_to([P, 10, 32])
                    sn = sing[:, t:t + 1, :].broadcast_to([P, 10, 32])
                    rope(e, ch, qk[:, :, 0:32], qk[:, :, 32:64], cb, sn, [x[:, t] for x in tmp])
                for g in range(KV_HEADS):
                    for r in range(2):
                        ch.add(e.tensor_copy(kd[:, :, g, r, :], ZA[:, :, Z_GK + g * HD:Z_GK + (g + 1) * HD]))
                ch.sync()
                e.sem_inc(s_k, 1)

            def pe(e):
                e.wait_ge(s_k, 1)
                for i, (kind, t, _) in enumerate(groups):
                    if i >= 4:
                        e.wait_ge(s_te, i - 3)
                    for j in range(2 if kind == "k" else 4):
                        src = kd[:, t, j].rearrange("p r n -> p (r n)") if kind == "k" else ZA[:, t, Z_GQ + j * P:Z_GQ + (j + 1) * P]
                        m = e.transpose(PS[:, i % 4, j * P:(j + 1) * P], src, ident)
                    m.then_inc(s_tp, 1)
            return dict(act=act, pe=pe, dve=dve)

        def stage_attend(l, gqa, t0):
            nm = f"s_at{int(gqa)}_"
            s_sc, s_mk, s_mx, s_ex, s_p, s_t, s_pt, s_pv, s_o, s_es = (sem(nm + x) for x in ("sc", "mk", "mx", "ex", "p", "t", "pt", "pv", "o", "es"))
            items = [(h, t) for h in range(H) for t in range(t0, NT)]
            n = len(items)
            scale = GQA_SCALE if gqa else MLA_SCALE
            dst = O_GQA if gqa else O_MLA
            sink = sm(0, H)
            mx, nm_, rs, es, rr = sm(16, 4), sm(20, 4), sm(24, 4), sm(28, 4), sm(32, 4)
            SB = ar(C0, 3, 512)
            PT = ar(C0 + 1536, 2, 4, P)

            def keys(t):
                return SEG if t < 2 else T

            def pe(e):
                for s in range(n + 3):
                    if s < n:
                        h, t = items[s]
                        if s >= 3:
                            e.wait_ge(s_mk if gqa else s_ex, s - 2)
                        if gqa:
                            r, q, k = slice(64 * (h % 2), 64 * (h % 2) + 64), qT[:, h // 2, :], kT2[:, h // 4, :]
                        else:
                            r, q, k = slice(0, QK), qT[:, h, :], kTm[:, h, :]
                        e.matmul(PS[:, s % 3, 0:keys(t)], q[r, t * P:(t + 1) * P], k[r, 0:keys(t)], start=True, stop=True).then_inc(s_sc, 1)
                    i = s - 2
                    if 0 <= i < n:
                        h, t = items[i]
                        e.wait_ge(s_p, i + 1)
                        if i >= 2:
                            e.wait_ge(s_pt, i - 1)
                        for k in range(keys(t) // P):
                            m = e.transpose(PS[:, 3 + i % 2, k * P:(k + 1) * P], PB[:, i % 3, k * P:(k + 1) * P], ident)
                        m.then_inc(s_t, 1)
                    i = s - 3
                    if 0 <= i < n:
                        h, t = items[i]
                        e.wait_ge(s_pt, i + 1)
                        if i >= 2:
                            e.wait_ge(s_o, i - 1)
                        r = slice(64 * (h % 2), 64 * (h % 2) + 64)
                        nk = keys(t) // P
                        for k in range(nk):
                            if gqa:
                                v = ZA[:, k, Z_GV + (h // 4) * HD:Z_GV + (h // 4 + 1) * HD]
                            else:
                                v = V[:, k, h * HD:(h + 1) * HD]
                            m = e.matmul(PS[r, 5 + i % 2, 0:P], v, PT[:, i % 2, k, :], start=k == 0, stop=k == nk - 1)
                        m.then_inc(s_pv, 1)

            def act(e, ch):
                for s in range(n + 3):
                    if s < n:
                        h, t = items[s]
                        nk = keys(t)
                        e.wait_ge(s_mx, s + 1)
                        if s >= 3:
                            e.wait_ge(s_t, s - 2)
                        c = s % 4
                        if gqa:
                            e.activation(es[:, c:c + 1], sink[:, h:h + 1], ACT.Exp, bias=nm_[:, c:c + 1])
                        e.activation(PB[:, s % 3, 0:nk], SB[:, s % 3, 0:nk] if gqa else PS[:, s % 3, 0:nk], ACT.Exp,
                                     bias=nm_[:, c:c + 1], scale=scale, accum_out=rs[:, c:c + 1]).then_inc(s_ex, 1)
                    i = s - 2
                    if 0 <= i < n:
                        h, t = items[i]
                        nk = keys(t) // P
                        e.wait_ge(s_t, i + 1)
                        if i >= 2:
                            e.wait_ge(s_pv, i - 1)
                        e.activation(PT[:, i % 2, 0:nk, :], PS[:, 3 + i % 2, 0:nk * P].rearrange("p (k q) -> p k q", k=nk), ACT.Copy).then_inc(s_pt, 1)
                    i = s - 3
                    if 0 <= i < n:
                        h, t = items[i]
                        r = slice(64 * (h % 2), 64 * (h % 2) + 64)
                        e.wait_ge(s_pv, i + 1)
                        e.activation(dst[r, h // 2, t * P:(t + 1) * P], PS[r, 5 + i % 2, 0:P], ACT.Copy).then_inc(s_o, 1)

            def dve(e, ch):
                for s in range(n + 1):
                    if s < n:
                        h, t = items[s]
                        nk = keys(t)
                        c = s % 4
                        e.wait_ge(s_sc, s + 1)
                        if s >= 3:
                            e.wait_ge(s_ex, s - 2)
                        src = PS[:, s % 3, 0:nk]
                        if gqa:
                            if t >= 2:
                                e.tensor_tensor(SB[:, s % 3, :], src, cst(f"win{t - 2}"), ALU.add).then_inc(s_mk, 1)
                            else:
                                e.tensor_copy(SB[:, s % 3, 0:nk], src).then_inc(s_mk, 1)
                            e.wait_ge(s_mk, s + 1)
                            src = SB[:, s % 3, 0:nk]
                        ch.run(e.tensor_reduce(mx[:, c:c + 1], src, AX.X, ALU.max))
                        if gqa:
                            ch.run(e.tensor_scalar(mx[:, c:c + 1], mx[:, c:c + 1], scale, sink[:, h:h + 1], ALU.mult, ALU.max))
                        e.tensor_scalar(nm_[:, c:c + 1], mx[:, c:c + 1], -1.0 if gqa else -scale, None, ALU.mult).then_inc(s_mx, 1)
                    i = s - 1
                    if 0 <= i:
                        h, t = items[i]
                        nk = keys(t)
                        c = i % 4
                        e.wait_ge(s_ex, i + 1)
                        if gqa:
                            ch.run(e.tensor_tensor(rs[:, c:c + 1], rs[:, c:c + 1], es[:, c:c + 1], ALU.add))
                        ch.run(e.reciprocal(rr[:, c:c + 1], rs[:, c:c + 1]))
                        e.tensor_scalar(PB[:, i % 3, 0:nk], PB[:, i % 3, 0:nk], rr[:, c:c + 1], None, ALU.mult).then_inc(s_p, 1)
            return dict(act=act, pe=pe, dve=dve)

        DT = ar(B0, NT, 3 * DW)
        qTd = ar(B0 + 6144, 4, T)
        kTd = ar(B0 + 8192, 4, T)
        E0 = B0 + 10240
        g2, gc, egc, ekg, beta, beg = (sm(64 * i, 2, NT, H) for i in range(6))
        glb = sm(384, 2, NT, 2, 4)

        def stage_dn_prep(l, t0):
            nm = f"s_dp_"
            s_w, s_zp, s_xc, s_cv, s_sl, s_tp, s_te, s_cw, s_cwe, s_ab, s_sq, s_ss, s_rt, s_nrm, s_qp, s_qe, s_g, s_gp, s_ga, s_gb, s_gz = (
                sem(nm + x) for x in ("w", "zp", "xc", "cv", "sl", "tp", "te", "cw", "cwe", "ab", "sq", "ss", "rt", "nrm", "qp", "qe", "g", "gp", "ga", "gb", "gz"))
            cwr = ar(E0 + 2064, 1536)[0:CONV]
            CW = sm(512, 12, CONV)
            XC = ar(E0, 2, 2, SEG + 4)
            YC = ar(E0 + 1040, 2, 2, SEG)
            sq = ar(E0, 2, D)
            ss, rt = sm(576, NT, 16), sm(640, NT, 16)
            alog, dtb = sm(704, 16), sm(720, 16)
            w1, w2, w3, w4 = (sm(736 + 64 * i, NT, 16) for i in range(4))

            def act(e, ch):
                e.dma_start(cwr, a["dn_conv"][l]).then_inc(s_w, 16)
                e.dma_start(alog, a["dn_a_log"][l:l + 1].rearrange("o d h -> o (d h)").broadcast_to([P, 16])).then_inc(s_ab, 16)
                e.dma_start(dtb, a["dn_dt_bias"][l:l + 1].rearrange("o d h -> o (d h)").broadcast_to([P, 16])).then_inc(s_ab, 16)
                e.wait_ge(s_g, 1)
                ch.run(e.activation(w2, w1, ACT.Abs))
                ch.run(e.activation(w2, w2, ACT.Exp, scale=-1.0))
                ch.run(e.activation(w2, w2, ACT.Ln, bias=1.0))
                e.wait_ge(s_ab, 32)
                ch.run(e.activation(alog, alog, ACT.Exp))
                e.sem_inc(s_ga, 1)
                for d in range(2):
                    ch.run(e.activation(beta[:, d], ZA[:, :, Z_B + d * H:Z_B + (d + 1) * H], ACT.Sigmoid))
                e.sem_inc(s_gb, 1)
                for m in range(12 + 2):
                    if m < 12:
                        e.wait_ge(s_zp, m + 1)
                        if m == 0:
                            e.wait_ge(s_gz, 1)
                        if m >= 2:
                            e.wait_ge(s_cv, m - 1)
                        e.activation(XC[:, m % 2, :, 2:2 + SEG], PS[:, m % 2, :].rearrange("p (s n) -> p s n", s=2), ACT.Copy).then_inc(s_xc, 1)
                    if m >= 1 and m - 1 < 12:
                        i = m - 1
                        e.wait_ge(s_cv, i + 1)
                        e.activation(YC[:, i % 2], YC[:, i % 2], ACT.Silu).then_inc(s_sl, 1)
                    if m >= 2:
                        i = m - 2
                        e.wait_ge(s_tp, i + 1)
                        e.activation(DT[:, :, i * P:(i + 1) * P], PS[:, 2 + i % 2, :].rearrange("p (t c) -> p t c", t=NT), ACT.Copy).then_inc(s_te, 1)
                for t in range(NT):
                    if t == 0:
                        e.wait_ge(s_te, 12)
                        e.wait_ge(s_cv, 12)
                        e.wait_ge(s_tp, 12)
                    if t >= 2:
                        e.wait_ge(s_ss, t - 1)
                    e.activation(sq[:, t % 2, :], DT[:, t, 0:D], ACT.Square).then_inc(s_sq, 1)
                e.wait_ge(s_ss, NT + 1)
                e.activation(rt, ss, ACT.Sqrt).then_inc(s_rt, 1)
                for i in range(2 * NT):
                    e.wait_ge(s_qp, i + 1)
                    t, half = i // 2, i % 2
                    dst = (qTd, kTd)[half]
                    e.activation(dst[:, :, t * P:(t + 1) * P], PS[:, 4 + i % 2, :].rearrange("p (j q) -> p j q", j=4), ACT.Copy).then_inc(s_qe, 1)
                e.wait_ge(s_gp, 1)
                pg = PS[:, 7, :]
                v64 = lambda o: pg[:, o:o + 64].rearrange("p (d t h) -> p d t h", d=2, t=NT)
                ch.run(e.activation(gc, v64(0), ACT.Copy))
                ch.run(e.activation(egc, v64(0), ACT.Exp))
                for c in range(2):
                    for p in range(2):
                        src = pg[64 * p:64 * p + 64, 128 + 64 * c:192 + 64 * c].rearrange("p (u j q) -> p u j q", u=8, q=2)[:, :, :, p]
                        o = glb[64 * p:64 * p + 64].rearrange("p d t c j -> p (d t) c j")[:, :, c, :]
                        ch.add(e.activation(o, src, ACT.Exp))
                ch.run(e.activation(w4.rearrange("p t n -> p (t n)"), pg[:, 64:128], ACT.Copy))
                e.sem_inc(s_ga, 1)
                e.wait_ge(s_g, 3)
                ch.run(e.activation(ekg, w3.rearrange("p t (a n) -> p (t a n)", a=2).rearrange("p (d t n) -> p d t n", d=2, t=NT), ACT.Exp))

            def dve(e, ch):
                ch.run(e.memset(XC[:, 0], 0.0))
                ch.run(e.memset(XC[:, 1], 0.0))
                e.sem_inc(s_gz, 1)
                e.wait_ge(s_ab, 32)
                ch.run(e.tensor_tensor(w1, ZA[:, :, Z_A:Z_A + 16], dtb.rearrange("p (o n) -> p o n", o=1).broadcast_to([P, NT, 16]), ALU.add))
                e.sem_inc(s_g, 1)
                e.wait_ge(s_ga, 1)
                ch.run(e.scalar_tensor_tensor(out=w1, in0=w1, scalar=0.0, in1=w2, op0=ALU.max, op1=ALU.add))
                ch.run(e.tensor_scalar(w1, w1, -1.0, None, ALU.mult))
                for d in range(2):
                    ch.run(e.tensor_tensor(g2[:, d], w1[:, :, d * H:(d + 1) * H],
                                           alog[:, d * H:(d + 1) * H].rearrange("p (o n) -> p o n", o=1).broadcast_to([P, NT, H]), ALU.mult))
                e.sem_inc(s_g, 1)
                e.wait_ge(s_cw, 1)
                ch.run(e.tensor_copy(CW, PS[:, 6, 0:60].rearrange("p (m j) -> p m j", m=12)))
                for m in range(12):
                    e.wait_ge(s_xc, m + 1)
                    if m >= 2:
                        e.wait_ge(s_tp, m - 1)
                    x, y = XC[:, m % 2], YC[:, m % 2]
                    ch.run(e.tensor_scalar(y, x[:, :, 0:SEG], CW[:, m, 0:1], None, ALU.mult))
                    for j in range(1, CONV):
                        ins = e.scalar_tensor_tensor(out=y, in0=x[:, :, j:j + SEG], scalar=CW[:, m, j:j + 1], in1=y, op0=ALU.mult, op1=ALU.add)
                        if j < CONV - 1:
                            ch.run(ins)
                        else:
                            ins.then_inc(s_cv, 1)
                            e.wait_ge(s_cv, m + 1)
                for t in range(NT):
                    e.wait_ge(s_sq, t + 1)
                    e.tensor_reduce(ss[:, t, :], sq[:, t % 2, :].rearrange("p (h n) -> p h n", n=HD), AX.X, ALU.add).then_inc(s_ss, 1)
                e.wait_ge(s_ss, NT)
                ch.run(e.tensor_scalar(ss, ss, 1e-6, None, ALU.add))
                e.sem_inc(s_ss, 1)
                e.wait_ge(s_rt, 1)
                ch.run(e.reciprocal(ss, rt))
                ch.run(e.tensor_scalar(ss[:, :, 0:H], ss[:, :, 0:H], HD ** -0.5, None, ALU.mult))
                for t in range(NT):
                    qk = DT[:, t, 0:D].rearrange("p (h n) -> p h n", n=HD)
                    e.tensor_tensor(qk, qk, ss[:, t, :].rearrange("p (h o) -> p h o", o=1).broadcast_to([P, 16, HD]), ALU.mult).then_inc(s_nrm, 1)
                e.wait_ge(s_ga, 2)
                ch.run(e.tensor_tensor(w3.rearrange("p t n -> p (t n)"), w4.rearrange("p t n -> p (t n)"), gc.rearrange("p d t h -> p (d t h)"), ALU.subtract))
                e.sem_inc(s_g, 1)
                e.wait_ge(s_gb, 1)
                ch.run(e.tensor_tensor(beg, beta, egc, ALU.mult))
                ch.run(e.tensor_copy(DZ[:, t0:NT], ZA[:, t0:NT, Z_DZ:Z_DZ + DW]))

            def pe(e):
                e.wait_ge(s_w, 16)
                for m in range(12):
                    x = e.transpose(PS[:, 6, m * CONV:(m + 1) * CONV], cwr[:, m * P:(m + 1) * P], ident[0:CONV, 0:CONV])
                x.then_inc(s_cw, 1)
                for m in range(12 + 1):
                    if m < 12:
                        key = ("dqkv", l, m // 4)
                        landed(e, key)
                        w = slot(key, 0, KT, 512)
                        if m >= 2:
                            e.wait_ge(s_xc, m - 1)
                        for k in range(KT):
                            x = e.matmul(PS[:, m % 2, :], w[:, k, (m % 4) * P:(m % 4 + 1) * P], UT[:, k, :], start=k == 0, stop=k == KT - 1)
                        x.then_inc(s_zp, 1)
                        if m % 4 == 3:
                            e.wait_ge(s_zp, m + 1)
                            e.sem_inc(s_wfree, 1)
                    if m >= 1:
                        i = m - 1
                        e.wait_ge(s_sl, i + 1)
                        if i >= 2:
                            e.wait_ge(s_te, i - 1)
                        for t in range(NT):
                            y = YC[:, i % 2].rearrange("p s n -> p (s n)")
                            x = e.transpose(PS[:, 2 + i % 2, t * P:(t + 1) * P], y[:, t * P:(t + 1) * P], ident)
                        x.then_inc(s_tp, 1)
                for i in range(2 * NT):
                    t, half = i // 2, i % 2
                    e.wait_ge(s_nrm, t + 1)
                    if i >= 2:
                        e.wait_ge(s_qe, i - 1)
                    for j in range(4):
                        x = e.transpose(PS[:, 4 + i % 2, j * P:(j + 1) * P], DT[:, t, half * DW + j * P:half * DW + (j + 1) * P], ident)
                    x.then_inc(s_qp, 1)
                e.wait_ge(s_g, 2)
                g2f = g2.rearrange("p d t h -> p (d t h)")
                for d in range(2):
                    e.matmul(PS[:, 7, 32 * d:32 * d + 32], cst(f"tri{d}"), g2f[:, 32 * d:32 * d + 32], start=True, stop=True)
                e.matmul(PS[:, 7, 64:128], cst("blk"), g2f, start=True, stop=True)
                for c in range(2):
                    x = e.matmul(PS[:, 7, 128 + 64 * c:192 + 64 * c], cst(f"sel{c}"), g2f, start=True, stop=True)
                x.then_inc(s_gp, 1)
            return dict(act=act, pe=pe, dve=dve)

        O_DN = ar(B0 + 6144, 4, T)

        def by_parity(v, p):
            return v.rearrange("q (j p) -> q j p", p=2)[:, :, p:p + 1]

        def stage_dn_scan(l, t0):
            nm = f"s_ds_"
            pp = {k: [sem(f"{nm}{k}{p}") for p in range(2)] for k in ("gr", "df", "e", "a", "al", "x", "rt", "xp", "y", "vb", "uw", "ue", "kd")}
            s_S, s_ab, s_vn, s_cd = (sem(nm + x) for x in ("S", "ab", "vn", "cd"))
            U = ar(0, 2, 4, HD)
            WT = ar(512, 4, P)
            QKD = ar(1024, 2, 4, P)
            KG = ar(2048, 2, 4, HD)
            S = ar(2560, 2, 4, HD)
            O1, VN = ar(3072, 2, 4, HD), ar(3584, 2, 4, HD)
            AL = ar(4096, 2, 2, 4, P)
            A, R, TT, XP = (ar(E0 + 1024 * i, 2, 4, P) for i in range(4))
            VB = [AL[:, p, 0, 0:2, :].rearrange("q j n -> q (j n)").rearrange("q (j n) -> q j n", n=HD) for p in range(2)]
            KBG = [AL[:, p, 0, 2:4, :].rearrange("q j n -> q (j n)").rearrange("q (j n) -> q j n", n=HD) for p in range(2)]
            units = [(d, t) for s in range(4) for d, t in ((0, s), (1, (1, 0, 3, 2)[s]))]
            first = {}
            for u, (d, t) in enumerate(units):
                first.setdefault(t, u)

            def bank(p, b):
                return PS[:, 4 * p + b, :].rearrange("q (j n) -> q j n", j=4)

            def mask(x):
                return x.rearrange("q (o n) -> q o n", o=1).broadcast_to([P, 4, P])

            def per_head(v, d, t, p, n=P, r=slice(0, P)):
                return by_parity(v[r, d, t, :], p).broadcast_to([r.stop - r.start, 4, n])

            def heads(part, t, p):
                return DT[:, t, part * DW:(part + 1) * DW].rearrange("q (j p n) -> q j p n", p=2, n=HD)[:, :, p, :]

            def rows(p):
                return slice(64 * p, 64 * p + 64)

            def order(d):
                return (0, 1) if d == 0 else (1, 0)

            def pe(e):
                for u, (d, t) in enumerate(units):
                    tc = slice(t * P, (t + 1) * P)
                    e.wait_ge(s_S, 2 * u + 1)
                    for p in range(2):
                        for j in range(4):
                            h = 2 * j + p
                            g = g2[:, d, t, h:h + 1].broadcast_to([P, P])
                            e.matmul(bank(p, 0)[:, j], g, cst(f"tri{d}"), start=True, stop=True)
                            k, q = kTd[rows(p), j, tc], qTd[rows(p), j, tc]
                            e.matmul(bank(p, 1)[:, j], k, k, start=True, stop=True)
                            m = e.matmul(bank(p, 2)[:, j], k, q, start=True, stop=True)
                        m.then_inc(pp["gr"][p], 1)
                    for s in range(LEVELS):
                        for p in range(2):
                            e.wait_ge(pp["al"][p], LEVELS * u + s + 1)
                            if s:
                                e.wait_ge(pp["rt"][p], LEVELS * u + s)
                            for j in range(4):
                                m = e.matmul(bank(p, 3 if s == 0 else 0)[:, j], AL[:, p, s % 2, j, :], ident if s == 0 else R[:, p, j, :], start=True, stop=True)
                            m.then_inc(pp["x"][p], 1)
                        for p in range(2):
                            if s:
                                e.wait_ge(pp["xp"][p], (LEVELS - 1) * u + s)
                                for j in range(4):
                                    m = e.matmul(bank(p, 1)[:, j], TT[:, p, j, :], XP[:, p, j, :], start=True, stop=True)
                                    if s < LEVELS - 1:
                                        m = e.matmul(bank(p, 2)[:, j], XP[:, p, j, :], TT[:, p, j, :], start=True, stop=True)
                                m.then_inc(pp["y"][p], 1)
                    for p in range(2):
                        e.wait_ge(pp["vb"][p], u + 1)
                        e.wait_ge(pp["rt"][p], LEVELS * (u + 1))
                        for j in range(4):
                            e.matmul(PS[:, 4 * p + 3, j * HD:(j + 1) * HD], R[:, p, j, :], VB[p][:, j, :], start=True, stop=True)
                            m = e.matmul(bank(p, 0)[rows(p), j], KBG[p][:, j, :], R[:, p, j, :], start=True, stop=True)
                        m.then_inc(pp["uw"][p], 1)
                    for ci, c in enumerate(order(d)):
                        r = rows(c)
                        n = 2 * u + ci
                        if ci == 0:
                            for p in range(2):
                                e.wait_ge(pp["ue"][p], u + 1)
                                e.wait_ge(pp["kd"][p], u + 1)
                        e.wait_ge(s_S, n + 1)
                        for p in range(2):
                            for j in range(4):
                                m = e.matmul(PS[r, 4 * p, j * HD:(j + 1) * HD], WT[rows(p), j, r], S[rows(p), d, j, :], start=True, stop=True)
                                if t >= t0:
                                    m = e.matmul(PS[r, 4 * p, 256 + j * HD:256 + (j + 1) * HD], qTd[rows(p), j, t * P + 64 * c:t * P + 64 * c + 64], S[rows(p), d, j, :], start=True, stop=True)
                        m.then_inc(s_ab, 1)
                        e.wait_ge(s_vn, n + 1)
                        for p in range(2):
                            for j in range(4):
                                if t >= t0:
                                    e.matmul(PS[r, 4 * p + 1, j * HD:(j + 1) * HD], QKD[r, p, j, r], VN[r, p, j, :], start=True, stop=True)
                                m = e.matmul(PS[rows(p), 4 * p + 2, j * HD:(j + 1) * HD], KG[r, p, j, :], VN[r, p, j, :], start=True, stop=True)
                        m.then_inc(s_cd, 1)

            def act(e, ch):
                for u, (d, t) in enumerate(units):
                    for p in range(2):
                        e.wait_ge(pp["df"][p], u + 1)
                        ch.run(e.activation(XP[:, p], XP[:, p], ACT.Abs))
                        e.activation(XP[:, p], XP[:, p], ACT.Exp, scale=-1.0).then_inc(pp["e"][p], 1)
                    for s in range(1, LEVELS):
                        for p in range(2):
                            e.wait_ge(pp["x"][p], LEVELS * u + s + 1)
                            if s == 1:
                                e.wait_ge(pp["a"][p], u + 1)
                            e.activation(XP[:, p], bank(p, 0), ACT.Copy).then_inc(pp["xp"][p], 1)
                    for p in range(2):
                        e.wait_ge(pp["uw"][p], u + 1)
                        e.activation(U[:, p], PS[:, 4 * p + 3, 0:256].rearrange("q (j n) -> q j n", j=4), ACT.Copy)
                        e.activation(WT[rows(p)], bank(p, 0)[rows(p)], ACT.Copy).then_inc(pp["ue"][p], 1)

            def dve(e, ch):
                ch.run(e.memset(S, 0.0))
                e.sem_inc(s_S, 1)
                for u, (d, t) in enumerate(units):
                    for p in range(2):
                        e.wait_ge(pp["gr"][p], u + 1)
                        e.tensor_tensor(XP[:, p], bank(p, 0), per_head(gc, d, t, p), ALU.subtract).then_inc(pp["df"][p], 1)
                    for p in range(2):
                        e.wait_ge(pp["e"][p], u + 1)
                        ch.add(e.tensor_tensor(QKD[:, p], bank(p, 2), XP[:, p], ALU.mult))
                        ch.run(e.tensor_tensor(A[:, p], bank(p, 1), XP[:, p], ALU.mult))
                        e.tensor_tensor(A[:, p], A[:, p], per_head(beta, d, t, p), ALU.mult).then_inc(pp["a"][p], 1)
                    for s in range(LEVELS):
                        for p in range(2):
                            n = LEVELS * u + s + 1
                            if s == 0:
                                e.wait_ge(pp["al"][p], n)
                                ch.add(e.tensor_tensor(TT[:, p], mask(ident), AL[:, p, 0], ALU.subtract))
                                e.wait_ge(pp["x"][p], n)
                                ch.add(e.tensor_tensor(R[:, p], mask(ident), bank(p, 3), ALU.subtract))
                            else:
                                e.wait_ge(pp["y"][p], (LEVELS - 1) * u + s)
                                ch.add(e.tensor_tensor(R[:, p], R[:, p], bank(p, 1), ALU.subtract))
                                if s < LEVELS - 1:
                                    ch.add(e.tensor_tensor(TT[:, p], TT[:, p], bank(p, 2), ALU.subtract))
                            ch.sync()
                            e.sem_inc(pp["rt"][p], 1)
                    for ci, c in enumerate(order(d)):
                        r = rows(c)
                        n = 2 * u + ci
                        e.wait_ge(s_ab, n + 1)
                        for p in range(2):
                            if ci == 0:
                                e.wait_ge(pp["ue"][p], u + 1)
                            ch.add(e.tensor_tensor(VN[r, p], U[r, p], PS[r, 4 * p, 0:256].rearrange("q (j n) -> q j n", j=4), ALU.subtract))
                        ch.sync()
                        e.sem_inc(s_vn, 1)
                        for p in range(2):
                            if t >= t0:
                                ch.add(e.tensor_tensor(O1[r, p], PS[r, 4 * p, 256:512].rearrange("q (j n) -> q j n", j=4), per_head(egc, d, t, p, HD, r), ALU.mult))
                        ch.add(e.tensor_tensor(S[:, d], S[:, d], glb[:, d, t, c, :].rearrange("q (j o) -> q j o", o=1).broadcast_to([P, 4, HD]), ALU.mult))
                        ch.sync()
                        e.wait_ge(s_cd, n + 1)
                        for p in range(2):
                            ch.add(e.tensor_tensor(S[rows(p), d], S[rows(p), d], PS[rows(p), 4 * p + 2, 0:256].rearrange("q (j n) -> q j n", j=4), ALU.add))
                            if t >= t0:
                                o = heads(0, t, p)[r]
                                cc = PS[r, 4 * p + 1, 0:256].rearrange("q (j n) -> q j n", j=4)
                                if first[t] == u:
                                    ch.add(e.tensor_tensor(o, O1[r, p], cc, ALU.add))
                                else:
                                    ch.run(e.tensor_tensor(O1[r, p], O1[r, p], cc, ALU.add))
                                    ch.add(e.tensor_tensor(o, o, O1[r, p], ALU.add))
                        ch.sync()
                        e.sem_inc(s_S, 1)

            def pool(e, ch):
                for u, (d, t) in enumerate(units):
                    e.wait_ge(s_S, 2 * u + 1)
                    for p in range(2):
                        ch.run(e.tensor_tensor(KG[:, p], heads(1, t, p), per_head(ekg, d, t, p, HD), ALU.mult))
                    for s in range(LEVELS):
                        for p in range(2):
                            if s == 0:
                                e.wait_ge(pp["a"][p], u + 1)
                            if s >= 2:
                                e.wait_ge(pp["x"][p], LEVELS * u + s - 1)
                                e.wait_ge(pp["rt"][p], LEVELS * u + s - 1)
                            e.tensor_tensor(AL[:, p, s % 2], A[:, p], mask(cst(f"lvl{d}{s}")), ALU.mult).then_inc(pp["al"][p], 1)
                            if s == 1:
                                ch.run(e.tensor_tensor(QKD[:, p], QKD[:, p], mask(cst(f"tri{d}")), ALU.mult))
                                e.sem_inc(pp["kd"][p], 1)
                    for p in range(2):
                        e.wait_ge(pp["x"][p], LEVELS * u + LEVELS - 1)
                        ch.add(e.tensor_tensor(VB[p], heads(2, t, p), per_head(beta, d, t, p, HD), ALU.mult))
                        ch.add(e.tensor_tensor(KBG[p], heads(1, t, p), per_head(beg, d, t, p, HD), ALU.mult))
                        ch.sync()
                        e.sem_inc(pp["vb"][p], 1)
            return dict(act=act, pe=pe, dve=dve, pool=pool)

        def stage_dn_out(l, t0):
            s_nw, s_sq, s_ss, s_rt, s_z, s_o, s_tp, s_te = (sem(f"s_do_{x}") for x in ("nw", "sq", "ss", "rt", "z", "o", "tp", "te"))
            nw = sm(576, HD)
            ss, rt = sm(640, NT, H), sm(672, NT, H)
            sq = ar(0, NT, DW)
            zs = ar(2048, NT, DW)
            tiles = range(t0, NT)
            nt = len(tiles)

            def act(e, ch):
                e.dma_start(nw, a["dn_norm"][l:l + 1, :].broadcast_to([P, HD])).then_inc(s_nw, 16)
                e.activation(sq[:, t0:NT], DT[:, t0:NT, 0:DW], ACT.Square).then_inc(s_sq, 1)
                e.activation(zs[:, t0:NT], DZ[:, t0:NT], ACT.Silu).then_inc(s_z, 1)
                e.wait_ge(s_ss, 1)
                e.activation(rt[:, t0:NT], ss[:, t0:NT], ACT.Sqrt).then_inc(s_rt, 1)
                for i, t in enumerate(tiles):
                    e.wait_ge(s_tp, i + 1)
                    e.activation(O_DN[:, :, t * P:(t + 1) * P], PS[:, i % 2, :].rearrange("p (j q) -> p j q", j=4), ACT.Copy).then_inc(s_te, 1)

            def dve(e, ch):
                e.wait_ge(s_sq, 1)
                ch.run(e.tensor_reduce(ss[:, t0:NT], sq[:, t0:NT].rearrange("p t (h n) -> p t h n", n=HD), AX.X, ALU.add))
                ch.run(e.tensor_scalar(ss[:, t0:NT], ss[:, t0:NT], 1.0 / HD, EPS, ALU.mult, ALU.add))
                e.sem_inc(s_ss, 1)
                e.wait_ge(s_rt, 1)
                ch.run(e.reciprocal(ss[:, t0:NT], rt[:, t0:NT]))
                e.wait_ge(s_nw, 16)
                e.wait_ge(s_z, 1)
                for t in tiles:
                    o = DT[:, t, 0:DW].rearrange("p (h n) -> p h n", n=HD)
                    z = zs[:, t].rearrange("p (h n) -> p h n", n=HD)
                    ch.add(e.tensor_tensor(z, z, nw.rearrange("p (o n) -> p o n", o=1).broadcast_to([P, H, HD]), ALU.mult))
                    ch.run(e.tensor_tensor(o, o, ss[:, t, :].rearrange("p (h o) -> p h o", o=1).broadcast_to([P, H, HD]), ALU.mult))
                    e.tensor_tensor(o, o, z, ALU.mult).then_inc(s_o, 1)

            def pe(e):
                for i, t in enumerate(tiles):
                    e.wait_ge(s_o, i + 1)
                    if i >= 2:
                        e.wait_ge(s_te, i - 1)
                    for j in range(4):
                        m = e.transpose(PS[:, i % 2, j * P:(j + 1) * P], DT[:, t, j * P:(j + 1) * P], ident)
                    m.then_inc(s_tp, 1)
            return dict(act=act, pe=pe, dve=dve)

        def layer_norm(e, ch, t, i, lnb, s_var, s_std):
            st, mv, rs = sm(0, 2, 6), sm(16 + 4 * i, 2), sm(48 + i, 1)
            for c in range(2):
                ch.add(e.bn_stats(st[:, c, :], X[:, t, c * 512:(c + 1) * 512]))
            ch.sync()
            ch.run(e.bn_aggr(mv, st.rearrange("p a b -> p (a b)")))
            ch.run(e.tensor_scalar(mv[:, 1:2], mv[:, 1:2], EPS, None, ALU.add))
            e.sem_inc(s_var, 1)
            e.wait_ge(s_std, i + 1)
            ch.run(e.reciprocal(rs, sm(32 + i, 1)))
            ch.run(e.tensor_scalar(X[:, t, :], X[:, t, :], mv[:, 0:1], rs, ALU.subtract, ALU.mult))
            ch.run(e.tensor_tensor(X[:, t, :], X[:, t, :], lnb[:, 0], ALU.mult))
            ch.run(e.tensor_tensor(X[:, t, :], X[:, t, :], lnb[:, 1], ALU.add))

        def roots(e, n, s_var, s_std):
            for i in range(n):
                e.wait_ge(s_var, i + 1)
                e.activation(sm(32 + i, 1), sm(17 + 4 * i, 1), ACT.Sqrt).then_inc(s_std, 1)

        def stage_merge(l, t0):
            nm = f"s_mg_"
            s_gp, s_sg, s_op, s_tm, s_mt, s_ld, s_yp, s_ye, s_var, s_std = (sem(nm + x) for x in ("gp", "sg", "op", "tm", "mt", "ld", "yp", "ye", "var", "std"))
            MT = ar(0, KT, T)
            TM = ar(4096, 2, T)
            SGb = ar(B0, KT, T)
            GM = ar(B0 + 4096 + 4096, 2, 1, D)
            LNB = ar(B0 + 4096 + 6144, 2, D)
            n0 = t0 * P
            tiles = range(t0, NT)
            nt = len(tiles)
            src = (O_MLA, O_DN, O_GQA)

            def pe(e):
                for b in range(3):
                    for mt in range(KT):
                        i = b * KT + mt
                        key = ("gate", l, b, mt // 4)
                        landed(e, key)
                        w = slot(key, 0, KT, 512)
                        if i >= 2:
                            e.wait_ge(s_sg, i - 1)
                        for k in range(KT):
                            m = e.matmul(PS[:, i % 2, n0:T], w[:, k, (mt % 4) * P:(mt % 4 + 1) * P], UT[:, k, n0:T], start=k == 0, stop=k == KT - 1)
                        m.then_inc(s_gp, 1)
                        if mt % 4 == 3:
                            e.wait_ge(s_gp, i + 1)
                            e.sem_inc(s_wfree, 1)
                    key = ("o", l, b)
                    landed(e, key)
                    w = slot(key, 0, 4, D)
                    for mt in range(KT):
                        i = b * KT + mt
                        if i >= 2:
                            e.wait_ge(s_tm, i - 1)
                        for k in range(4):
                            m = e.matmul(PS[:, 2 + i % 2, n0:T], w[:, k, mt * P:(mt + 1) * P], src[b][:, k, n0:T], start=k == 0, stop=k == 3)
                        m.then_inc(s_op, 1)
                    e.wait_ge(s_op, KT * (b + 1))
                    e.sem_inc(s_wfree, 1)
                e.wait_ge(s_tm, 3 * KT)
                e.wait_ge(s_mt, 2 * KT)
                for c in range(2):
                    key = ("out", l, c)
                    landed(e, key)
                    w = slot(key, 0, KT, 512)
                    for ti, t in enumerate(tiles):
                        i = c * nt + ti
                        if i >= 4:
                            e.wait_ge(s_ye, i - 3)
                        for k in range(KT):
                            m = e.matmul(PS[:, 4 + i % 4, :], MT[:, k, t * P:(t + 1) * P], w[:, k, :], start=k == 0, stop=k == KT - 1)
                        m.then_inc(s_yp, 1)
                    e.wait_ge(s_yp, nt * (c + 1))
                    e.sem_inc(s_wfree, 1)

            def act(e, ch):
                modulation(e, l, (2,), GM, s_ld, range(t0 // 2, 2))
                for i, nm_ in enumerate(("ln1_g", "ln1_b")):
                    e.dma_start(LNB[:, i, :], a[nm_][l:l + 1, :].broadcast_to([P, D])).then_inc(s_ld, 16)
                for i in range(3 * KT):
                    e.wait_ge(s_gp, i + 1)
                    if i >= KT:
                        e.wait_ge(s_tm, i - KT + 1)
                    e.activation(SGb[:, i % KT, n0:T], PS[:, i % 2, n0:T], ACT.Sigmoid).then_inc(s_sg, 1)
                roots(e, nt, s_var, s_std)

            def dve(e, ch):
                for i in range(3 * KT):
                    mt = i % KT
                    e.wait_ge(s_op, i + 1)
                    e.wait_ge(s_sg, i + 1)
                    if i >= KT + 2:
                        e.wait_ge(s_mt, i - KT - 1)
                    o = MT[:, mt, n0:T] if i < KT else TM[:, i % 2, n0:T]
                    e.tensor_tensor(o, SGb[:, mt, n0:T], PS[:, 2 + i % 2, n0:T], ALU.mult).then_inc(s_tm, 1)
                e.wait_ge(s_ld, 64 if t0 == 0 else 48)
                ty = TM
                for c in range(2):
                    for ti, t in enumerate(tiles):
                        i = c * nt + ti
                        e.wait_ge(s_yp, i + 1)
                        if i == 0:
                            e.wait_ge(s_mt, 2 * KT)
                        o = slice(c * 512, (c + 1) * 512)
                        e.tensor_tensor(ty[:, i % 2, :], PS[:, 4 + i % 4, :], GM[:, t // 2, 0, o], ALU.mult).then_inc(s_ye, 1)
                        e.wait_ge(s_ye, i + 1)
                        ch.run(e.scalar_tensor_tensor(out=X[:, t, o], in0=X[:, t, o], scalar=ALPHA, in1=ty[:, i % 2, :], op0=ALU.mult, op1=ALU.add))
                for i, t in enumerate(tiles):
                    layer_norm(e, ch, t, i, LNB, s_var, s_std)

            def pool(e, ch):
                for i in range(KT, 3 * KT):
                    e.wait_ge(s_tm, i + 1)
                    if i >= 2 * KT:
                        e.wait_ge(s_mt, i - 2 * KT + 1)
                    mt = i % KT
                    e.tensor_tensor(MT[:, mt, n0:T], MT[:, mt, n0:T], TM[:, i % 2, n0:T], ALU.add).then_inc(s_mt, 1)
            return dict(act=act, pe=pe, dve=dve, pool=pool)

        FS = ar(0, NT, D)
        R0 = 4096
        DEST = ar(R0, NT, NE)
        RV = ar(R0 + 256, NT, NE)
        WK = sm(1000, TOPK, NT)
        M0 = R0 + 512
        XG = ar(M0, 2, D)

        def stage_route(l, t0):
            nm = f"s_ro_"
            s_b, s_lg, s_sc, s_m, s_ct, s_ti, s_be, s_gp, s_sg, s_h, s_hp, s_he, s_yp, s_ye, s_cs = (
                sem(nm + x) for x in ("b", "lg", "sc", "m", "ct", "ti", "be", "gp", "sg", "h", "hp", "he", "yp", "ye", "cs"))
            tiles = range(t0, NT)
            nt = len(tiles)
            Q0 = M0 + 2048
            SC, SEL, MK, W, EQ, CUM, RM, TMP = (ar(Q0 + 256 * i, NT, NE) for i in range(8))
            PR = ar(Q0 + 2048, NT, NG, NG)
            PE_ = ar(Q0 + 2304, NT, NG, NG)
            M8 = ar(Q0 + 2560, NT, NG, 8)
            BIAS = ar(Q0 + 2816, NE)
            CNT, NBK, CB_, T64 = (ar(Q0 + 2880 + 64 * i, NE) for i in range(4))
            HS = ar(Q0 + 3200, 2, FE)
            SGs = ar(Q0 + 3712, 2, FE)
            HTs = ar(Q0 + 4224, 2, 2, P)
            GS, RK, GMK = (sm(128 + 32 * i, NT, NG) for i in range(3))
            V8, NGT, SUM = sm(224, NT, 8), sm(256, NT), sm(260, NT)
            n64 = sm(264, 1)
            be = sm(268, 1)

            def tb(v, n):
                return v.rearrange("p (o n) -> p o n", o=1).broadcast_to([P, nt, n])

            def act(e, ch):
                e.dma_start(BIAS, a["router_bias"][l:l + 1, :].broadcast_to([P, NE])).then_inc(s_b, 16)
                e.wait_ge(s_lg, 1)
                e.activation(SC[:, t0:NT], PS[:, 0, t0 * NE:NT * NE].rearrange("p (t n) -> p t n", t=nt), ACT.Sigmoid).then_inc(s_sc, 1)
                for i in range(nt):
                    e.wait_ge(s_gp, i + 1)
                    e.activation(SGs[:, i % 2], PS[:, 2 + i % 2, 0:FE], ACT.Silu).then_inc(s_sg, 1)
                    e.wait_ge(s_hp, i + 1)
                    e.activation(HTs[:, i % 2], PS[:, 4, 0:256].rearrange("p (k q) -> p k q", k=2), ACT.Copy).then_inc(s_he, 1)
                    for c in range(2):
                        e.wait_ge(s_yp, 2 * i + c + 1)
                        e.activation(FS[:, t0 + i, c * 512:(c + 1) * 512], PS[:, 6 + c, :], ACT.Copy).then_inc(s_ye, 1)
                e.wait_ge(s_ti, 1)
                e.dma_start(blk_d, BEI[:, :]).then_inc(s_be, 16)
                e.wait_ge(s_be, 16)
                e.dma_start(EXPERT[:, :], blk_d.rearrange("p o -> o p")).then_inc(s_be, 16)
                e.wait_ge(s_be, 32)

            def pe(e):
                landed(e, ("router", l))
                w = slot(("router", l), 0, KT, NE)
                for t in tiles:
                    for k in range(KT):
                        m = e.matmul(PS[:, 0, t * NE:(t + 1) * NE], UT[:, k, t * P:(t + 1) * P], w[:, k, :], start=k == 0, stop=k == KT - 1)
                m.then_inc(s_lg, 1)
                e.wait_ge(s_lg, 1)
                e.sem_inc(s_wfree, 1)
                landed(e, ("shgu", l))
                landed(e, ("shd", l))
                wg, wu = slot(("shgu", l), 0, KT, FE), slot(("shgu", l), KT * FE, KT, FE)
                wd = slot(("shd", l), 0, 2, D)
                for i in range(nt + 1):
                    if i < nt:
                        t = t0 + i
                        if i >= 2:
                            e.wait_ge(s_h, i - 1)
                        for half, ww in ((0, wg), (1, wu)):
                            for k in range(KT):
                                m = e.matmul(PS[:, 2 + i % 2, half * FE:(half + 1) * FE], UT[:, k, t * P:(t + 1) * P], ww[:, k, :], start=k == 0, stop=k == KT - 1)
                        m.then_inc(s_gp, 1)
                    if i >= 1:
                        j = i - 1
                        e.wait_ge(s_h, j + 1)
                        if j >= 1:
                            e.wait_ge(s_he, j)
                        for k in range(2):
                            m = e.transpose(PS[:, 4, k * P:(k + 1) * P], HS[:, j % 2, k * P:(k + 1) * P], ident)
                        m.then_inc(s_hp, 1)
                        e.wait_ge(s_he, j + 1)
                        for c in range(2):
                            if j >= 1:
                                e.wait_ge(s_ye, 2 * j + c - 1)
                            for k in range(2):
                                m = e.matmul(PS[:, 6 + c, :], HTs[:, j % 2, k, :], wd[:, k, c * 512:(c + 1) * 512], start=k == 0, stop=k == 1)
                            m.then_inc(s_yp, 1)
                e.wait_ge(s_yp, 2 * nt)
                e.sem_inc(s_wfree, 2)
                e.wait_ge(s_m, 1)
                for t in tiles:
                    for t2 in range(t0, t + 1):
                        m = e.matmul(PS[:, 1, t * NE:(t + 1) * NE], cst("ones" if t2 < t else "before"), MK[:, t2, :], start=t2 == t0, stop=t2 == t)
                for t in tiles:
                    m = e.matmul(PS[:, 1, 256:256 + NE], cst("ones"), MK[:, t, :], start=t == t0, stop=t == NT - 1)
                m.then_inc(s_ct, 1)

            def shared_hidden(e, i):
                e.wait_ge(s_sg, i + 1)
                if i >= 2:
                    e.wait_ge(s_hp, i - 1)
                e.tensor_tensor(HS[:, i % 2], SGs[:, i % 2], PS[:, 2 + i % 2, FE:2 * FE], ALU.mult).then_inc(s_h, 1)

            def dve(e, ch):
                R = slice(t0, NT)
                for i in range(nt):
                    shared_hidden(e, i)
                e.wait_ge(s_b, 16)
                e.wait_ge(s_sc, 1)
                ch.run(e.tensor_tensor(SEL[:, R], SC[:, R], tb(BIAS, NE), ALU.add))
                for t in tiles:
                    for g in range(NG):
                        ch.add(e.max(M8[:, t, g, :], SEL[:, t, g * 8:(g + 1) * 8]))
                ch.sync()
                ch.run(e.tensor_tensor(GS[:, R], M8[:, R, :, 0], M8[:, R, :, 1], ALU.add))
                gj = GS[:, R].rearrange("p t (o j) -> p t o j", o=1).broadcast_to([P, nt, NG, NG])
                gi = GS[:, R].rearrange("p t (i o) -> p t i o", o=1).broadcast_to([P, nt, NG, NG])
                low = cst("glow").rearrange("p (o i j) -> p o i j", o=1, i=NG).broadcast_to([P, nt, NG, NG])
                ch.add(e.tensor_tensor(PR[:, R], gj, gi, ALU.is_gt))
                ch.run(e.tensor_tensor(PE_[:, R], gj, gi, ALU.is_equal))
                ch.run(e.tensor_tensor(PE_[:, R], PE_[:, R], low, ALU.mult))
                ch.run(e.tensor_tensor(PR[:, R], PR[:, R], PE_[:, R], ALU.add))
                ch.run(e.tensor_reduce(RK[:, R], PR[:, R], AX.X, ALU.add))
                ch.run(e.tensor_scalar(GMK[:, R], RK[:, R], float(TOPG), None, ALU.is_lt))
                ch.run(e.tensor_scalar(RK[:, R], GMK[:, R], 1.0, -MASKED, ALU.subtract, ALU.mult))
                def grp(v):
                    return v.rearrange("p t (g o) -> p t g o", o=1).broadcast_to([P, nt, NG, 8])
                sel = SEL[:, R].rearrange("p t (g n) -> p t g n", g=NG)
                ch.run(e.tensor_tensor(sel, sel, grp(GMK[:, R]), ALU.mult))
                ch.run(e.tensor_tensor(sel, sel, grp(RK[:, R]), ALU.add))
                for t in tiles:
                    ch.add(e.max(V8[:, t, :], SEL[:, t, :]))
                ch.sync()
                thr = V8[:, R, 7:8].broadcast_to([P, nt, NE])
                ch.add(e.tensor_tensor(MK[:, R], SEL[:, R], thr, ALU.is_gt))
                ch.run(e.tensor_tensor(EQ[:, R], SEL[:, R], thr, ALU.is_equal))
                ch.run(e.tensor_reduce(NGT[:, R], MK[:, R], AX.X, ALU.add))
                ch.run(e.tensor_scalar(NGT[:, R], NGT[:, R], -1.0, float(TOPK), ALU.mult, ALU.add))
                ones = cst("ones")[:, 0:NE]
                for t in tiles:
                    ch.add(e.tensor_tensor_scan(CUM[:, t, :], ones, EQ[:, t, :], 0.0, ALU.mult, ALU.add))
                ch.sync()
                ch.run(e.tensor_tensor(CUM[:, R], CUM[:, R], NGT[:, R].rearrange("p (t o) -> p t o", o=1).broadcast_to([P, nt, NE]), ALU.is_le))
                ch.run(e.tensor_tensor(EQ[:, R], EQ[:, R], CUM[:, R], ALU.mult))
                ch.run(e.tensor_tensor(MK[:, R], MK[:, R], EQ[:, R], ALU.add))
                e.sem_inc(s_m, 1)
                ch.run(e.tensor_tensor(W[:, R], SC[:, R], MK[:, R], ALU.mult))
                ch.run(e.tensor_reduce(SUM[:, R], W[:, R], AX.X, ALU.add))
                ch.run(e.reciprocal(NGT[:, R], SUM[:, R]))
                ch.run(e.tensor_tensor(W[:, R], W[:, R], NGT[:, R].rearrange("p (t o) -> p t o", o=1).broadcast_to([P, nt, NE]), ALU.mult))
                ch.run(e.tensor_scalar(W[:, R], W[:, R], ROUTED_SCALE, None, ALU.mult))
                for t in tiles:
                    ch.add(e.tensor_tensor_scan(RM[:, t, :], ones, MK[:, t, :], 0.0, ALU.mult, ALU.add))
                ch.sync()
                ch.run(e.tensor_tensor(RM[:, R], RM[:, R], MK[:, R], ALU.mult))
                for k in range(TOPK):
                    ch.run(e.scalar_tensor_tensor(out=TMP[:, R], in0=RM[:, R], scalar=float(k + 1), in1=W[:, R], op0=ALU.is_equal, op1=ALU.mult))
                    ch.run(e.tensor_reduce(WK[:, k, R], TMP[:, R], AX.X, ALU.add))
                ch.run(e.tensor_scalar(RV[:, R], RM[:, R], float(T), -float(T + FAR), ALU.mult, ALU.add))
                ch.run(e.tensor_tensor(RV[:, R], RV[:, R], cst("tokid")[:, R].rearrange("p (t o) -> p t o", o=1).broadcast_to([P, nt, NE]), ALU.add))
                e.wait_ge(s_ct, 1)
                ch.run(e.tensor_copy(CNT, PS[:, 1, 256:256 + NE]))
                ch.run(e.tensor_scalar(NBK, CNT, 0.0, None, ALU.is_gt))
                for b in range(1, nt):
                    ch.run(e.scalar_tensor_tensor(out=NBK, in0=CNT, scalar=float(b * P), in1=NBK, op0=ALU.is_gt, op1=ALU.add))
                ch.run(e.tensor_tensor_scan(CB_, ones, NBK, 0.0, ALU.mult, ALU.add))
                ch.run(e.tensor_tensor(T64, CB_, NBK, ALU.subtract))
                ch.run(e.tensor_scalar(T64, T64, float(P), 1.0, ALU.mult, ALU.add))
                pos = PS[:, 1, t0 * NE:NT * NE].rearrange("p (t n) -> p t n", t=nt)
                ch.run(e.tensor_tensor(DEST[:, R], pos, tb(T64, NE), ALU.add))
                ch.run(e.tensor_tensor(DEST[:, R], DEST[:, R], MK[:, R], ALU.mult))
                ch.run(e.tensor_scalar(DEST[:, R], DEST[:, R], 1.0, None, ALU.subtract))
                ch.run(e.tensor_scalar(T64, CB_, cst("rowid"), None, ALU.is_le))
                ch.run(e.tensor_reduce(be, T64, AX.X, ALU.add))
                ch.run(e.tensor_scalar(be, be, float(NE - 1), None, ALU.min))
                ch.run(e.tensor_copy(BEI[:, :], be))
                ch.run(e.tensor_scalar(be, CB_[:, NE - 1:NE], 0.5, None, ALU.mult))
                ch.run(e.tensor_scalar(CNT[:, 0:NBLK // 2], cst("iota")[:, 0:NBLK // 2], be, None, ALU.is_lt))
                ch.run(e.tensor_reduce(n64, CNT[:, 0:NBLK // 2], AX.X, ALU.add))
                ch.run(e.tensor_copy(NPAIR[:, :], n64[0:1]))
                ch.run(e.memset(XG, 0.0))
                e.sem_inc(s_ti, 1)
            return dict(act=act, pe=pe, dve=dve)

        def expert_slot(q):
            flat = RING[:, :, :].rearrange("p s n -> p (s n)")[:, q * 6144:(q + 1) * 6144]
            return (flat[:, 0:2048].rearrange("p (k n) -> p k n", k=KT), flat[:, 2048:4096].rearrange("p (k n) -> p k n", k=KT),
                    flat[:, 4096:6144].rearrange("p (k n) -> p k n", k=2))

        def stage_experts(l, t0):
            m_ = moe[l] = {k: [sem(f"s_moe_{k}{q}") for q in range(2)] for k in MOE} | moe_dma[l]
            s_own = sem("s_moe_own")
            s_tick = sem("s_moe_tick")
            tiles = range(t0, NT)
            XT = ar(M0 + 2048, 2, KT, P)
            HB = ar(M0 + 4096, 2, FE)
            SGL = ar(M0 + 4608, 2, FE)
            HT = ar(M0 + 5120, 2, 2, P)
            YB = ar(M0 + 5632, 2, D)
            OH = ar(M0 + 7680, NT, P)
            DC = ar(M0 + 8192, NT)
            RC = ar(M0 + 8196, NT)
            LAST = ar(M0 + 8200, 1)

            def s(name, q):
                return m_[name][q]

            def pairs(e):
                return e.value_load(NPAIR[0:1, 0:1], min_val=1, max_val=NBLK // 2)

            def gather(e, q):
                e.indirect_dma_start(out=XG[:, q, :], out_offset=None, in_=u_d,
                                     in_offset=bass.IndirectOffsetOnAxis(ap=IXG[:, q:q + 1], axis=0),
                                     bounds_check=T - 1, oob_is_err=False).then_inc(s("xg", q), 16)

            def scatter(e, q):
                e.indirect_dma_start(out=y_d, out_offset=bass.IndirectOffsetOnAxis(ap=IXS[:, q:q + 1], axis=0),
                                     in_=YB[:, q, :], in_offset=None,
                                     bounds_check=TOPK * T - 1, oob_is_err=False).then_inc(s("sc", q), 16)

            def pool(e, ch):
                e.wait_ge(s_own, 4)
                for q in range(2):
                    scatter(e, q)
                for q in range(2):
                    e.wait_ge(s("ixd", q), 1)
                    gather(e, q)
                with e.Fori(0, pairs(e)) as i:
                    for q in range(2):
                        e.wait_ge(s("ixd", q), i + 2)
                        e.sem_inc(s_tick, 1)
                        gather(e, q)
                        e.wait_ge(s("ye", q), i * 2 + 4)
                        e.sem_inc(s_tick, 1)
                        scatter(e, q)

            def transposes(e, q):
                for k in range(KT):
                    mm = e.transpose(PS[:, k // 4, (k % 4) * P:(k % 4 + 1) * P], XG[:, q, k::KT], ident)
                mm.then_inc(s("tr", q), 1)

            def rows_of_slots(e, q):
                for t in tiles:
                    mm = e.matmul(PS[:, 6, 0:1], OH[:, t, :], RC[:, t:t + 1], start=t == t0, stop=t == NT - 1)
                mm.then_inc(s("ixp", q), 1)

            def pe(e):
                for q in range(2):
                    for x in ("gu", "ht", "y"):
                        e.sem_inc(s(x, q), 1)
                    e.wait_ge(s("oh", q), 1)
                    if q:
                        e.wait_ge(s("ixd", 0), 1)
                    rows_of_slots(e, q)
                e.wait_ge(s("xg", 0), 16)
                transposes(e, 0)
                with e.Fori(0, pairs(e)) as i:
                    for q in range(2):
                        wg, wu, wd = expert_slot(q)
                        e.wait_ge(s("xta", q), i + 1)
                        e.wait_ge(s("xtd", q), i + 1)
                        e.wait_ge(s("wl", q), i * 48 + 48)
                        e.wait_ge(s("h", 1 - q), i + 1 + q)
                        for k in range(KT):
                            e.matmul(PS[:, 2, 0:FE], XT[:, q, k, :], wg[:, k, :], start=k == 0, stop=k == KT - 1)
                        for k in range(KT):
                            mm = e.matmul(PS[:, 2, FE:2 * FE], XT[:, q, k, :], wu[:, k, :], start=k == 0, stop=k == KT - 1)
                        mm.then_inc(s("gu", q), 1)
                        e.wait_ge(s("xg", 1 - q), i * 16 + 16 * (q + 1))
                        transposes(e, 1 - q)
                        e.wait_ge(s("h", q), i + 2)
                        e.wait_ge(s("hte", 1 - q), i + 1 + q)
                        for k in range(2):
                            mm = e.transpose(PS[:, 3, k * P:(k + 1) * P], HB[:, q, k::2], ident)
                        mm.then_inc(s("ht", q), 1)
                        e.wait_ge(s("oh", q), i + 2)
                        e.wait_ge(s("ixd", 1 - q), i + 1 + q)
                        rows_of_slots(e, q)
                        e.wait_ge(s("hte", q), i + 2)
                        e.wait_ge(s("ye", 1 - q), i * 2 + 2 * q + 2)
                        for c in range(2):
                            for k in range(2):
                                mm = e.matmul(PS[:, 4 + c, :], HT[:, q, k, :], wd[:, k, c * 512:(c + 1) * 512], start=k == 0, stop=k == 1)
                        mm.then_inc(s("y", q), 1)

            def act(e, ch):
                def first_half(q):
                    return e.activation(XT[:, q, 0:4, :], PS[:, 0, :].rearrange("p (k n) -> p k n", k=4), ACT.Copy)
                for q in range(2):
                    e.sem_inc(s("hte", q), 1)
                    e.sem_inc(s("ye", q), 2)
                e.wait_ge(s("tr", 0), 1)
                first_half(0).then_inc(s("xta", 0), 1)
                with e.Fori(0, pairs(e)) as i:
                    for q in range(2):
                        e.wait_ge(s("gu", q), i + 2)
                        e.wait_ge(s("h", q), i + 1)
                        e.activation(SGL[:, q, :], PS[:, 2, 0:FE], ACT.Silu).then_inc(s("sg", q), 1)
                        e.wait_ge(s("tr", 1 - q), i + 1 + q)
                        e.wait_ge(s("gu", 1 - q), i + 1 + q)
                        first_half(1 - q).then_inc(s("xta", 1 - q), 1)
                        e.wait_ge(s("ht", q), i + 2)
                        e.wait_ge(s("y", q), i + 1)
                        e.activation(HT[:, q], PS[:, 3, 0:256].rearrange("p (k n) -> p k n", k=2), ACT.Copy).then_inc(s("hte", q), 1)
                        e.wait_ge(s("y", q), i + 2)
                        e.wait_ge(s("sc", q), i * 16 + 16)
                        e.activation(YB[:, q, 0:512], PS[:, 4, :], ACT.Copy).then_inc(s("ye", q), 1)
                n = pairs(e)
                for q in range(2):
                    e.wait_ge(s("xg", q), n * 16 + 16)
                    ch.run(e.activation(LAST, ident[:, 0:1], ACT.Copy))
                    e.wait_ge(s("sc", q), n * 16 + 16)
                    ch.run(e.activation(LAST, ident[:, 0:1], ACT.Copy))

            def dve(e, ch):

                def one_hot(q, blk, own):
                    x = e.value_load(EXPERT[0:1, bass.ds(blk, 1)], min_val=0, max_val=NE - 1)
                    e.tensor_tensor(DC[:, t0:NT].rearrange("p (t o) -> p t o", o=1), DEST[:, t0:NT, bass.ds(x, 1)],
                                    cst("blkbase")[:, bass.ds(blk, 1)].rearrange("p (t o) -> p t o", o=1).broadcast_to([P, len(tiles), 1]), ALU.subtract).then_inc(s_own, 1)
                    e.tensor_copy(RC[:, t0:NT].rearrange("p (t o) -> p t o", o=1), RV[:, t0:NT, bass.ds(x, 1)]).then_inc(s_own, 1)
                    e.wait_ge(s_own, own + 2)
                    for t in tiles:
                        mm = e.tensor_scalar(OH[:, t, :], cst("iota"), DC[:, t:t + 1], None, ALU.is_equal)
                    mm.then_inc(s("oh", q), 1)

                def indices(q, own):
                    e.tensor_scalar(IXV[:, q:q + 1], PS[:, 6, 0:1], float(FAR), None, ALU.add).then_inc(s_own, 1)
                    e.wait_ge(s_own, own + 1)
                    e.tensor_scalar(IXG[:, q:q + 1], IXV[:, q:q + 1], FAR | (T - 1), None, ALU.bitwise_and).then_inc(s("ixd", q), 1)

                def second_half(q):
                    return e.tensor_copy(XT[:, q, 4:8, :], PS[:, 1, :].rearrange("p (k n) -> p k n", k=4))
                for q in range(2):
                    e.sem_inc(s("h", q), 1)
                    e.memset(IXS[:, q:q + 1], FAR).then_inc(s_own, 1)
                    e.memset(YB[:, q, :], 0.0).then_inc(s_own, 1)
                for q in range(2):
                    if q:
                        e.wait_ge(s("ixp", 0), 1)
                    one_hot(q, q, 4 + 3 * q)
                    e.wait_ge(s("ixp", q), 1)
                    indices(q, 4 + 3 * q + 2)
                e.wait_ge(s("tr", 0), 1)
                second_half(0).then_inc(s("xtd", 0), 1)
                with e.Fori(0, pairs(e)) as i:
                    for q in range(2):
                        e.wait_ge(s("ixp", 1 - q), i + 1 + q)
                        one_hot(q, i * 2 + 2 + q, i * 8 + 10 + 4 * q)
                        e.wait_ge(s("sg", q), i + 1)
                        e.wait_ge(s("ht", q), i + 1)
                        e.tensor_tensor(HB[:, q, :], SGL[:, q, :], PS[:, 2, FE:2 * FE], ALU.mult).then_inc(s("h", q), 1)
                        e.wait_ge(s("tr", 1 - q), i + 1 + q)
                        e.wait_ge(s("gu", 1 - q), i + 1 + q)
                        second_half(1 - q).then_inc(s("xtd", 1 - q), 1)
                        e.wait_ge(s("sc", q), i * 16 + 16)
                        e.wait_ge(s("xg", q), i * 16 + 16)
                        e.tensor_copy(IXS[:, q:q + 1], IXV[:, q:q + 1]).then_inc(s_own, 1)
                        e.wait_ge(s_own, i * 8 + 13 + 4 * q)
                        e.wait_ge(s("ixp", q), i + 2)
                        indices(q, i * 8 + 13 + 4 * q)
                        e.wait_ge(s("y", q), i + 2)
                        e.tensor_copy(YB[:, q, 512:1024], PS[:, 5, :]).then_inc(s("ye", q), 1)
            return dict(act=act, pe=pe, dve=dve, pool=pool)

        def load_experts(sp, l, done):
            m_ = moe[l]
            sp.wait_ge(s_wfree, done)
            n = sp.value_load(NPAIR[0:1, 0:1], min_val=1, max_val=NBLK // 2)
            with sp.Fori(0, n) as i:
                for q in range(2):
                    x = sp.value_load(EXPERT[0:1, bass.ds(i * 2 + q, 1)], min_val=0, max_val=NE - 1)
                    sp.wait_ge(m_["y"][q], i + 1)
                    for dst, w, k in zip(expert_slot(q), ("w_exp_gate", "w_exp_up", "w_exp_down"), (KT, KT, 2)):
                        sp.dma_start(dst, a[w][l, bass.ds(x, 1)].rearrange("o (p k) n -> p (o k) n", k=k)).then_inc(m_["wl"][q], 16)

        def stage_combine(l, t0):
            nm = f"s_cb_"
            s_ld, s_y, s_dn, s_var, s_std, s_out = (sem(nm + x) for x in ("ld", "y", "dn", "var", "std", "out"))
            s_yr = [sem(f"{nm}yr{i}") for i in range(4)]
            YR = ar(M0, 4, D)
            GM = ar(M0 + 4096, 2, 1, D)
            LNB = ar(M0 + 6144, 2, D)
            tiles = range(t0, NT)
            nt = len(tiles)
            items = [(t, k) for t in tiles for k in range(TOPK)]

            def act(e, ch):
                modulation(e, l, (5,), GM, s_ld, range(t0 // 2, 2))
                for i, nm_ in enumerate(("ln2_g", "ln2_b")):
                    e.dma_start(LNB[:, i, :], a[nm_][l:l + 1, :].broadcast_to([P, D])).then_inc(s_ld, 16)
                for i, (t, k) in enumerate(items):
                    if i >= 4:
                        e.wait_ge(s_dn, i - 3)
                    e.dma_start(YR[:, i % 4, :], y_d[k * T + t * P:k * T + (t + 1) * P, :]).then_inc(s_yr[i % 4], 16)
                roots(e, nt, s_var, s_std)
                if l == depth - 1:
                    e.wait_ge(s_y, 1)
                    e.dma_start(out[0].rearrange("(t p) d -> p t d", p=P), X[:, 2:4, :]).then_inc(s_out, 16)
                    e.wait_ge(s_out, 16)

            def dve(e, ch):
                for i, (t, k) in enumerate(items):
                    e.wait_ge(s_yr[i % 4], 16 * (i // 4 + 1))
                    if i:
                        e.wait_ge(s_dn, i)
                    e.scalar_tensor_tensor(out=FS[:, t, :], in0=YR[:, i % 4, :], scalar=WK[:, k, t:t + 1], in1=FS[:, t, :], op0=ALU.mult, op1=ALU.add).then_inc(s_dn, 1)
                e.wait_ge(s_dn, len(items))
                e.wait_ge(s_ld, 64 if t0 == 0 else 48)
                for t in tiles:
                    ch.add(e.tensor_tensor(FS[:, t, :], FS[:, t, :], GM[:, t // 2, 0, :], ALU.mult))
                ch.sync()
                for t in tiles:
                    ch.add(e.scalar_tensor_tensor(out=X[:, t, :], in0=X[:, t, :], scalar=ALPHA, in1=FS[:, t, :], op0=ALU.mult, op1=ALU.add))
                ch.sync()
                for i, t in enumerate(tiles):
                    layer_norm(e, ch, t, i, LNB, s_var, s_std)
                e.sem_inc(s_y, 1)
            return dict(act=act, dve=dve)

        def phase(*made):
            taken.clear()
            phases.append([(name, f(*args)) for name, f, *args in made])

        for l in range(depth):
            t0 = 0 if l < DEPTH - 1 else 2
            if l == 0:
                phase(("mod", stage_mod))
            phase((f"u{l}", stage_u, l, False, 0), (f"z{l}", stage_z, l, t0),
                  (f"mla{l}", stage_mla, l, t0), (f"matt{l}", stage_attend, l, False, t0),
                  (f"gqa{l}", stage_gqa, l, t0), (f"gatt{l}", stage_attend, l, True, t0))
            phase((f"dnp{l}", stage_dn_prep, l, t0), (f"dns{l}", stage_dn_scan, l, t0), (f"dno{l}", stage_dn_out, l, t0))
            phase((f"mrg{l}", stage_merge, l, t0), (f"uf{l}", stage_u, l, True, t0), (f"rt{l}", stage_route, l, t0))
            phase((f"ex{l}", stage_experts, l, t0), (f"cb{l}", stage_combine, l, t0))
        stage_of_experts = {f"ex{l}": l for l in range(depth)}
        last_of = {l: n for n, l in moe_after.items()}
        uses = {"mod": 12 * depth, "z": len(ZCH), "mla": 1, "dnp": 3, "mrg": 11, "rt": 3}
        sent = ended = 0
        met = {}

        def barrier(e, who):
            met[who] = met.get(who, 0) + 1
            e.drain().then_inc(s_bar, 1)
            e.wait_ge(s_bar, 5 * met[who])

        def send(sp, upto):
            nonlocal sent
            for n in range(sent, upto):
                if n >= 3:
                    sp.wait_ge(s_wfree, n - 2)
                for off, src, k, w in plan[n]:
                    dst = RING[:, n % 3, off:off + k * w].rearrange("p (k n) -> p k n", k=k)
                    sp.dma_start(dst, src).then_inc(s_slot[n % 3], 16)
            sent = max(sent, upto)

        chains = {"act": Chain(nc.scalar, s_act), "dve": Chain(nc.vector, s_dve), "pool": Chain(nc.gpsimd, s_pool)}

        def run_phase(e, which, n):
            if n == 0:
                barrier(e, which)
            for name, st in phases[n]:
                if which in st:
                    st[which](e, chains[which]) if which in chains else st[which](e)
                barrier(e, which)

        def run_sync(sp, n):
            nonlocal ended
            if n == 0:
                for i in range(4):
                    sp.dma_start(X[:, i, :], (a["ctx"][0], a["x"][0])[i // 2][(i % 2) * P:(i % 2 + 1) * P, :]).then_inc(s_const, 16)
                sp.dma_start(CB[:, :], a["const"]).then_inc(s_const, 16)
                sp.wait_ge(s_const, 80)
                barrier(sp, "sp")
            for name, st in phases[n]:
                if name in stage_of_experts:
                    load_experts(sp, stage_of_experts[name], last_of[stage_of_experts[name]])
                else:
                    ended += uses.get(name if name == "mod" else name[:-1], 0)
                    send(sp, min([ended + 3, len(plan)] + [b for b in moe_after if b >= ended and (b > ended or name[:-1] != "cb")]))
                barrier(sp, "sp")
        for n in range(len(phases)):
            if n:
                nc.all_engine_barrier(sems_to_clear=range(shared[0].num, shared[-1].num + 1))
            with nc.Block() as block:
                @block.sync
                def _(sp):
                    run_sync(sp, n)

                @block.gpsimd
                def _(pool):
                    run_phase(pool, "pool", n)

                @block.scalar
                def _(act):
                    run_phase(act, "act", n)

                @block.tensor
                def _(pe):
                    run_phase(pe, "pe", n)

                @block.vector
                def _(dve):
                    run_phase(dve, "dve", n)


_INS = ["x", "c", "ctx", "c_ctx", "w_ada", "b_ada", "w_in", "mla_q_norm", "mla_kv_norm", "w_uq", "w_ukv",
        "dn_conv", "dn_a_log", "dn_dt_bias", "dn_norm", "gqa_sink", "w_o_mla", "w_o_dn", "w_o_gqa", "w_out",
        "ln1_g", "ln1_b", "w_router", "router_bias", "w_exp_gate", "w_exp_up", "w_exp_down",
        "w_sh_gate", "w_sh_up", "w_sh_down", "ln2_g", "ln2_b"]


def kernel(**inputs):
    import numpy as _np
    import concourse.bacc as _bacc
    from concourse import mybir as _mybir
    from concourse.bass_utils import run_bass_kernel_spmd as _run

    nc = _bacc.Bacc("TRN2", target_bir_lowering=False, num_devices=1)
    arrays, aps = {}, {}
    for name in _INS:
        v = _np.ascontiguousarray(inputs[name])
        arrays[f"in_{name}"] = v
        aps[name] = nc.dram_tensor(f"in_{name}", v.shape, _mybir.dt.from_np(v.dtype), kind="ExternalInput").ap()
    arrays["in_const"] = CONST
    aps["const"] = nc.dram_tensor("in_const", CONST.shape, F32, kind="ExternalInput").ap()
    out = nc.dram_tensor("out_0", (1, SEG, D), F32, kind="ExternalOutput").ap()
    trunk(nc, aps, out)
    r = _run(nc, [arrays], core_ids=[0])
    return r.results[0]["out_0"]
```

```python
from contextlib import ExitStack

import numpy as np

import concourse.bass as bass
from concourse import mybir

F32 = mybir.dt.float32
I32 = mybir.dt.int32
ALU = mybir.AluOpType
ACT = mybir.ActivationFunctionType
AX = mybir.AxisListType

P = 128
D = 1024
KT = D // P
DEPTH = 2
SEG = 256
T = 2 * SEG
NT = T // P
EPS = 1e-6
ALPHA = (2.0 * DEPTH) ** 0.25
GRID_W = 64

Q_LORA, KV_LORA = 256, 128
H = 8
NOPE, ROPE, HD = 64, 32, 64
QK = NOPE + ROPE
MLA_SCALE = QK ** -0.5
GQA_SCALE = HD ** -0.5
KV_HEADS = 2
WINDOW = 128
CONV = 5
CH = 64
DW = H * HD

NE, TOPK, NG, TOPG = 64, 8, 8, 4
FE = 256
ROUTED_SCALE = 2.5
NBLK = T * TOPK // P + NE
FAR = 1 << 14
MASKED = -1e30

C_DQKV, C_AB, C_GATES = 416, 1952, 3264
ZCH = [(0, 0, 416), (1952, 416, 512), (2464, 928, 512), (2976, 1440, 288)]
ZW = 1728
Z_CQ, Z_CKV, Z_KR, Z_A, Z_B, Z_DZ, Z_GQ, Z_GK, Z_GV = 0, 256, 384, 416, 432, 448, 960, 1472, 1600

LEVELS = 6


def constants():
    i = np.arange(P)
    same = (i[:, None] // CH) == (i[None, :] // CH)
    parts = {}
    parts["ident"] = np.eye(P)
    parts["tri0"] = same & (i[:, None] <= i[None, :])
    parts["tri1"] = same & (i[:, None] >= i[None, :])
    parts["blk"] = same
    parts["sel0"] = np.repeat((i < CH)[:, None], P, 1)
    parts["sel1"] = np.repeat((i >= CH)[:, None], P, 1)
    for d in range(2):
        for s in range(LEVELS):
            b = 1 << s
            a, c = (i[:, None], i[None, :]) if d == 0 else (i[None, :], i[:, None])
            parts[f"lvl{d}{s}"] = (a // (2 * b) == c // (2 * b)) & (a // b % 2 == 1) & (c // b % 2 == 0)
    for t in range(2):
        q = t * P + i[:, None]
        k = np.arange(SEG)[None, :]
        ok = np.abs(q - k) <= WINDOW
        parts[f"win{t}"] = np.concatenate([np.zeros((P, SEG)), np.where(ok, 0.0, MASKED)], 1)
    for name, dim in (("m", ROPE), ("g", HD)):
        n = dim // 4
        inv = np.float32(10000.0) ** (-np.arange(n, dtype=np.float32) / np.float32(n))
        t = np.arange(SEG)
        ang = np.concatenate([(t // GRID_W).astype(np.float32)[:, None] * inv,
                              (t % GRID_W).astype(np.float32)[:, None] * inv], 1)
        for f, nm in ((np.cos, "cos"), (np.sin, "sin")):
            tab = f(ang.astype(np.float32)).reshape(2, P, 2 * n).transpose(1, 0, 2)
            parts[nm + name] = tab.reshape(P, 4 * n)
    parts["before"] = i[:, None] < i[None, :]
    parts["ones"] = np.ones((P, P))
    g = np.arange(NG)
    parts["glow"] = np.tile((g[None, :] < g[:, None]).reshape(1, -1), (P, 1))
    parts["rowid"] = i[:, None]
    parts["iota"] = np.tile(i[None, :], (P, 1))
    parts["blkbase"] = np.tile(P * i[None, :], (P, 1))
    parts["tokid"] = i[:, None] + P * np.arange(NT)[None, :]
    at, cols = {}, 0
    for n, v in parts.items():
        at[n] = (cols, v.shape[1])
        cols += v.shape[1]
    return np.concatenate([np.asarray(v, np.float32) for v in parts.values()], 1), at


CONST, CAT = constants()
NCONST = CONST.shape[1]


class Chain:

    def __init__(self, eng, sem):
        self.eng, self.sem, self.n = eng, sem, 0

    def add(self, ins):
        ins.then_inc(self.sem, 1)
        self.n += 1

    def sync(self):
        self.eng.wait_ge(self.sem, self.n)

    def run(self, ins):
        self.add(ins)
        self.sync()


def trunk(nc, a, out, depth=DEPTH):
    with ExitStack() as ctx:
        def sb(name, shape, dt=F32):
            return ctx.enter_context(nc.sbuf_tensor(name, shape, dt))

        shared = [ctx.enter_context(nc.semaphore(f"s_stage{i}")) for i in range(72)]
        taken = {}

        def sem(name):
            if name not in taken:
                taken[name] = shared[len(taken)]
            return taken[name]

        def own_sem(name):
            return ctx.enter_context(nc.semaphore(name))

        X = sb("X", [P, NT, D])
        UT = sb("UT", [P, KT, T])
        CB = sb("CB", [P, NCONST])
        RING = sb("RING", [P, 3, 8 * 512])
        AR = sb("AR", [P, 27392])
        SM = sb("SM", [P, 1040])
        EXPERT = sb("EXPERT", [1, P], I32)
        NPAIR = sb("NPAIR", [1, 1], I32)
        IXG = sb("IXG", [P, 2], I32)
        IXV = sb("IXV", [P, 2], I32)
        IXS = sb("IXS", [P, 2], I32)
        BEI = sb("BEI", [P, 1], I32)
        PS = ctx.enter_context(nc.psum_tensor("PS", [P, 8, 512], F32))

        mod_d = nc.dram_tensor("mod_d", [DEPTH, 2, 6 * D], F32).ap()
        u_d = nc.dram_tensor("u_d", [T, D], F32).ap()
        y_d = nc.dram_tensor("y_d", [TOPK * T, D], F32).ap()
        blk_d = nc.dram_tensor("blk_d", [P, 1], I32).ap()

        def cst(name):
            o, n = CAT[name]
            return CB[:, o:o + n]

        ident = cst("ident")

        def ar(off, *dims):
            n = int(np.prod(dims))
            v = AR[:, off:off + n]
            if len(dims) == 1:
                return v
            names = "abcde"[:len(dims)]
            return v.rearrange(f"p ({' '.join(names)}) -> p {' '.join(names)}", **{c: k for c, k in zip(names[1:], dims[1:])})

        def sm(off, *dims):
            n = int(np.prod(dims))
            v = SM[:, off:off + n]
            if len(dims) == 1:
                return v
            names = "abcde"[:len(dims)]
            return v.rearrange(f"p ({' '.join(names)}) -> p {' '.join(names)}", **{c: k for c, k in zip(names[1:], dims[1:])})

        s_bar = own_sem("s_bar")
        s_act = own_sem("s_act_chain")
        s_dve = own_sem("s_dve_chain")
        s_pool = own_sem("s_pool_chain")
        s_const = own_sem("s_const")
        s_slot = [own_sem(f"s_slot{i}") for i in range(3)]
        s_wfree = own_sem("s_wfree")

        plan, where = [], {}

        def use(key, moves):
            where[key] = len(plan)
            plan.append(moves)

        def by_k(w, n):
            return (w.rearrange("(k p) n -> p k n", p=P), w.shape[0] // P, n)

        moe_after = {}
        for l in range(depth):
            for n in range(12):
                use(("ada", l, n), [(0, *by_k(a["w_ada"][l, :, n * 512:(n + 1) * 512], 512))])
            for c, (src, _, n) in enumerate(ZCH):
                use(("z", l, c), [(0, *by_k(a["w_in"][l, :, src:src + n], n))])
            use(("uqkv", l), [(0, *by_k(a["w_uq"][l], 768)), (1536, *by_k(a["w_ukv"][l], 1024))])
            for c in range(3):
                use(("dqkv", l, c), [(0, *by_k(a["w_in"][l, :, C_DQKV + 512 * c:C_DQKV + 512 * (c + 1)], 512))])
            for b, nm in enumerate(("w_o_mla", "w_o_dn", "w_o_gqa")):
                for c in range(2):
                    g0 = C_GATES + b * D + c * 512
                    use(("gate", l, b, c), [(0, *by_k(a["w_in"][l, :, g0:g0 + 512], 512))])
                use(("o", l, b), [(0, *by_k(a[nm][l], D))])
            for c in range(2):
                use(("out", l, c), [(0, *by_k(a["w_out"][l, :, c * 512:(c + 1) * 512], 512))])
            use(("router", l), [(0, *by_k(a["w_router"][l], NE))])
            use(("shgu", l), [(0, *by_k(a["w_sh_gate"][l], FE)), (KT * FE, *by_k(a["w_sh_up"][l], FE))])
            use(("shd", l), [(0, *by_k(a["w_sh_down"][l], D))])
            moe_after[len(plan)] = l
        ready = []
        count = [0, 0, 0]
        for n, moves in enumerate(plan):
            count[n % 3] += 16 * len(moves)
            ready.append(count[n % 3])

        def slot(key, off=0, *dims):
            base = RING[:, where[key] % 3, off:off + int(np.prod(dims))]
            return base.rearrange("p (k n) -> p k n", k=dims[0])

        def landed(pe, key):
            n = where[key]
            pe.wait_ge(s_slot[n % 3], ready[n])

        phases = []
        MOE = ("wl", "oh", "ixp", "ixd", "tr", "xta", "xtd", "gu", "sg", "h", "ht", "hte", "y", "ye")
        moe_dma = [{k: [own_sem(f"s_moe{l}_{k}{q}") for q in range(2)] for k in ("xg", "sc")} for l in range(depth)]
        moe = {}

        def mod_parts(l):
            s_c, s_cs, s_ps, s_ev, s_st = (sem(f"s_mod_{x}") for x in ("c", "cs", "ps", "ev", "st"))
            cv = sm(64, KT, 2)
            cs = sm(80, KT, 2)
            row = AR[0:2, 16896:16896 + 6 * D]

            def begin(e):
                e.dma_start(cv[:, :, 0], a["c_ctx"].rearrange("(k p) -> p k", p=P), allow_slow_non_contiguous=True).then_inc(s_c, 16)
                e.dma_start(cv[:, :, 1], a["c"][0].rearrange("(k p) -> p k", p=P), allow_slow_non_contiguous=True).then_inc(s_c, 16)
                for i in range(2):
                    e.dma_start(row[i:i + 1], a["b_ada"][l:l + 1]).then_inc(s_st, 16)
                e.wait_ge(s_c, 32)
                e.activation(cs, cv, ACT.Silu).then_inc(s_cs, 1)

            def end(e):
                e.wait_ge(s_ev, 12)
                for i in range(2):
                    e.dma_start(mod_d[l, i:i + 1, :], row[i:i + 1]).then_inc(s_st, 16)
                e.wait_ge(s_st, 64)

            def pe(e):
                e.wait_ge(s_cs, 1)
                for i in range(12):
                    key = ("ada", l, i)
                    landed(e, key)
                    w = slot(key, 0, KT, 512)
                    if i >= 8:
                        e.wait_ge(s_ev, i - 7)
                    for k in range(KT):
                        m = e.matmul(PS[0:2, i % 8, :], cs[:, k, :], w[:, k, :], start=k == 0, stop=k == KT - 1)
                    m.then_inc(s_ps, 1)
                    e.wait_ge(s_ps, i + 1)
                    e.sem_inc(s_wfree, 1)

            def add_bias(e, i):
                if i == 0:
                    e.wait_ge(s_st, 32)
                e.wait_ge(s_ps, i + 1)
                r = row[:, i * 512:(i + 1) * 512]
                e.tensor_tensor(r, PS[0:2, i % 8, :], r, ALU.add).then_inc(s_ev, 1)
            return begin, end, pe, add_bias

        def stage_mod():
            begin, end, pe, add_bias = mod_parts(0)

            def act(e, ch):
                begin(e)
                end(e)

            def dve(e, ch):
                for i in range(12):
                    add_bias(e, i)
            return dict(act=act, pe=pe, dve=dve)

        def modulation(e, l, which, dst, s, segs):
            n = 0
            for i, w in enumerate(which):
                for g in segs:
                    e.dma_start(dst[:, g, i, :], mod_d[l, g:g + 1, w * D:(w + 1) * D].broadcast_to([P, D])).then_inc(s, 16)
                    n += 16
            return n

        B0 = ZW * NT + 3 * 2048
        s_ahead = own_sem("s_ahead")

        def stage_u(l, ffn, t0):
            nm = f"s_u{int(ffn)}_"
            s_m, s_u, s_tp, s_te, s_ud0, s_ud1, s_t1 = (sem(nm + x) for x in ("m", "u", "tp", "te", "ud0", "ud1", "t1"))
            s_ud = (s_ud0, s_ud1)
            mb, u, tmp = (ar(ZW * NT, 2, 2, D), ar(4096, 2, D), ar(ZW * NT + 4096, 2, D)) if ffn else (ar(B0 + 10240, 2, 2, D), ar(B0, 2, D), ar(B0 + 2048, 2, D))
            tiles = list(range(t0, NT))
            segs = range(t0 // 2, 2)

            def act(e, ch):
                if l == 0 and not ffn:
                    modulation(e, l, (0, 1), mb, s_m, segs)
                for i, t in enumerate(tiles):
                    if ffn:
                        e.wait_ge(s_u, i + 1)
                        e.dma_start(u_d[t * P:(t + 1) * P, :], u[:, i % 2, :]).then_inc(s_ud[i % 2], 16)
                    for g in range(2):
                        e.wait_ge(s_tp, 2 * i + g + 1)
                        e.activation(UT[:, 4 * g:4 * g + 4, t * P:(t + 1) * P],
                                     PS[:, (2 * i + g) % 4, :].rearrange("p (k q) -> p k q", k=4), ACT.Copy).then_inc(s_te, 1)
                if ffn:
                    for q in range(2):
                        e.wait_ge(s_ud[q], 8 * len(tiles))

            def pe(e):
                for i, t in enumerate(tiles):
                    e.wait_ge(s_u, i + 1)
                    for g in range(2):
                        n = 2 * i + g
                        if n >= 4:
                            e.wait_ge(s_te, n - 3)
                        for k in range(4):
                            m = e.transpose(PS[:, n % 4, k * P:(k + 1) * P], u[:, i % 2, (4 * g + k) * P:(4 * g + k + 1) * P], ident)
                        m.then_inc(s_tp, 1)

            def dve(e, ch):
                if l and not ffn:
                    e.wait_ge(s_ahead, 64)
                else:
                    e.wait_ge(s_m, 64 if t0 == 0 else 32)
                for i, t in enumerate(tiles):
                    e.scalar_tensor_tensor(out=tmp[:, i % 2, :], in0=mb[:, t // 2, 1, :], scalar=1.0, in1=X[:, t, :],
                                           op0=ALU.add, op1=ALU.mult).then_inc(s_t1, 1)
                    e.wait_ge(s_t1, i + 1)
                    if i >= 2:
                        e.wait_ge(s_tp, 2 * (i - 1))
                        if ffn:
                            e.wait_ge(s_ud[i % 2], 16 * (i // 2))
                    e.tensor_tensor(u[:, i % 2, :], tmp[:, i % 2, :], mb[:, t // 2, 0, :], ALU.add).then_inc(s_u, 1)
            return dict(act=act, pe=pe, dve=dve)

        ZA = ar(0, NT, ZW)

        def stage_z(l, t0):
            s_ps, s_ea, s_ed = (sem(f"s_z_{x}") for x in ("ps", "ea", "ed"))
            s_ute = sem("s_u0_te")
            items = []
            for c, (_, dst, n) in enumerate(ZCH):
                for t in range(NT):
                    width = n if t >= t0 or c in (0, 3) else (32 if c == 1 else 0)
                    if width:
                        items.append((c, t, dst, width))

            def evac(e, parity, s, fn):
                for i, (c, t, dst, n) in enumerate(items):
                    if i % 2 == parity:
                        e.wait_ge(s_ps, i + 1)
                        fn(ZA[:, t, dst:dst + n], PS[:, 4 + i % 4, 0:n]).then_inc(s, 1)

            def act(e, ch):
                evac(e, 0, s_ea, lambda o, i: e.activation(o, i, ACT.Copy))

            def dve(e, ch):
                evac(e, 1, s_ed, lambda o, i: e.tensor_copy(o, i))

            def pe(e):
                for i, (c, t, dst, n) in enumerate(items):
                    landed(e, ("z", l, c))
                    w = slot(("z", l, c), 0, KT, ZCH[c][2])
                    if i >= 4:
                        e.wait_ge(s_ea if i % 2 == 0 else s_ed, (i - 4) // 2 + 1)
                    if c == 0:
                        e.wait_ge(s_ute, 2 * (t + 1))
                    for k in range(KT):
                        m = e.matmul(PS[:, 4 + i % 4, 0:n], UT[:, k, t * P:(t + 1) * P], w[:, k, 0:n], start=k == 0, stop=k == KT - 1)
                    m.then_inc(s_ps, 1)
                    if i + 1 == len(items) or items[i + 1][0] != c:
                        e.wait_ge(s_ps, i + 1)
                        e.sem_inc(s_wfree, 1)
            return dict(act=act, pe=pe, dve=dve)

        def rope(e, ch, x1, x2, cos, sin, tmp):
            ch.add(e.tensor_tensor(tmp[0], x1, cos, ALU.mult))
            ch.add(e.tensor_tensor(tmp[1], x2, sin, ALU.mult))
            ch.add(e.tensor_tensor(tmp[2], x2, cos, ALU.mult))
            ch.add(e.tensor_tensor(tmp[3], x1, sin, ALU.mult))
            ch.sync()
            ch.add(e.tensor_tensor(x1, tmp[0], tmp[1], ALU.subtract))
            ch.add(e.tensor_tensor(x2, tmp[2], tmp[3], ALU.add))
            ch.sync()

        OT = [ar(ZW * NT, 4, T), ar(ZW * NT + 2048, 4, T), ar(ZW * NT + 4096, 4, T)]
        O_MLA, O_GQA, _ = OT
        DZ = ar(ZW * NT + 4096, NT, DW)

        qT = ar(B0, H, T)
        kTm = ar(B0 + 4096, H, T)
        V = ar(B0 + 8192, NT, DW)
        PB = ar(B0 + 10240, 3, 512)
        C0 = B0 + 11776

        def stage_mla(l, t0):
            s_g, s_ms, s_rt, s_cn, s_tp, s_te, s_pj, s_pe_, s_rq, s_kk, s_hp, s_he = (
                sem(f"s_ml_{x}") for x in ("g", "ms", "rt", "cn", "tp", "te", "pj", "ev", "rq", "kk", "hp", "he"))
            gain = sm(0, 384)
            ss, rt = sm(384, 8), sm(392, 8)
            cT = ar(C0, 3, T)
            tile = ar(B0 + 10240, 2, 768)
            tmp = [ar(C0 + 1536 + 128 * i, H, 16) for i in range(4)]
            cosm = cst("cosm").rearrange("p (t n) -> p t n", t=2)
            sinm = cst("sinm").rearrange("p (t n) -> p t n", t=2)
            sqd = ar(B0 + 10240, 256)
            jobs = [("kv", t) for t in range(NT)] + [("q", t) for t in range(t0, NT)]

            def act(e, ch):
                e.dma_start(gain[:, 0:256], a["mla_q_norm"][l:l + 1, :].broadcast_to([P, 256])).then_inc(s_g, 16)
                e.dma_start(gain[:, 256:384], a["mla_kv_norm"][l:l + 1, :].broadcast_to([P, 128])).then_inc(s_g, 16)
                e.wait_ge(s_ms, 1)
                e.activation(rt, ss, ACT.Sqrt).then_inc(s_rt, 1)
                for t in range(NT):
                    e.wait_ge(s_tp, t + 1)
                    lo = 0 if t >= t0 else 2
                    e.activation(cT[:, lo:3, t * P:(t + 1) * P],
                                 PS[:, t % 2, lo * P:384].rearrange("p (k q) -> p k q", q=P), ACT.Copy).then_inc(s_te, 1)
                for i, (kind, t) in enumerate(jobs):
                    o = tile[:, i % 2, :].rearrange("p (h n) -> p h n", h=H)
                    if i >= 2:
                        e.wait_ge(s_hp, 2 * (i - 1))
                    for g in range(2):
                        e.wait_ge(s_pj, 2 * i + g + 1)
                        b = PS[:, 2 + g, :]
                        if kind == "q":
                            e.activation(o[:, 4 * g:4 * g + 4, :], b[:, 0:384].rearrange("p (h n) -> p h n", h=4), ACT.Copy).then_inc(s_pe_, 1)
                        else:
                            kv = b.rearrange("p (h n) -> p h n", h=4)
                            e.activation(o[:, 4 * g:4 * g + 4, 0:NOPE], kv[:, :, 0:NOPE], ACT.Copy)
                            e.activation(V[:, t, 256 * g:256 * (g + 1)].rearrange("p (h n) -> p h n", h=4), kv[:, :, NOPE:], ACT.Copy).then_inc(s_pe_, 1)
                    for g in range(2):
                        e.wait_ge(s_hp, 2 * i + g + 1)
                        dst = qT if kind == "q" else kTm
                        e.activation(dst[0:QK, 4 * g:4 * g + 4, t * P:(t + 1) * P],
                                     PS[0:QK, 4 + g, :].rearrange("p (h q) -> p h q", h=4), ACT.Copy).then_inc(s_he, 1)

            def dve(e, ch):
                cq = [ZA[:, t, Z_CQ:Z_CQ + 256] for t in range(NT)]
                ckv = [ZA[:, t, Z_CKV:Z_CKV + 128] for t in range(NT)]
                ch.run(e.memset(ss, 1.0))
                for t in range(NT):
                    if t >= t0:
                        ch.run(e.tensor_tensor_reduce(sqd, cq[t], cq[t], 1.0 / 256, EPS, ALU.mult, ALU.add, ss[:, t:t + 1]))
                    ch.run(e.tensor_tensor_reduce(sqd[:, 0:128], ckv[t], ckv[t], 1.0 / 128, EPS, ALU.mult, ALU.add, ss[:, 4 + t:5 + t]))
                e.sem_inc(s_ms, 1)
                e.wait_ge(s_rt, 1)
                ch.run(e.reciprocal(ss, rt))
                e.wait_ge(s_g, 32)
                for t in range(NT):
                    if t >= t0:
                        ch.add(e.scalar_tensor_tensor(out=cq[t], in0=cq[t], scalar=ss[:, t:t + 1], in1=gain[:, 0:256], op0=ALU.mult, op1=ALU.mult))
                    e.scalar_tensor_tensor(out=ckv[t], in0=ckv[t], scalar=ss[:, 4 + t:5 + t], in1=gain[:, 256:384],
                                           op0=ALU.mult, op1=ALU.mult).then_inc(s_cn, 1)
                kr = ZA[:, 2:4, Z_KR:Z_KR + ROPE]
                rope(e, ch, kr[:, :, 0:16], kr[:, :, 16:32], cosm, sinm, [x[:, 0:2, :] for x in tmp])
                for i, (kind, t) in enumerate(jobs):
                    o = tile[:, i % 2, :].rearrange("p (h n) -> p h n", h=H)
                    e.wait_ge(s_pe_, 2 * i + 2)
                    if kind == "q":
                        if t >= 2:
                            cb = cosm[:, t - 2:t - 1, :].broadcast_to([P, H, 16])
                            sn = sinm[:, t - 2:t - 1, :].broadcast_to([P, H, 16])
                            rope(e, ch, o[:, :, NOPE:NOPE + 16], o[:, :, NOPE + 16:QK], cb, sn, tmp)
                    else:
                        ch.run(e.tensor_copy(o[:, :, NOPE:QK], ZA[:, t:t + 1, Z_KR:Z_KR + ROPE].broadcast_to([P, H, ROPE])))
                    e.sem_inc(s_rq, 1)

            def pe(e):
                for t in range(NT):
                    e.wait_ge(s_cn, t + 1)
                    if t >= 2:
                        e.wait_ge(s_te, t - 1)
                    for k in range(3):
                        if k == 2 or t >= t0:
                            src = Z_CQ + k * P
                            m = e.transpose(PS[:, t % 2, k * P:(k + 1) * P], ZA[:, t, src:src + P], ident)
                    m.then_inc(s_tp, 1)
                e.wait_ge(s_te, NT)
                landed(e, ("uqkv", l))
                wq = slot(("uqkv", l), 0, 2, 768)
                wkv = slot(("uqkv", l), 1536, 1, D)
                for i in range(len(jobs) + 1):
                    if i < len(jobs):
                        kind, t = jobs[i]
                        for g in range(2):
                            if i >= 1:
                                e.wait_ge(s_pe_, 2 * (i - 1) + g + 1)
                            if kind == "q":
                                for k in range(2):
                                    m = e.matmul(PS[:, 2 + g, 0:384], cT[:, k, t * P:(t + 1) * P], wq[:, k, g * 384:(g + 1) * 384], start=k == 0, stop=k == 1)
                            else:
                                m = e.matmul(PS[:, 2 + g, :], cT[:, 2, t * P:(t + 1) * P], wkv[:, 0, g * 512:(g + 1) * 512], start=True, stop=True)
                            m.then_inc(s_pj, 1)
                    if i >= 1:
                        j = i - 1
                        o = tile[:, j % 2, :].rearrange("p (h n) -> p h n", h=H)
                        e.wait_ge(s_rq, j + 1)
                        for g in range(2):
                            if j >= 1:
                                e.wait_ge(s_he, 2 * (j - 1) + g + 1)
                            for h in range(4):
                                m = e.transpose(PS[0:QK, 4 + g, h * P:(h + 1) * P], o[:, 4 * g + h, :], ident)
                            m.then_inc(s_hp, 1)
                e.wait_ge(s_hp, 2 * len(jobs))
                e.sem_inc(s_wfree, 1)
            return dict(act=act, pe=pe, dve=dve)

        kT2 = ar(B0 + 4096, KV_HEADS, T)

        def stage_gqa(l, t0):
            s_k, s_sk, s_tp, s_te = (sem(f"s_gq_{x}") for x in ("k", "sk", "tp", "te"))
            kd = ar(B0 + 8192, NT, KV_HEADS, 2, HD)
            tmp = [ar(B0 + 9216 + 640 * i, 2, 10, 32) for i in range(4)]
            cosg = cst("cosg").rearrange("p (t n) -> p t n", t=2)
            sing = cst("sing").rearrange("p (t n) -> p t n", t=2)
            groups = [("k", t, 0) for t in range(NT)] + [("q", t, 0) for t in range(t0, NT)]

            def act(e, ch):
                e.dma_start(sm(0, H), a["gqa_sink"][l:l + 1, :].broadcast_to([P, H])).then_inc(s_sk, 16)
                for i, (kind, t, _) in enumerate(groups):
                    e.wait_ge(s_tp, i + 1)
                    if kind == "k":
                        e.activation(kT2[:, :, t * P:(t + 1) * P], PS[:, i % 4, 0:256].rearrange("p (g q) -> p g q", g=2), ACT.Copy).then_inc(s_te, 1)
                    else:
                        e.activation(qT[:, 0:4, t * P:(t + 1) * P], PS[:, i % 4, :].rearrange("p (g q) -> p g q", g=4), ACT.Copy).then_inc(s_te, 1)
                e.wait_ge(s_sk, 16)

            def dve(e, ch):
                for t in range(2):
                    qk = ZA[:, 2 + t, Z_GQ:Z_GV].rearrange("p (h n) -> p h n", n=HD)
                    cb = cosg[:, t:t + 1, :].broadcast_to([P, 10, 32])
                    sn = sing[:, t:t + 1, :].broadcast_to([P, 10, 32])
                    rope(e, ch, qk[:, :, 0:32], qk[:, :, 32:64], cb, sn, [x[:, t] for x in tmp])
                for g in range(KV_HEADS):
                    for r in range(2):
                        ch.add(e.tensor_copy(kd[:, :, g, r, :], ZA[:, :, Z_GK + g * HD:Z_GK + (g + 1) * HD]))
                ch.sync()
                e.sem_inc(s_k, 1)

            def pe(e):
                e.wait_ge(s_k, 1)
                for i, (kind, t, _) in enumerate(groups):
                    if i >= 4:
                        e.wait_ge(s_te, i - 3)
                    for j in range(2 if kind == "k" else 4):
                        src = kd[:, t, j].rearrange("p r n -> p (r n)") if kind == "k" else ZA[:, t, Z_GQ + j * P:Z_GQ + (j + 1) * P]
                        m = e.transpose(PS[:, i % 4, j * P:(j + 1) * P], src, ident)
                    m.then_inc(s_tp, 1)
            return dict(act=act, pe=pe, dve=dve)

        def stage_attend(l, gqa, t0):
            nm = f"s_at{int(gqa)}_"
            s_sc, s_mk, s_mx, s_ex, s_p, s_t, s_pt, s_pv, s_o, s_es = (sem(nm + x) for x in ("sc", "mk", "mx", "ex", "p", "t", "pt", "pv", "o", "es"))
            items = [(h, t) for h in range(H) for t in range(t0, NT)]
            n = len(items)
            scale = GQA_SCALE if gqa else MLA_SCALE
            dst = O_GQA if gqa else O_MLA
            sink = sm(0, H)
            mx, nm_, rs, es, rr = sm(16, 4), sm(20, 4), sm(24, 4), sm(28, 4), sm(32, 4)
            SB = ar(C0, 3, 512)
            PT = ar(C0 + 1536, 2, 4, P)

            def keys(t):
                return SEG if t < 2 else T

            def pe(e):
                for s in range(n + 3):
                    if s < n:
                        h, t = items[s]
                        if s >= 3:
                            e.wait_ge(s_mk if gqa else s_ex, s - 2)
                        if gqa:
                            r, q, k = slice(64 * (h % 2), 64 * (h % 2) + 64), qT[:, h // 2, :], kT2[:, h // 4, :]
                        else:
                            r, q, k = slice(0, QK), qT[:, h, :], kTm[:, h, :]
                        e.matmul(PS[:, s % 3, 0:keys(t)], q[r, t * P:(t + 1) * P], k[r, 0:keys(t)], start=True, stop=True).then_inc(s_sc, 1)
                    i = s - 2
                    if 0 <= i < n:
                        h, t = items[i]
                        e.wait_ge(s_p, i + 1)
                        if i >= 2:
                            e.wait_ge(s_pt, i - 1)
                        for k in range(keys(t) // P):
                            m = e.transpose(PS[:, 3 + i % 2, k * P:(k + 1) * P], PB[:, i % 3, k * P:(k + 1) * P], ident)
                        m.then_inc(s_t, 1)
                    i = s - 3
                    if 0 <= i < n:
                        h, t = items[i]
                        e.wait_ge(s_pt, i + 1)
                        if i >= 2:
                            e.wait_ge(s_o, i - 1)
                        r = slice(64 * (h % 2), 64 * (h % 2) + 64)
                        nk = keys(t) // P
                        for k in range(nk):
                            if gqa:
                                v = ZA[:, k, Z_GV + (h // 4) * HD:Z_GV + (h // 4 + 1) * HD]
                            else:
                                v = V[:, k, h * HD:(h + 1) * HD]
                            m = e.matmul(PS[r, 5 + i % 2, 0:P], v, PT[:, i % 2, k, :], start=k == 0, stop=k == nk - 1)
                        m.then_inc(s_pv, 1)

            def act(e, ch):
                for s in range(n + 3):
                    if s < n:
                        h, t = items[s]
                        nk = keys(t)
                        e.wait_ge(s_mx, s + 1)
                        if s >= 3:
                            e.wait_ge(s_t, s - 2)
                        c = s % 4
                        if gqa:
                            e.activation(es[:, c:c + 1], sink[:, h:h + 1], ACT.Exp, bias=nm_[:, c:c + 1])
                        e.activation(PB[:, s % 3, 0:nk], SB[:, s % 3, 0:nk] if gqa else PS[:, s % 3, 0:nk], ACT.Exp,
                                     bias=nm_[:, c:c + 1], scale=scale, accum_out=rs[:, c:c + 1]).then_inc(s_ex, 1)
                    i = s - 2
                    if 0 <= i < n:
                        h, t = items[i]
                        nk = keys(t) // P
                        e.wait_ge(s_t, i + 1)
                        if i >= 2:
                            e.wait_ge(s_pv, i - 1)
                        e.activation(PT[:, i % 2, 0:nk, :], PS[:, 3 + i % 2, 0:nk * P].rearrange("p (k q) -> p k q", k=nk), ACT.Copy).then_inc(s_pt, 1)
                    i = s - 3
                    if 0 <= i < n:
                        h, t = items[i]
                        r = slice(64 * (h % 2), 64 * (h % 2) + 64)
                        e.wait_ge(s_pv, i + 1)
                        e.activation(dst[r, h // 2, t * P:(t + 1) * P], PS[r, 5 + i % 2, 0:P], ACT.Copy).then_inc(s_o, 1)

            def dve(e, ch):
                for s in range(n + 1):
                    if s < n:
                        h, t = items[s]
                        nk = keys(t)
                        c = s % 4
                        e.wait_ge(s_sc, s + 1)
                        if s >= 3:
                            e.wait_ge(s_ex, s - 2)
                        src = PS[:, s % 3, 0:nk]
                        if gqa:
                            if t >= 2:
                                e.tensor_tensor(SB[:, s % 3, :], src, cst(f"win{t - 2}"), ALU.add).then_inc(s_mk, 1)
                            else:
                                e.tensor_copy(SB[:, s % 3, 0:nk], src).then_inc(s_mk, 1)
                            e.wait_ge(s_mk, s + 1)
                            src = SB[:, s % 3, 0:nk]
                        ch.run(e.tensor_reduce(mx[:, c:c + 1], src, AX.X, ALU.max))
                        if gqa:
                            ch.run(e.tensor_scalar(mx[:, c:c + 1], mx[:, c:c + 1], scale, sink[:, h:h + 1], ALU.mult, ALU.max))
                        e.tensor_scalar(nm_[:, c:c + 1], mx[:, c:c + 1], -1.0 if gqa else -scale, None, ALU.mult).then_inc(s_mx, 1)
                    i = s - 1
                    if 0 <= i:
                        h, t = items[i]
                        nk = keys(t)
                        c = i % 4
                        e.wait_ge(s_ex, i + 1)
                        if gqa:
                            ch.run(e.tensor_tensor(rs[:, c:c + 1], rs[:, c:c + 1], es[:, c:c + 1], ALU.add))
                        ch.run(e.reciprocal(rr[:, c:c + 1], rs[:, c:c + 1]))
                        e.tensor_scalar(PB[:, i % 3, 0:nk], PB[:, i % 3, 0:nk], rr[:, c:c + 1], None, ALU.mult).then_inc(s_p, 1)
            return dict(act=act, pe=pe, dve=dve)

        DT = ar(B0, NT, 3 * DW)
        qTd = ar(B0 + 6144, 4, T)
        kTd = ar(B0 + 8192, 4, T)
        E0 = B0 + 10240
        g2, gc, egc, ekg, beta, beg = (sm(64 * i, 2, NT, H) for i in range(6))
        glb = sm(384, 2, NT, 2, 4)

        def stage_dn_prep(l, t0):
            nm = f"s_dp_"
            s_w, s_zp, s_xc, s_cv, s_sl, s_tp, s_te, s_cw, s_cwe, s_ab, s_sq, s_ss, s_rt, s_nrm, s_qp, s_qe, s_g, s_gp, s_ga, s_gb, s_gz = (
                sem(nm + x) for x in ("w", "zp", "xc", "cv", "sl", "tp", "te", "cw", "cwe", "ab", "sq", "ss", "rt", "nrm", "qp", "qe", "g", "gp", "ga", "gb", "gz"))
            cwr = ar(E0 + 2064, 1536)[0:CONV]
            CW = sm(512, 12, CONV)
            XC = ar(E0, 2, 2, SEG + 4)
            YC = ar(E0 + 1040, 2, 2, SEG)
            sq = ar(E0, 2, D)
            ss, rt = sm(576, NT, 16), sm(640, NT, 16)
            alog, dtb = sm(704, 16), sm(720, 16)
            w1, w2, w3, w4 = (sm(736 + 64 * i, NT, 16) for i in range(4))

            def act(e, ch):
                e.dma_start(cwr, a["dn_conv"][l]).then_inc(s_w, 16)
                e.dma_start(alog, a["dn_a_log"][l:l + 1].rearrange("o d h -> o (d h)").broadcast_to([P, 16])).then_inc(s_ab, 16)
                e.dma_start(dtb, a["dn_dt_bias"][l:l + 1].rearrange("o d h -> o (d h)").broadcast_to([P, 16])).then_inc(s_ab, 16)
                e.wait_ge(s_g, 1)
                ch.run(e.activation(w2, w1, ACT.Abs))
                ch.run(e.activation(w2, w2, ACT.Exp, scale=-1.0))
                ch.run(e.activation(w2, w2, ACT.Ln, bias=1.0))
                e.wait_ge(s_ab, 32)
                ch.run(e.activation(alog, alog, ACT.Exp))
                e.sem_inc(s_ga, 1)
                for d in range(2):
                    ch.run(e.activation(beta[:, d], ZA[:, :, Z_B + d * H:Z_B + (d + 1) * H], ACT.Sigmoid))
                e.sem_inc(s_gb, 1)
                for m in range(12 + 2):
                    if m < 12:
                        e.wait_ge(s_zp, m + 1)
                        if m == 0:
                            e.wait_ge(s_gz, 1)
                        if m >= 2:
                            e.wait_ge(s_cv, m - 1)
                        e.activation(XC[:, m % 2, :, 2:2 + SEG], PS[:, m % 2, :].rearrange("p (s n) -> p s n", s=2), ACT.Copy).then_inc(s_xc, 1)
                    if m >= 1 and m - 1 < 12:
                        i = m - 1
                        e.wait_ge(s_cv, i + 1)
                        e.activation(YC[:, i % 2], YC[:, i % 2], ACT.Silu).then_inc(s_sl, 1)
                    if m >= 2:
                        i = m - 2
                        e.wait_ge(s_tp, i + 1)
                        e.activation(DT[:, :, i * P:(i + 1) * P], PS[:, 2 + i % 2, :].rearrange("p (t c) -> p t c", t=NT), ACT.Copy).then_inc(s_te, 1)
                for t in range(NT):
                    if t == 0:
                        e.wait_ge(s_te, 12)
                        e.wait_ge(s_cv, 12)
                        e.wait_ge(s_tp, 12)
                    if t >= 2:
                        e.wait_ge(s_ss, t - 1)
                    e.activation(sq[:, t % 2, :], DT[:, t, 0:D], ACT.Square).then_inc(s_sq, 1)
                e.wait_ge(s_ss, NT + 1)
                e.activation(rt, ss, ACT.Sqrt).then_inc(s_rt, 1)
                for i in range(2 * NT):
                    e.wait_ge(s_qp, i + 1)
                    t, half = i // 2, i % 2
                    dst = (qTd, kTd)[half]
                    e.activation(dst[:, :, t * P:(t + 1) * P], PS[:, 4 + i % 2, :].rearrange("p (j q) -> p j q", j=4), ACT.Copy).then_inc(s_qe, 1)
                e.wait_ge(s_gp, 1)
                pg = PS[:, 7, :]
                v64 = lambda o: pg[:, o:o + 64].rearrange("p (d t h) -> p d t h", d=2, t=NT)
                ch.run(e.activation(gc, v64(0), ACT.Copy))
                ch.run(e.activation(egc, v64(0), ACT.Exp))
                for c in range(2):
                    for p in range(2):
                        src = pg[64 * p:64 * p + 64, 128 + 64 * c:192 + 64 * c].rearrange("p (u j q) -> p u j q", u=8, q=2)[:, :, :, p]
                        o = glb[64 * p:64 * p + 64].rearrange("p d t c j -> p (d t) c j")[:, :, c, :]
                        ch.add(e.activation(o, src, ACT.Exp))
                ch.run(e.activation(w4.rearrange("p t n -> p (t n)"), pg[:, 64:128], ACT.Copy))
                e.sem_inc(s_ga, 1)
                e.wait_ge(s_g, 3)
                ch.run(e.activation(ekg, w3.rearrange("p t (a n) -> p (t a n)", a=2).rearrange("p (d t n) -> p d t n", d=2, t=NT), ACT.Exp))

            def dve(e, ch):
                ch.run(e.memset(XC[:, 0], 0.0))
                ch.run(e.memset(XC[:, 1], 0.0))
                e.sem_inc(s_gz, 1)
                e.wait_ge(s_ab, 32)
                ch.run(e.tensor_tensor(w1, ZA[:, :, Z_A:Z_A + 16], dtb.rearrange("p (o n) -> p o n", o=1).broadcast_to([P, NT, 16]), ALU.add))
                e.sem_inc(s_g, 1)
                e.wait_ge(s_ga, 1)
                ch.run(e.scalar_tensor_tensor(out=w1, in0=w1, scalar=0.0, in1=w2, op0=ALU.max, op1=ALU.add))
                ch.run(e.tensor_scalar(w1, w1, -1.0, None, ALU.mult))
                for d in range(2):
                    ch.run(e.tensor_tensor(g2[:, d], w1[:, :, d * H:(d + 1) * H],
                                           alog[:, d * H:(d + 1) * H].rearrange("p (o n) -> p o n", o=1).broadcast_to([P, NT, H]), ALU.mult))
                e.sem_inc(s_g, 1)
                e.wait_ge(s_cw, 1)
                ch.run(e.tensor_copy(CW, PS[:, 6, 0:60].rearrange("p (m j) -> p m j", m=12)))
                for m in range(12):
                    e.wait_ge(s_xc, m + 1)
                    if m >= 2:
                        e.wait_ge(s_tp, m - 1)
                    x, y = XC[:, m % 2], YC[:, m % 2]
                    ch.run(e.tensor_scalar(y, x[:, :, 0:SEG], CW[:, m, 0:1], None, ALU.mult))
                    for j in range(1, CONV):
                        ins = e.scalar_tensor_tensor(out=y, in0=x[:, :, j:j + SEG], scalar=CW[:, m, j:j + 1], in1=y, op0=ALU.mult, op1=ALU.add)
                        if j < CONV - 1:
                            ch.run(ins)
                        else:
                            ins.then_inc(s_cv, 1)
                            e.wait_ge(s_cv, m + 1)
                for t in range(NT):
                    e.wait_ge(s_sq, t + 1)
                    e.tensor_reduce(ss[:, t, :], sq[:, t % 2, :].rearrange("p (h n) -> p h n", n=HD), AX.X, ALU.add).then_inc(s_ss, 1)
                e.wait_ge(s_ss, NT)
                ch.run(e.tensor_scalar(ss, ss, 1e-6, None, ALU.add))
                e.sem_inc(s_ss, 1)
                e.wait_ge(s_rt, 1)
                ch.run(e.reciprocal(ss, rt))
                ch.run(e.tensor_scalar(ss[:, :, 0:H], ss[:, :, 0:H], HD ** -0.5, None, ALU.mult))
                for t in range(NT):
                    qk = DT[:, t, 0:D].rearrange("p (h n) -> p h n", n=HD)
                    e.tensor_tensor(qk, qk, ss[:, t, :].rearrange("p (h o) -> p h o", o=1).broadcast_to([P, 16, HD]), ALU.mult).then_inc(s_nrm, 1)
                e.wait_ge(s_ga, 2)
                ch.run(e.tensor_tensor(w3.rearrange("p t n -> p (t n)"), w4.rearrange("p t n -> p (t n)"), gc.rearrange("p d t h -> p (d t h)"), ALU.subtract))
                e.sem_inc(s_g, 1)
                e.wait_ge(s_gb, 1)
                ch.run(e.tensor_tensor(beg, beta, egc, ALU.mult))
                ch.run(e.tensor_copy(DZ[:, t0:NT], ZA[:, t0:NT, Z_DZ:Z_DZ + DW]))

            def pe(e):
                e.wait_ge(s_w, 16)
                for m in range(12):
                    x = e.transpose(PS[:, 6, m * CONV:(m + 1) * CONV], cwr[:, m * P:(m + 1) * P], ident[0:CONV, 0:CONV])
                x.then_inc(s_cw, 1)
                for m in range(12 + 1):
                    if m < 12:
                        key = ("dqkv", l, m // 4)
                        landed(e, key)
                        w = slot(key, 0, KT, 512)
                        if m >= 2:
                            e.wait_ge(s_xc, m - 1)
                        for k in range(KT):
                            x = e.matmul(PS[:, m % 2, :], w[:, k, (m % 4) * P:(m % 4 + 1) * P], UT[:, k, :], start=k == 0, stop=k == KT - 1)
                        x.then_inc(s_zp, 1)
                        if m % 4 == 3:
                            e.wait_ge(s_zp, m + 1)
                            e.sem_inc(s_wfree, 1)
                    if m >= 1:
                        i = m - 1
                        e.wait_ge(s_sl, i + 1)
                        if i >= 2:
                            e.wait_ge(s_te, i - 1)
                        for t in range(NT):
                            y = YC[:, i % 2].rearrange("p s n -> p (s n)")
                            x = e.transpose(PS[:, 2 + i % 2, t * P:(t + 1) * P], y[:, t * P:(t + 1) * P], ident)
                        x.then_inc(s_tp, 1)
                for i in range(2 * NT):
                    t, half = i // 2, i % 2
                    e.wait_ge(s_nrm, t + 1)
                    if i >= 2:
                        e.wait_ge(s_qe, i - 1)
                    for j in range(4):
                        x = e.transpose(PS[:, 4 + i % 2, j * P:(j + 1) * P], DT[:, t, half * DW + j * P:half * DW + (j + 1) * P], ident)
                    x.then_inc(s_qp, 1)
                e.wait_ge(s_g, 2)
                g2f = g2.rearrange("p d t h -> p (d t h)")
                for d in range(2):
                    e.matmul(PS[:, 7, 32 * d:32 * d + 32], cst(f"tri{d}"), g2f[:, 32 * d:32 * d + 32], start=True, stop=True)
                e.matmul(PS[:, 7, 64:128], cst("blk"), g2f, start=True, stop=True)
                for c in range(2):
                    x = e.matmul(PS[:, 7, 128 + 64 * c:192 + 64 * c], cst(f"sel{c}"), g2f, start=True, stop=True)
                x.then_inc(s_gp, 1)
            return dict(act=act, pe=pe, dve=dve)

        O_DN = ar(B0 + 6144, 4, T)

        def by_parity(v, p):
            return v.rearrange("q (j p) -> q j p", p=2)[:, :, p:p + 1]

        def stage_dn_scan(l, t0):
            nm = f"s_ds_"
            pp = {k: [sem(f"{nm}{k}{p}") for p in range(2)] for k in ("gr", "df", "e", "a", "al", "x", "r", "tp", "t", "xp", "y", "vb", "uw", "ue", "kd")}
            s_S, s_ws, s_vn, s_o1, s_kv, s_kg = (sem(nm + x) for x in ("S", "ws", "vn", "o1", "kv", "kg"))
            U = ar(0, H, HD)
            WT = ar(512, 4, P)
            QKD = ar(1024, 2, 2, 4, P)
            KG = ar(3072, H, HD)
            S = ar(3584, 2, 4, P)
            O1, VN = ar(4608, H, HD), ar(5120, H, HD)
            AL = ar(5632, 2, 4, P)
            A, R, TT, XP = (ar(E0 + 1024 * i, 2, 4, P) for i in range(4))
            VB = [AL[:, p, 0:2, :].rearrange("q j n -> q (j n)").rearrange("q (j n) -> q j n", n=HD) for p in range(2)]
            KBG = [AL[:, p, 2:4, :].rearrange("q j n -> q (j n)").rearrange("q (j n) -> q j n", n=HD) for p in range(2)]
            units = [(d, t) for s in range(4) for d, t in ((0, s), (1, (1, 0, 3, 2)[s]))]
            n = len(units)
            first = {}
            for u, (d, t) in enumerate(units):
                first.setdefault(t, u)
            BA, BB = 6, 7

            def bank(p, b):
                return PS[:, 3 * p + b, :].rearrange("q (j n) -> q j n", j=4)

            def mask(x):
                return x.rearrange("q (o n) -> q o n", o=1).broadcast_to([P, 4, P])

            def per_head(v, d, t, p, n=P):
                return by_parity(v[:, d, t, :], p).broadcast_to([P, 4, n])

            def all_heads(v, d, t, r=slice(0, P)):
                return v[r, d, t, :].rearrange("q (h o) -> q h o", o=1).broadcast_to([r.stop - r.start, H, HD])

            def heads(part, t, p):
                return DT[:, t, part * DW:(part + 1) * DW].rearrange("q (j p n) -> q j p n", p=2, n=HD)[:, :, p, :]

            def rows(p):
                return slice(64 * p, 64 * p + 64)

            def chunk(u, ci):
                d, t = units[u]
                c = ci if d == 0 else 1 - ci
                return d, t, c, rows(c)

            def pe(e):
                def w_s(u, ci):
                    d, t, c, r = chunk(u, ci)
                    if ci == 0:
                        for p in range(2):
                            e.wait_ge(pp["ue"][p], u + 1)
                            e.wait_ge(pp["kd"][p], u + 1)
                    e.wait_ge(s_S, 2 * u + ci + 1)
                    for j in range(4):
                        m = e.matmul(PS[r, BA, j * P:(j + 1) * P], WT[:, j, r], S[:, d, j, :], start=True, stop=True)
                        if t >= t0:
                            m = e.matmul(PS[r, BB, j * P:(j + 1) * P], qTd[:, j, t * P + 64 * c:t * P + 64 * c + 64], S[:, d, j, :], start=True, stop=True)
                    m.then_inc(s_ws, 1)

                def k_v(u, ci):
                    d, t, c, r = chunk(u, ci)
                    e.wait_ge(s_kg, u + 1)
                    e.wait_ge(s_vn, 2 * u + ci + 1)
                    for j in range(4):
                        m = e.matmul(PS[:, BA, j * P:(j + 1) * P], KG[r, 2 * j:2 * j + 2, :].rearrange("q h n -> q (h n)"),
                                     VN[r, 2 * j:2 * j + 2, :].rearrange("q h n -> q (h n)"), start=True, stop=True)
                    if t >= t0:
                        e.wait_ge(s_o1, 2 * u + ci + 1)
                        for h in range(H):
                            m = e.matmul(PS[r, BB, h * HD:(h + 1) * HD], QKD[r, u % 2, h % 2, h // 2, r], VN[r, h, :], start=True, stop=True)
                    m.then_inc(s_kv, 1)

                def level(u, s):
                    for p in range(2):
                        e.wait_ge(pp["al"][p], LEVELS * u + s + 1)
                        if s:
                            e.wait_ge(pp["r"][p], LEVELS * u + s)
                        for j in range(4):
                            if s == 0:
                                m = e.transpose(bank(p, 0)[:, j], AL[:, p, j, :], ident)
                            else:
                                m = e.matmul(bank(p, 0)[:, j], AL[:, p, j, :], R[:, p, j, :], start=True, stop=True)
                        m.then_inc(pp["x"][p], 1)
                        if s > 1:
                            for j in range(4):
                                m = e.transpose(bank(p, 2)[:, j], R[:, p, j, :], ident)
                            m.then_inc(pp["tp"][p], 1)
                    for p in range(2):
                        if s:
                            e.wait_ge(pp["t"][p], (LEVELS - 1) * u + s)
                            e.wait_ge(pp["xp"][p], (LEVELS - 1) * u + s)
                            for j in range(4):
                                m = e.matmul(bank(p, 1)[:, j], TT[:, p, j, :], XP[:, p, j, :], start=True, stop=True)
                            m.then_inc(pp["y"][p], 1)

                for u in range(n + 1):
                    if u < n:
                        d, t = units[u]
                        tc = slice(t * P, (t + 1) * P)
                        for p in range(2):
                            if u:
                                e.wait_ge(pp["ue"][p], u)
                            for j in range(4):
                                h = 2 * j + p
                                g = g2[:, d, t, h:h + 1].broadcast_to([P, P])
                                e.matmul(bank(p, 0)[:, j], g, cst(f"tri{d}"), start=True, stop=True)
                                k, q = kTd[rows(p), j, tc], qTd[rows(p), j, tc]
                                m = e.matmul(bank(p, 1)[:, j], k, k, start=True, stop=True)
                                if t >= t0:
                                    m = e.matmul(bank(p, 2)[:, j], k, q, start=True, stop=True)
                            m.then_inc(pp["gr"][p], 1)
                    if u:
                        w_s(u - 1, 0)
                        k_v(u - 1, 0)
                    if u < n:
                        level(u, 0)
                    if u:
                        w_s(u - 1, 1)
                    if u < n:
                        level(u, 1)
                    if u:
                        k_v(u - 1, 1)
                    if u < n:
                        for s in range(2, LEVELS):
                            level(u, s)
                        for p in range(2):
                            e.wait_ge(pp["vb"][p], u + 1)
                            e.wait_ge(pp["r"][p], LEVELS * (u + 1))
                            for j in range(4):
                                e.matmul(PS[:, 3 * p + 2, j * HD:(j + 1) * HD], R[:, p, j, :], VB[p][:, j, :], start=True, stop=True)
                                m = e.matmul(bank(p, 0)[rows(p), j], KBG[p][:, j, :], R[:, p, j, :], start=True, stop=True)
                            m.then_inc(pp["uw"][p], 1)

            def act(e, ch):
                for u, (d, t) in enumerate(units):
                    for p in range(2):
                        e.wait_ge(pp["df"][p], u + 1)
                        ch.run(e.activation(XP[:, p], XP[:, p], ACT.Abs))
                        e.activation(XP[:, p], XP[:, p], ACT.Exp, scale=-1.0).then_inc(pp["e"][p], 1)
                    for s in range(1, LEVELS):
                        for p in range(2):
                            e.wait_ge(pp["x"][p], LEVELS * u + s + 1)
                            if s == 1:
                                e.wait_ge(pp["a"][p], u + 1)
                            e.activation(XP[:, p], bank(p, 0), ACT.Copy).then_inc(pp["xp"][p], 1)
                    e.wait_ge(s_S, 2 * u + 1)
                    for p in range(2):
                        e.wait_ge(pp["uw"][p], u + 1)
                        e.activation(U.rearrange("q (j p) n -> q j p n", p=2)[:, :, p, :],
                                     PS[:, 3 * p + 2, 0:256].rearrange("q (j n) -> q j n", j=4), ACT.Copy)
                        e.activation(WT[rows(p)], bank(p, 0)[rows(p)], ACT.Copy).then_inc(pp["ue"][p], 1)

            def dve(e, ch):
                def v_new(u, ci):
                    d, t, c, r = chunk(u, ci)
                    e.wait_ge(s_ws, 2 * u + ci + 1)
                    if ci == 0:
                        for p in range(2):
                            e.wait_ge(pp["ue"][p], u + 1)
                    e.tensor_tensor(VN[r], U[r], PS[r, BA, :].rearrange("q (h n) -> q h n", h=H), ALU.subtract).then_inc(s_vn, 1)
                    if t >= t0:
                        e.tensor_tensor(O1[r], PS[r, BB, :].rearrange("q (h n) -> q h n", h=H), all_heads(egc, d, t, r), ALU.mult).then_inc(s_o1, 1)
                    else:
                        e.sem_inc(s_o1, 1)
                    ch.add(e.tensor_tensor(S[:, d], S[:, d], glb[:, d, t, c, :].rearrange("q (j o) -> q j o", o=1).broadcast_to([P, 4, P]), ALU.mult))

                def finish(u, ci):
                    d, t, c, r = chunk(u, ci)
                    ch.sync()
                    e.wait_ge(s_kv, 2 * u + ci + 1)
                    for p in range(2):
                        o = slice(p * HD, (p + 1) * HD)
                        ch.add(e.tensor_tensor(S[rows(p), d, :, o], S[rows(p), d, :, o],
                                               PS[rows(p), BA, :].rearrange("q (j n) -> q j n", j=4)[:, :, o], ALU.add))
                    if t >= t0:
                        o = DT[r, t, 0:DW].rearrange("q (h n) -> q h n", n=HD)
                        kv = PS[r, BB, :].rearrange("q (h n) -> q h n", h=H)
                        e.wait_ge(s_o1, 2 * u + ci + 1)
                        if first[t] == u:
                            ch.add(e.tensor_tensor(o, O1[r], kv, ALU.add))
                        else:
                            ch.run(e.tensor_tensor(O1[r], O1[r], kv, ALU.add))
                            ch.add(e.tensor_tensor(o, o, O1[r], ALU.add))
                    ch.sync()
                    e.sem_inc(s_S, 1)

                def level(u, s):
                    for p in range(2):
                        if s == 0:
                            e.wait_ge(pp["al"][p], LEVELS * u + 1)
                            e.tensor_tensor(TT[:, p], mask(ident), AL[:, p], ALU.subtract).then_inc(pp["t"][p], 1)
                            e.wait_ge(pp["x"][p], LEVELS * u + 1)
                            e.tensor_tensor(R[:, p], mask(ident), bank(p, 0), ALU.subtract).then_inc(pp["r"][p], 1)
                        else:
                            if s > 1:
                                e.wait_ge(pp["tp"][p], (LEVELS - 2) * u + s - 1)
                                e.tensor_copy(TT[:, p], bank(p, 2)).then_inc(pp["t"][p], 1)
                    for p in range(2):
                        if s:
                            e.wait_ge(pp["y"][p], (LEVELS - 1) * u + s)
                            e.tensor_tensor(R[:, p], R[:, p], bank(p, 1), ALU.subtract).then_inc(pp["r"][p], 1)

                ch.run(e.memset(S, 0.0))
                e.sem_inc(s_S, 1)
                for u in range(n + 1):
                    if u < n:
                        d, t = units[u]
                        for p in range(2):
                            e.wait_ge(pp["gr"][p], u + 1)
                            e.tensor_tensor(XP[:, p], bank(p, 0), per_head(gc, d, t, p), ALU.subtract).then_inc(pp["df"][p], 1)
                    if u:
                        v_new(u - 1, 0)
                    if u < n:
                        for p in range(2):
                            e.wait_ge(pp["e"][p], u + 1)
                            if t >= t0:
                                ch.add(e.tensor_tensor(QKD[:, u % 2, p], bank(p, 2), XP[:, p], ALU.mult))
                            ch.run(e.tensor_tensor(A[:, p], bank(p, 1), XP[:, p], ALU.mult))
                            e.tensor_tensor(A[:, p], A[:, p], per_head(beta, d, t, p), ALU.mult).then_inc(pp["a"][p], 1)
                    if u:
                        finish(u - 1, 0)
                    if u < n:
                        level(u, 0)
                    if u:
                        v_new(u - 1, 1)
                    if u < n:
                        level(u, 1)
                    if u:
                        finish(u - 1, 1)
                    if u < n:
                        for s in range(2, LEVELS):
                            level(u, s)

            def pool(e, ch):
                for u, (d, t) in enumerate(units):
                    for s in range(LEVELS):
                        for p in range(2):
                            if s == 0:
                                e.wait_ge(pp["a"][p], u + 1)
                                if u:
                                    e.wait_ge(pp["uw"][p], u)
                            else:
                                e.wait_ge(pp["x"][p], LEVELS * u + s)
                                if s == 1:
                                    e.wait_ge(pp["t"][p], (LEVELS - 1) * u + 1)
                            e.tensor_tensor(AL[:, p], A[:, p], mask(cst(f"lvl{d}{s}")), ALU.mult).then_inc(pp["al"][p], 1)
                            if s == 2:
                                if t >= t0:
                                    ch.run(e.tensor_tensor(QKD[:, u % 2, p], QKD[:, u % 2, p], mask(cst(f"tri{d}")), ALU.mult))
                                e.sem_inc(pp["kd"][p], 1)
                        if s == 3:
                            e.wait_ge(s_S, 2 * u + 1)
                            e.tensor_tensor(KG, DT[:, t, DW:2 * DW].rearrange("q (h n) -> q h n", n=HD), all_heads(ekg, d, t), ALU.mult).then_inc(s_kg, 1)
                    for p in range(2):
                        e.wait_ge(pp["x"][p], LEVELS * (u + 1))
                        ch.add(e.tensor_tensor(VB[p], heads(2, t, p), per_head(beta, d, t, p, HD), ALU.mult))
                        ch.add(e.tensor_tensor(KBG[p], heads(1, t, p), per_head(beg, d, t, p, HD), ALU.mult))
                        ch.sync()
                        e.sem_inc(pp["vb"][p], 1)
            return dict(act=act, pe=pe, dve=dve, pool=pool)

        def stage_dn_out(l, t0):
            s_nw, s_sq, s_ss, s_rt, s_z, s_o, s_tp, s_te = (sem(f"s_do_{x}") for x in ("nw", "sq", "ss", "rt", "z", "o", "tp", "te"))
            nw = sm(576, HD)
            ss, rt = sm(640, NT, H), sm(672, NT, H)
            sq = ar(0, NT, DW)
            zs = ar(2048, NT, DW)
            tiles = range(t0, NT)
            nt = len(tiles)

            def act(e, ch):
                e.dma_start(nw, a["dn_norm"][l:l + 1, :].broadcast_to([P, HD])).then_inc(s_nw, 16)
                e.activation(sq[:, t0:NT], DT[:, t0:NT, 0:DW], ACT.Square).then_inc(s_sq, 1)
                e.activation(zs[:, t0:NT], DZ[:, t0:NT], ACT.Silu).then_inc(s_z, 1)
                e.wait_ge(s_ss, 1)
                e.activation(rt[:, t0:NT], ss[:, t0:NT], ACT.Sqrt).then_inc(s_rt, 1)
                for i, t in enumerate(tiles):
                    e.wait_ge(s_tp, i + 1)
                    e.activation(O_DN[:, :, t * P:(t + 1) * P], PS[:, i % 2, :].rearrange("p (j q) -> p j q", j=4), ACT.Copy).then_inc(s_te, 1)

            def dve(e, ch):
                e.wait_ge(s_sq, 1)
                ch.run(e.tensor_reduce(ss[:, t0:NT], sq[:, t0:NT].rearrange("p t (h n) -> p t h n", n=HD), AX.X, ALU.add))
                ch.run(e.tensor_scalar(ss[:, t0:NT], ss[:, t0:NT], 1.0 / HD, EPS, ALU.mult, ALU.add))
                e.sem_inc(s_ss, 1)
                e.wait_ge(s_rt, 1)
                ch.run(e.reciprocal(ss[:, t0:NT], rt[:, t0:NT]))
                e.wait_ge(s_nw, 16)
                e.wait_ge(s_z, 1)
                for t in tiles:
                    o = DT[:, t, 0:DW].rearrange("p (h n) -> p h n", n=HD)
                    z = zs[:, t].rearrange("p (h n) -> p h n", n=HD)
                    ch.add(e.tensor_tensor(z, z, nw.rearrange("p (o n) -> p o n", o=1).broadcast_to([P, H, HD]), ALU.mult))
                    ch.run(e.tensor_tensor(o, o, ss[:, t, :].rearrange("p (h o) -> p h o", o=1).broadcast_to([P, H, HD]), ALU.mult))
                    e.tensor_tensor(o, o, z, ALU.mult).then_inc(s_o, 1)

            def pe(e):
                for i, t in enumerate(tiles):
                    e.wait_ge(s_o, i + 1)
                    if i >= 2:
                        e.wait_ge(s_te, i - 1)
                    for j in range(4):
                        m = e.transpose(PS[:, i % 2, j * P:(j + 1) * P], DT[:, t, j * P:(j + 1) * P], ident)
                    m.then_inc(s_tp, 1)
            return dict(act=act, pe=pe, dve=dve)

        def ln_stats(e, ch, t, i, s_var):
            st, mv = sm(0, 2, 6), sm(16 + 4 * i, 2)
            for c in range(2):
                ch.add(e.bn_stats(st[:, c, :], X[:, t, c * 512:(c + 1) * 512]))
            ch.sync()
            ch.run(e.bn_aggr(mv, st.rearrange("p a b -> p (a b)")))
            e.tensor_scalar(mv[:, 1:2], mv[:, 1:2], EPS, None, ALU.add).then_inc(s_var, 1)

        def root(e, i, s_var, s_std):
            e.wait_ge(s_var, i + 1)
            e.activation(sm(32 + i, 1), sm(17 + 4 * i, 1), ACT.Sqrt).then_inc(s_std, 1)

        def ln_roots(e, n, s_var, s_std):
            for i in range(n):
                root(e, i, s_var, s_std)

        def ln_scale(e, ch, t, i, s_std, s_nx):
            mv, rs = sm(16 + 4 * i, 2), sm(48 + i, 1)
            e.wait_ge(s_std, i + 1)
            ch.run(e.reciprocal(rs, sm(32 + i, 1)))
            e.tensor_scalar(X[:, t, :], X[:, t, :], mv[:, 0:1], rs, ALU.subtract, ALU.mult).then_inc(s_nx, 1)

        def ln_gains(e, ch, tiles, lnb, s_nx):
            for i, t in enumerate(tiles):
                e.wait_ge(s_nx, i + 1)
                ch.run(e.tensor_tensor(X[:, t, :], X[:, t, :], lnb[:, 0], ALU.mult))
                ch.run(e.tensor_tensor(X[:, t, :], X[:, t, :], lnb[:, 1], ALU.add))

        def stage_merge(l, t0):
            nm = f"s_mg_"
            s_gp, s_sg, s_op, s_tm, s_mt, s_ld, s_yp, s_ye, s_var, s_std, s_nx = (sem(nm + x) for x in ("gp", "sg", "op", "tm", "mt", "ld", "yp", "ye", "var", "std", "nx"))
            s_next = sem("s_u1_m")
            MT = ar(0, KT, T)
            TM = ar(4096, 2, T)
            SGb = ar(B0, KT, T)
            GM = ar(B0 + 4096 + 4096, 2, 1, D)
            LNB = ar(B0 + 4096 + 6144, 2, D)
            n0 = t0 * P
            tiles = range(t0, NT)
            nt = len(tiles)
            src = (O_MLA, O_DN, O_GQA)

            def pe(e):
                for b in range(3):
                    for mt in range(KT):
                        i = b * KT + mt
                        key = ("gate", l, b, mt // 4)
                        landed(e, key)
                        w = slot(key, 0, KT, 512)
                        if i >= 2:
                            e.wait_ge(s_sg, i - 1)
                        for k in range(KT):
                            m = e.matmul(PS[:, i % 2, n0:T], w[:, k, (mt % 4) * P:(mt % 4 + 1) * P], UT[:, k, n0:T], start=k == 0, stop=k == KT - 1)
                        m.then_inc(s_gp, 1)
                        if mt % 4 == 3:
                            e.wait_ge(s_gp, i + 1)
                            e.sem_inc(s_wfree, 1)
                    key = ("o", l, b)
                    landed(e, key)
                    w = slot(key, 0, 4, D)
                    for mt in range(KT):
                        i = b * KT + mt
                        if i >= 2:
                            e.wait_ge(s_tm, i - 1)
                        for k in range(4):
                            m = e.matmul(PS[:, 2 + i % 2, n0:T], w[:, k, mt * P:(mt + 1) * P], src[b][:, k, n0:T], start=k == 0, stop=k == 3)
                        m.then_inc(s_op, 1)
                    e.wait_ge(s_op, KT * (b + 1))
                    e.sem_inc(s_wfree, 1)
                e.wait_ge(s_tm, 3 * KT)
                e.wait_ge(s_mt, 2 * KT)
                for c in range(2):
                    key = ("out", l, c)
                    landed(e, key)
                    w = slot(key, 0, KT, 512)
                    for ti, t in enumerate(tiles):
                        i = c * nt + ti
                        if i >= 4:
                            e.wait_ge(s_ye, i - 3)
                        for k in range(KT):
                            m = e.matmul(PS[:, 4 + i % 4, :], MT[:, k, t * P:(t + 1) * P], w[:, k, :], start=k == 0, stop=k == KT - 1)
                        m.then_inc(s_yp, 1)
                    e.wait_ge(s_yp, nt * (c + 1))
                    e.sem_inc(s_wfree, 1)

            def act(e, ch):
                modulation(e, l, (2,), GM, s_ld, range(t0 // 2, 2))
                for i, nm_ in enumerate(("ln1_g", "ln1_b")):
                    e.dma_start(LNB[:, i, :], a[nm_][l:l + 1, :].broadcast_to([P, D])).then_inc(s_ld, 16)
                for i in range(3 * KT):
                    e.wait_ge(s_gp, i + 1)
                    if i >= KT:
                        e.wait_ge(s_tm, i - KT + 1)
                    e.activation(SGb[:, i % KT, n0:T], PS[:, i % 2, n0:T], ACT.Sigmoid).then_inc(s_sg, 1)
                e.wait_ge(s_op, 3 * KT)
                modulation(e, l, (3, 4), ar(ZW * NT, 2, 2, D), s_next, range(t0 // 2, 2))
                ln_roots(e, nt, s_var, s_std)

            def dve(e, ch):
                for i in range(3 * KT):
                    mt = i % KT
                    e.wait_ge(s_op, i + 1)
                    e.wait_ge(s_sg, i + 1)
                    if i >= KT + 2:
                        e.wait_ge(s_mt, i - KT - 1)
                    o = MT[:, mt, n0:T] if i < KT else TM[:, i % 2, n0:T]
                    e.tensor_tensor(o, SGb[:, mt, n0:T], PS[:, 2 + i % 2, n0:T], ALU.mult).then_inc(s_tm, 1)
                e.wait_ge(s_ld, 64 if t0 == 0 else 48)
                ty = TM
                for c in range(2):
                    for ti, t in enumerate(tiles):
                        i = c * nt + ti
                        e.wait_ge(s_yp, i + 1)
                        if i == 0:
                            e.wait_ge(s_mt, 2 * KT)
                        o = slice(c * 512, (c + 1) * 512)
                        e.tensor_tensor(ty[:, i % 2, :], PS[:, 4 + i % 4, :], GM[:, t // 2, 0, o], ALU.mult).then_inc(s_ye, 1)
                        e.wait_ge(s_ye, i + 1)
                        ch.run(e.scalar_tensor_tensor(out=X[:, t, o], in0=X[:, t, o], scalar=ALPHA, in1=ty[:, i % 2, :], op0=ALU.mult, op1=ALU.add))
                        if c == 1:
                            ln_stats(e, ch, t, ti, s_var)
                for i, t in enumerate(tiles):
                    ln_scale(e, ch, t, i, s_std, s_nx)

            def pool(e, ch):
                for i in range(KT, 3 * KT):
                    e.wait_ge(s_tm, i + 1)
                    if i >= 2 * KT:
                        e.wait_ge(s_mt, i - 2 * KT + 1)
                    mt = i % KT
                    e.tensor_tensor(MT[:, mt, n0:T], MT[:, mt, n0:T], TM[:, i % 2, n0:T], ALU.add).then_inc(s_mt, 1)
                e.wait_ge(s_ld, 64 if t0 == 0 else 48)
                ln_gains(e, ch, tiles, LNB, s_nx)
            return dict(act=act, pe=pe, dve=dve, pool=pool)

        FS = ar(0, NT, D)
        R0 = 4096
        DEST = ar(R0, NT, NE)
        RV = ar(R0 + 256, NT, NE)
        WK = sm(1000, TOPK, NT)
        M0 = R0 + 512
        XG = ar(M0, 2, D)

        def stage_route(l, t0):
            nm = f"s_ro_"
            s_b, s_lg, s_sc, s_m, s_ct, s_ti, s_be, s_gp, s_sg, s_h, s_hp, s_he, s_yp, s_ye, s_cs = (
                sem(nm + x) for x in ("b", "lg", "sc", "m", "ct", "ti", "be", "gp", "sg", "h", "hp", "he", "yp", "ye", "cs"))
            tiles = range(t0, NT)
            nt = len(tiles)
            Q0 = M0 + 2048
            SC, SEL, MK, W, EQ, CUM, RM, TMP = (ar(Q0 + 256 * i, NT, NE) for i in range(8))
            PR = ar(Q0 + 2048, NT, NG, NG)
            PE_ = ar(Q0 + 2304, NT, NG, NG)
            M8 = ar(Q0 + 2560, NT, NG, 8)
            BIAS = ar(Q0 + 2816, NE)
            CNT, NBK, CB_, T64 = (ar(Q0 + 2880 + 64 * i, NE) for i in range(4))
            HS = ar(Q0 + 3200, 2, FE)
            SGs = ar(Q0 + 3712, 2, FE)
            HTs = ar(Q0 + 4224, 2, 2, P)
            GS, RK, GMK = (sm(128 + 32 * i, NT, NG) for i in range(3))
            V8, NGT, SUM = sm(224, NT, 8), sm(256, NT), sm(260, NT)
            n64 = sm(264, 1)
            be = sm(268, 1)

            def tb(v, n):
                return v.rearrange("p (o n) -> p o n", o=1).broadcast_to([P, nt, n])

            def act(e, ch):
                e.dma_start(BIAS, a["router_bias"][l:l + 1, :].broadcast_to([P, NE])).then_inc(s_b, 16)
                e.wait_ge(s_lg, 1)
                e.activation(SC[:, t0:NT], PS[:, 0, t0 * NE:NT * NE].rearrange("p (t n) -> p t n", t=nt), ACT.Sigmoid).then_inc(s_sc, 1)
                for i in range(nt):
                    e.wait_ge(s_gp, i + 1)
                    e.activation(SGs[:, i % 2], PS[:, 2 + i % 2, 0:FE], ACT.Silu).then_inc(s_sg, 1)
                    e.wait_ge(s_hp, i + 1)
                    e.activation(HTs[:, i % 2], PS[:, 4, 0:256].rearrange("p (k q) -> p k q", k=2), ACT.Copy).then_inc(s_he, 1)
                    for c in range(2):
                        e.wait_ge(s_yp, 2 * i + c + 1)
                        e.activation(FS[:, t0 + i, c * 512:(c + 1) * 512], PS[:, 6 + c, :], ACT.Copy).then_inc(s_ye, 1)
                e.wait_ge(s_ti, 1)
                e.dma_start(blk_d, BEI[:, :]).then_inc(s_be, 16)
                e.wait_ge(s_be, 16)
                e.dma_start(EXPERT[:, :], blk_d.rearrange("p o -> o p")).then_inc(s_be, 16)
                e.wait_ge(s_be, 32)

            def pe(e):
                landed(e, ("router", l))
                w = slot(("router", l), 0, KT, NE)
                for t in tiles:
                    for k in range(KT):
                        m = e.matmul(PS[:, 0, t * NE:(t + 1) * NE], UT[:, k, t * P:(t + 1) * P], w[:, k, :], start=k == 0, stop=k == KT - 1)
                m.then_inc(s_lg, 1)
                e.wait_ge(s_lg, 1)
                e.sem_inc(s_wfree, 1)
                landed(e, ("shgu", l))
                landed(e, ("shd", l))
                wg, wu = slot(("shgu", l), 0, KT, FE), slot(("shgu", l), KT * FE, KT, FE)
                wd = slot(("shd", l), 0, 2, D)
                for i in range(nt + 1):
                    if i < nt:
                        t = t0 + i
                        if i >= 2:
                            e.wait_ge(s_h, i - 1)
                        for half, ww in ((0, wg), (1, wu)):
                            for k in range(KT):
                                m = e.matmul(PS[:, 2 + i % 2, half * FE:(half + 1) * FE], UT[:, k, t * P:(t + 1) * P], ww[:, k, :], start=k == 0, stop=k == KT - 1)
                        m.then_inc(s_gp, 1)
                    if i >= 1:
                        j = i - 1
                        e.wait_ge(s_h, j + 1)
                        if j >= 1:
                            e.wait_ge(s_he, j)
                        for k in range(2):
                            m = e.transpose(PS[:, 4, k * P:(k + 1) * P], HS[:, j % 2, k * P:(k + 1) * P], ident)
                        m.then_inc(s_hp, 1)
                        if j == nt - 1:
                            e.wait_ge(s_m, 1)
                            for t in tiles:
                                for t2 in range(t0, t + 1):
                                    m = e.matmul(PS[:, 1, t * NE:(t + 1) * NE], cst("ones" if t2 < t else "before"), MK[:, t2, :], start=t2 == t0, stop=t2 == t)
                            for t in tiles:
                                m = e.matmul(PS[:, 1, 256:256 + NE], cst("ones"), MK[:, t, :], start=t == t0, stop=t == NT - 1)
                            m.then_inc(s_ct, 1)
                        e.wait_ge(s_he, j + 1)
                        for c in range(2):
                            if j >= 1:
                                e.wait_ge(s_ye, 2 * j + c - 1)
                            for k in range(2):
                                m = e.matmul(PS[:, 6 + c, :], HTs[:, j % 2, k, :], wd[:, k, c * 512:(c + 1) * 512], start=k == 0, stop=k == 1)
                            m.then_inc(s_yp, 1)
                e.wait_ge(s_yp, 2 * nt)
                e.sem_inc(s_wfree, 2)

            def shared_hidden(e, i):
                e.wait_ge(s_sg, i + 1)
                if i >= 2:
                    e.wait_ge(s_hp, i - 1)
                e.tensor_tensor(HS[:, i % 2], SGs[:, i % 2], PS[:, 2 + i % 2, FE:2 * FE], ALU.mult).then_inc(s_h, 1)

            def dve(e, ch):
                R = slice(t0, NT)
                e.wait_ge(s_b, 16)
                e.wait_ge(s_sc, 1)
                ch.run(e.tensor_tensor(SEL[:, R], SC[:, R], tb(BIAS, NE), ALU.add))
                for t in tiles:
                    for g in range(NG):
                        ch.add(e.max(M8[:, t, g, :], SEL[:, t, g * 8:(g + 1) * 8]))
                ch.sync()
                ch.run(e.tensor_tensor(GS[:, R], M8[:, R, :, 0], M8[:, R, :, 1], ALU.add))
                if 0 < nt:
                    shared_hidden(e, 0)
                gj = GS[:, R].rearrange("p t (o j) -> p t o j", o=1).broadcast_to([P, nt, NG, NG])
                gi = GS[:, R].rearrange("p t (i o) -> p t i o", o=1).broadcast_to([P, nt, NG, NG])
                low = cst("glow").rearrange("p (o i j) -> p o i j", o=1, i=NG).broadcast_to([P, nt, NG, NG])
                ch.add(e.tensor_tensor(PR[:, R], gj, gi, ALU.is_gt))
                ch.run(e.tensor_tensor(PE_[:, R], gj, gi, ALU.is_equal))
                ch.run(e.tensor_tensor(PE_[:, R], PE_[:, R], low, ALU.mult))
                ch.run(e.tensor_tensor(PR[:, R], PR[:, R], PE_[:, R], ALU.add))
                ch.run(e.tensor_reduce(RK[:, R], PR[:, R], AX.X, ALU.add))
                ch.run(e.tensor_scalar(GMK[:, R], RK[:, R], float(TOPG), None, ALU.is_lt))
                ch.run(e.tensor_scalar(RK[:, R], GMK[:, R], 1.0, -MASKED, ALU.subtract, ALU.mult))
                def grp(v):
                    return v.rearrange("p t (g o) -> p t g o", o=1).broadcast_to([P, nt, NG, 8])
                sel = SEL[:, R].rearrange("p t (g n) -> p t g n", g=NG)
                ch.run(e.tensor_tensor(sel, sel, grp(GMK[:, R]), ALU.mult))
                ch.run(e.tensor_tensor(sel, sel, grp(RK[:, R]), ALU.add))
                for t in tiles:
                    ch.add(e.max(V8[:, t, :], SEL[:, t, :]))
                ch.sync()
                thr = V8[:, R, 7:8].broadcast_to([P, nt, NE])
                ch.add(e.tensor_tensor(MK[:, R], SEL[:, R], thr, ALU.is_gt))
                ch.run(e.tensor_tensor(EQ[:, R], SEL[:, R], thr, ALU.is_equal))
                ch.run(e.tensor_reduce(NGT[:, R], MK[:, R], AX.X, ALU.add))
                ch.run(e.tensor_scalar(NGT[:, R], NGT[:, R], -1.0, float(TOPK), ALU.mult, ALU.add))
                ones = cst("ones")[:, 0:NE]
                for t in tiles:
                    ch.add(e.tensor_tensor_scan(CUM[:, t, :], ones, EQ[:, t, :], 0.0, ALU.mult, ALU.add))
                ch.sync()
                ch.run(e.tensor_tensor(CUM[:, R], CUM[:, R], NGT[:, R].rearrange("p (t o) -> p t o", o=1).broadcast_to([P, nt, NE]), ALU.is_le))
                ch.run(e.tensor_tensor(EQ[:, R], EQ[:, R], CUM[:, R], ALU.mult))
                ch.run(e.tensor_tensor(MK[:, R], MK[:, R], EQ[:, R], ALU.add))
                e.sem_inc(s_m, 1)
                if 1 < nt:
                    shared_hidden(e, 1)
                ch.run(e.tensor_tensor(W[:, R], SC[:, R], MK[:, R], ALU.mult))
                ch.run(e.tensor_reduce(SUM[:, R], W[:, R], AX.X, ALU.add))
                ch.run(e.reciprocal(NGT[:, R], SUM[:, R]))
                ch.run(e.tensor_tensor(W[:, R], W[:, R], NGT[:, R].rearrange("p (t o) -> p t o", o=1).broadcast_to([P, nt, NE]), ALU.mult))
                ch.run(e.tensor_scalar(W[:, R], W[:, R], ROUTED_SCALE, None, ALU.mult))
                for t in tiles:
                    ch.add(e.tensor_tensor_scan(RM[:, t, :], ones, MK[:, t, :], 0.0, ALU.mult, ALU.add))
                ch.sync()
                ch.run(e.tensor_tensor(RM[:, R], RM[:, R], MK[:, R], ALU.mult))
                if 2 < nt:
                    shared_hidden(e, 2)
                for k in range(TOPK):
                    ch.run(e.scalar_tensor_tensor(out=TMP[:, R], in0=RM[:, R], scalar=float(k + 1), in1=W[:, R], op0=ALU.is_equal, op1=ALU.mult))
                    ch.run(e.tensor_reduce(WK[:, k, R], TMP[:, R], AX.X, ALU.add))
                if 3 < nt:
                    shared_hidden(e, 3)
                ch.run(e.tensor_scalar(RV[:, R], RM[:, R], float(T), -float(T + FAR), ALU.mult, ALU.add))
                ch.run(e.tensor_tensor(RV[:, R], RV[:, R], cst("tokid")[:, R].rearrange("p (t o) -> p t o", o=1).broadcast_to([P, nt, NE]), ALU.add))
                e.wait_ge(s_ct, 1)
                ch.run(e.tensor_copy(CNT, PS[:, 1, 256:256 + NE]))
                ch.run(e.tensor_scalar(NBK, CNT, 0.0, None, ALU.is_gt))
                for b in range(1, nt):
                    ch.run(e.scalar_tensor_tensor(out=NBK, in0=CNT, scalar=float(b * P), in1=NBK, op0=ALU.is_gt, op1=ALU.add))
                ch.run(e.tensor_tensor_scan(CB_, ones, NBK, 0.0, ALU.mult, ALU.add))
                ch.run(e.tensor_tensor(T64, CB_, NBK, ALU.subtract))
                ch.run(e.tensor_scalar(T64, T64, float(P), 1.0, ALU.mult, ALU.add))
                pos = PS[:, 1, t0 * NE:NT * NE].rearrange("p (t n) -> p t n", t=nt)
                ch.run(e.tensor_tensor(DEST[:, R], pos, tb(T64, NE), ALU.add))
                ch.run(e.tensor_tensor(DEST[:, R], DEST[:, R], MK[:, R], ALU.mult))
                ch.run(e.tensor_scalar(DEST[:, R], DEST[:, R], 1.0, None, ALU.subtract))
                ch.run(e.tensor_scalar(T64, CB_, cst("rowid"), None, ALU.is_le))
                ch.run(e.tensor_reduce(be, T64, AX.X, ALU.add))
                ch.run(e.tensor_scalar(be, be, float(NE - 1), None, ALU.min))
                ch.run(e.tensor_copy(BEI[:, :], be))
                ch.run(e.tensor_scalar(be, CB_[:, NE - 1:NE], 0.5, None, ALU.mult))
                ch.run(e.tensor_scalar(CNT[:, 0:NBLK // 2], cst("iota")[:, 0:NBLK // 2], be, None, ALU.is_lt))
                ch.run(e.tensor_reduce(n64, CNT[:, 0:NBLK // 2], AX.X, ALU.add))
                ch.run(e.tensor_copy(NPAIR[:, :], n64[0:1]))
                ch.run(e.memset(XG, 0.0))
                e.sem_inc(s_ti, 1)
            return dict(act=act, pe=pe, dve=dve)

        def expert_slot(q):
            flat = RING[:, :, :].rearrange("p s n -> p (s n)")[:, q * 6144:(q + 1) * 6144]
            return (flat[:, 0:2048].rearrange("p (k n) -> p k n", k=KT), flat[:, 2048:4096].rearrange("p (k n) -> p k n", k=KT),
                    flat[:, 4096:6144].rearrange("p (k n) -> p k n", k=2))

        def stage_experts(l, t0):
            m_ = moe[l] = {k: [sem(f"s_moe_{k}{q}") for q in range(2)] for k in MOE} | moe_dma[l]
            s_own = sem("s_moe_own")
            s_tick = sem("s_moe_tick")
            tiles = range(t0, NT)
            XT = ar(M0 + 2048, 2, KT, P)
            HB = ar(M0 + 4096, 2, FE)
            SGL = ar(M0 + 4608, 2, FE)
            HT = ar(M0 + 5120, 2, 2, P)
            YB = ar(M0 + 5632, 2, D)
            OH = ar(M0 + 7680, NT, P)
            DC = ar(M0 + 8192, NT)
            RC = ar(M0 + 8196, NT)
            LAST = ar(M0 + 8200, 1)

            def s(name, q):
                return m_[name][q]

            def pairs(e):
                return e.value_load(NPAIR[0:1, 0:1], min_val=1, max_val=NBLK // 2)

            def gather(e, q):
                e.indirect_dma_start(out=XG[:, q, :], out_offset=None, in_=u_d,
                                     in_offset=bass.IndirectOffsetOnAxis(ap=IXG[:, q:q + 1], axis=0),
                                     bounds_check=T - 1, oob_is_err=False).then_inc(s("xg", q), 16)

            def scatter(e, q):
                e.indirect_dma_start(out=y_d, out_offset=bass.IndirectOffsetOnAxis(ap=IXS[:, q:q + 1], axis=0),
                                     in_=YB[:, q, :], in_offset=None,
                                     bounds_check=TOPK * T - 1, oob_is_err=False).then_inc(s("sc", q), 16)

            def pool(e, ch):
                e.wait_ge(s_own, 4)
                for q in range(2):
                    scatter(e, q)
                for q in range(2):
                    e.wait_ge(s("ixd", q), 1)
                    gather(e, q)
                with e.Fori(0, pairs(e)) as i:
                    for q in range(2):
                        e.wait_ge(s("ixd", q), i + 2)
                        e.sem_inc(s_tick, 1)
                        gather(e, q)
                        e.wait_ge(s("ye", q), i * 2 + 4)
                        e.sem_inc(s_tick, 1)
                        scatter(e, q)

            def transposes(e, q):
                for k in range(KT):
                    mm = e.transpose(PS[:, k // 4, (k % 4) * P:(k % 4 + 1) * P], XG[:, q, k::KT], ident)
                mm.then_inc(s("tr", q), 1)

            def rows_of_slots(e, q):
                for t in tiles:
                    mm = e.matmul(PS[:, 6, 0:1], OH[:, t, :], RC[:, t:t + 1], start=t == t0, stop=t == NT - 1)
                mm.then_inc(s("ixp", q), 1)

            def pe(e):
                for q in range(2):
                    for x in ("gu", "ht", "y"):
                        e.sem_inc(s(x, q), 1)
                    e.wait_ge(s("oh", q), 1)
                    if q:
                        e.wait_ge(s("ixd", 0), 1)
                    rows_of_slots(e, q)
                e.wait_ge(s("xg", 0), 16)
                transposes(e, 0)
                with e.Fori(0, pairs(e)) as i:
                    for q in range(2):
                        wg, wu, wd = expert_slot(q)
                        e.wait_ge(s("xta", q), i + 1)
                        e.wait_ge(s("xtd", q), i + 1)
                        e.wait_ge(s("wl", q), i * 48 + 48)
                        e.wait_ge(s("h", 1 - q), i + 1 + q)
                        for k in range(KT):
                            e.matmul(PS[:, 2, 0:FE], XT[:, q, k, :], wg[:, k, :], start=k == 0, stop=k == KT - 1)
                        for k in range(KT):
                            mm = e.matmul(PS[:, 2, FE:2 * FE], XT[:, q, k, :], wu[:, k, :], start=k == 0, stop=k == KT - 1)
                        mm.then_inc(s("gu", q), 1)
                        e.wait_ge(s("xg", 1 - q), i * 16 + 16 * (q + 1))
                        transposes(e, 1 - q)
                        e.wait_ge(s("h", q), i + 2)
                        e.wait_ge(s("hte", 1 - q), i + 1 + q)
                        for k in range(2):
                            mm = e.transpose(PS[:, 3, k * P:(k + 1) * P], HB[:, q, k::2], ident)
                        mm.then_inc(s("ht", q), 1)
                        e.wait_ge(s("oh", q), i + 2)
                        e.wait_ge(s("ixd", 1 - q), i + 1 + q)
                        rows_of_slots(e, q)
                        e.wait_ge(s("hte", q), i + 2)
                        e.wait_ge(s("ye", 1 - q), i * 2 + 2 * q + 2)
                        for c in range(2):
                            for k in range(2):
                                mm = e.matmul(PS[:, 4 + c, :], HT[:, q, k, :], wd[:, k, c * 512:(c + 1) * 512], start=k == 0, stop=k == 1)
                        mm.then_inc(s("y", q), 1)

            def act(e, ch):
                def first_half(q):
                    return e.activation(XT[:, q, 0:4, :], PS[:, 0, :].rearrange("p (k n) -> p k n", k=4), ACT.Copy)
                for q in range(2):
                    e.sem_inc(s("hte", q), 1)
                    e.sem_inc(s("ye", q), 2)
                e.wait_ge(s("tr", 0), 1)
                first_half(0).then_inc(s("xta", 0), 1)
                with e.Fori(0, pairs(e)) as i:
                    for q in range(2):
                        e.wait_ge(s("gu", q), i + 2)
                        e.wait_ge(s("h", q), i + 1)
                        e.activation(SGL[:, q, :], PS[:, 2, 0:FE], ACT.Silu).then_inc(s("sg", q), 1)
                        e.wait_ge(s("tr", 1 - q), i + 1 + q)
                        e.wait_ge(s("gu", 1 - q), i + 1 + q)
                        first_half(1 - q).then_inc(s("xta", 1 - q), 1)
                        e.wait_ge(s("ht", q), i + 2)
                        e.wait_ge(s("y", q), i + 1)
                        e.activation(HT[:, q], PS[:, 3, 0:256].rearrange("p (k n) -> p k n", k=2), ACT.Copy).then_inc(s("hte", q), 1)
                        e.wait_ge(s("y", q), i + 2)
                        e.wait_ge(s("sc", q), i * 16 + 16)
                        e.activation(YB[:, q, 0:512], PS[:, 4, :], ACT.Copy).then_inc(s("ye", q), 1)
                n = pairs(e)
                for q in range(2):
                    e.wait_ge(s("xg", q), n * 16 + 16)
                    ch.run(e.activation(LAST, ident[:, 0:1], ACT.Copy))
                    e.wait_ge(s("sc", q), n * 16 + 16)
                    ch.run(e.activation(LAST, ident[:, 0:1], ACT.Copy))

            def dve(e, ch):

                def one_hot(q, blk, own):
                    x = e.value_load(EXPERT[0:1, bass.ds(blk, 1)], min_val=0, max_val=NE - 1)
                    e.tensor_tensor(DC[:, t0:NT].rearrange("p (t o) -> p t o", o=1), DEST[:, t0:NT, bass.ds(x, 1)],
                                    cst("blkbase")[:, bass.ds(blk, 1)].rearrange("p (t o) -> p t o", o=1).broadcast_to([P, len(tiles), 1]), ALU.subtract).then_inc(s_own, 1)
                    e.tensor_copy(RC[:, t0:NT].rearrange("p (t o) -> p t o", o=1), RV[:, t0:NT, bass.ds(x, 1)]).then_inc(s_own, 1)
                    e.wait_ge(s_own, own + 2)
                    for t in tiles:
                        mm = e.tensor_scalar(OH[:, t, :], cst("iota"), DC[:, t:t + 1], None, ALU.is_equal)
                    mm.then_inc(s("oh", q), 1)

                def indices(q, own):
                    e.tensor_scalar(IXV[:, q:q + 1], PS[:, 6, 0:1], float(FAR), None, ALU.add).then_inc(s_own, 1)
                    e.wait_ge(s_own, own + 1)
                    e.tensor_scalar(IXG[:, q:q + 1], IXV[:, q:q + 1], FAR | (T - 1), None, ALU.bitwise_and).then_inc(s("ixd", q), 1)

                def second_half(q):
                    return e.tensor_copy(XT[:, q, 4:8, :], PS[:, 1, :].rearrange("p (k n) -> p k n", k=4))
                for q in range(2):
                    e.sem_inc(s("h", q), 1)
                    e.memset(IXS[:, q:q + 1], FAR).then_inc(s_own, 1)
                    e.memset(YB[:, q, :], 0.0).then_inc(s_own, 1)
                for q in range(2):
                    if q:
                        e.wait_ge(s("ixp", 0), 1)
                    one_hot(q, q, 4 + 3 * q)
                    e.wait_ge(s("ixp", q), 1)
                    indices(q, 4 + 3 * q + 2)
                e.wait_ge(s("tr", 0), 1)
                second_half(0).then_inc(s("xtd", 0), 1)
                with e.Fori(0, pairs(e)) as i:
                    for q in range(2):
                        e.wait_ge(s("ixp", 1 - q), i + 1 + q)
                        one_hot(q, i * 2 + 2 + q, i * 8 + 10 + 4 * q)
                        e.wait_ge(s("sg", q), i + 1)
                        e.wait_ge(s("ht", q), i + 1)
                        e.tensor_tensor(HB[:, q, :], SGL[:, q, :], PS[:, 2, FE:2 * FE], ALU.mult).then_inc(s("h", q), 1)
                        e.wait_ge(s("tr", 1 - q), i + 1 + q)
                        e.wait_ge(s("gu", 1 - q), i + 1 + q)
                        second_half(1 - q).then_inc(s("xtd", 1 - q), 1)
                        e.wait_ge(s("sc", q), i * 16 + 16)
                        e.wait_ge(s("xg", q), i * 16 + 16)
                        e.tensor_copy(IXS[:, q:q + 1], IXV[:, q:q + 1]).then_inc(s_own, 1)
                        e.wait_ge(s_own, i * 8 + 13 + 4 * q)
                        e.wait_ge(s("ixp", q), i + 2)
                        indices(q, i * 8 + 13 + 4 * q)
                        e.wait_ge(s("y", q), i + 2)
                        e.tensor_copy(YB[:, q, 512:1024], PS[:, 5, :]).then_inc(s("ye", q), 1)
            return dict(act=act, pe=pe, dve=dve, pool=pool)

        def load_experts(sp, l, done):
            m_ = moe[l]
            sp.wait_ge(s_wfree, done)
            n = sp.value_load(NPAIR[0:1, 0:1], min_val=1, max_val=NBLK // 2)
            with sp.Fori(0, n) as i:
                for q in range(2):
                    x = sp.value_load(EXPERT[0:1, bass.ds(i * 2 + q, 1)], min_val=0, max_val=NE - 1)
                    sp.wait_ge(m_["y"][q], i + 1)
                    for dst, w, k in zip(expert_slot(q), ("w_exp_gate", "w_exp_up", "w_exp_down"), (KT, KT, 2)):
                        sp.dma_start(dst, a[w][l, bass.ds(x, 1)].rearrange("o (p k) n -> p (o k) n", k=k)).then_inc(m_["wl"][q], 16)

        def stage_combine(l, t0):
            ahead = l < depth - 1
            if ahead:
                mod_begin, mod_end, mod_pe, add_bias = mod_parts(l + 1)
            nm = f"s_cb_"
            s_ld, s_y, s_dn, s_var, s_std, s_nx, s_out = (sem(nm + x) for x in ("ld", "y", "dn", "var", "std", "nx", "out"))
            NB, KB = 2, 4
            s_yr = [sem(f"{nm}yr{i}") for i in range(NB)]
            YR = ar(M0, NB, KB, D)
            GM = ar(M0 + NB * KB * D, 2, 1, D)
            LNB = ar(M0 + NB * KB * D + 2 * D, 2, D)
            tiles = range(t0, NT)
            nt = len(tiles)
            items = [(t, k) for t in tiles for k in range(0, TOPK, KB)]

            def act(e, ch):
                if ahead:
                    mod_begin(e)
                rooted = 0
                for i, (t, k) in enumerate(items):
                    while KB * (i - NB + 1) >= TOPK * (rooted + 1) + 2:
                        root(e, rooted, s_var, s_std)
                        rooted += 1
                    if i >= NB:
                        e.wait_ge(s_dn, KB * (i - NB + 1))
                    e.dma_start(YR[:, i % NB], y_d.rearrange("(k t) d -> t k d", k=TOPK)[t * P:(t + 1) * P, k:k + KB, :]).then_inc(s_yr[i % NB], 16)
                    if i == 1:
                        modulation(e, l, (5,), GM, s_ld, range(t0 // 2, 2))
                        for j, nm_ in enumerate(("ln2_g", "ln2_b")):
                            e.dma_start(LNB[:, j, :], a[nm_][l:l + 1, :].broadcast_to([P, D])).then_inc(s_ld, 16)
                for i in range(rooted, nt - 1):
                    root(e, i, s_var, s_std)
                root(e, nt - 1, s_var, s_std)
                if ahead:
                    mod_end(e)
                    modulation(e, l + 1, (0, 1), ar(B0 + 10240, 2, 2, D), s_ahead, range(2))
                if l == depth - 1:
                    e.wait_ge(s_y, 1)
                    e.dma_start(out[0].rearrange("(t p) d -> p t d", p=P), X[:, 2:4, :]).then_inc(s_out, 16)
                    e.wait_ge(s_out, 16)

            def dve(e, ch):
                for i, (t, k) in enumerate((t, k) for t in tiles for k in range(TOPK)):
                    b = i // KB
                    e.wait_ge(s_yr[b % NB], 16 * (b // NB + 1))
                    if i:
                        e.wait_ge(s_dn, i)
                    e.scalar_tensor_tensor(out=FS[:, t, :], in0=YR[:, b % NB, i % KB, :], scalar=WK[:, k, t:t + 1], in1=FS[:, t, :], op0=ALU.mult, op1=ALU.add).then_inc(s_dn, 1)
                    if k == TOPK - 1:
                        e.wait_ge(s_dn, i + 1)
                        if t == t0:
                            e.wait_ge(s_ld, 64 if t0 == 0 else 48)
                        ch.run(e.tensor_tensor(FS[:, t, :], FS[:, t, :], GM[:, t // 2, 0, :], ALU.mult))
                        ch.run(e.scalar_tensor_tensor(out=X[:, t, :], in0=X[:, t, :], scalar=ALPHA, in1=FS[:, t, :], op0=ALU.mult, op1=ALU.add))
                        ln_stats(e, ch, t, t - t0, s_var)
                    if ahead and i >= 8 and i % 2 == 0:
                        add_bias(e, i // 2 - 4)
                    if k == 1 and t > t0:
                        ln_scale(e, ch, t - 1, t - 1 - t0, s_std, s_nx)
                ln_scale(e, ch, NT - 1, nt - 1, s_std, s_nx)

            def pool(e, ch):
                e.wait_ge(s_ld, 64 if t0 == 0 else 48)
                ln_gains(e, ch, tiles, LNB, s_nx)
                e.sem_inc(s_y, 1)
            return dict(act=act, dve=dve, pool=pool) | (dict(pe=mod_pe) if ahead else {})

        def phase(*made):
            taken.clear()
            phases.append([(name, f(*args)) for name, f, *args in made])

        for l in range(depth):
            t0 = 0 if l < DEPTH - 1 else 2
            if l == 0:
                phase(("mod", stage_mod))
            phase((f"u{l}", stage_u, l, False, 0), (f"z{l}", stage_z, l, t0),
                  (f"mla{l}", stage_mla, l, t0), (f"matt{l}", stage_attend, l, False, t0),
                  (f"gqa{l}", stage_gqa, l, t0), (f"gatt{l}", stage_attend, l, True, t0))
            phase((f"dnp{l}", stage_dn_prep, l, t0), (f"dns{l}", stage_dn_scan, l, t0), (f"dno{l}", stage_dn_out, l, t0))
            phase((f"mrg{l}", stage_merge, l, t0), (f"uf{l}", stage_u, l, True, t0), (f"rt{l}", stage_route, l, t0))
            phase((f"ex{l}", stage_experts, l, t0), (f"cb{l}", stage_combine, l, t0))
        stage_of_experts = {f"ex{l}": l for l in range(depth)}
        last_of = {l: n for n, l in moe_after.items()}
        uses = {"mod": 12, "z": len(ZCH), "mla": 1, "dnp": 3, "mrg": 11, "rt": 3}
        sent = ended = 0
        met = {}

        def barrier(e, who):
            met[who] = met.get(who, 0) + 1
            e.drain().then_inc(s_bar, 1)
            e.wait_ge(s_bar, 5 * met[who])

        def send(sp, upto):
            nonlocal sent
            for n in range(sent, upto):
                if n >= 3:
                    sp.wait_ge(s_wfree, n - 2)
                for off, src, k, w in plan[n]:
                    dst = RING[:, n % 3, off:off + k * w].rearrange("p (k n) -> p k n", k=k)
                    sp.dma_start(dst, src).then_inc(s_slot[n % 3], 16)
            sent = max(sent, upto)

        chains = {"act": Chain(nc.scalar, s_act), "dve": Chain(nc.vector, s_dve), "pool": Chain(nc.gpsimd, s_pool)}

        def run_phase(e, which, n):
            for name, st in phases[n]:
                if which in st:
                    st[which](e, chains[which]) if which in chains else st[which](e)
                if name[:-1] != "u":
                    barrier(e, which)

        def run_sync(sp, n):
            nonlocal ended
            if n == 0:
                send(sp, 3)
                for i in range(4):
                    sp.dma_start(X[:, i, :], (a["ctx"][0], a["x"][0])[i // 2][(i % 2) * P:(i % 2 + 1) * P, :]).then_inc(s_const, 16)
                sp.dma_start(CB[:, :], a["const"]).then_inc(s_const, 16)
            for name, st in phases[n]:
                if name in stage_of_experts:
                    load_experts(sp, stage_of_experts[name], last_of[stage_of_experts[name]])
                else:
                    ended += uses.get(name if name == "mod" else name[:-1], 0) + (12 if name[:-1] == "cb" and name != f"cb{depth - 1}" else 0)
                    send(sp, min([ended + 3, len(plan)] + [b for b in moe_after if b >= ended and (b > ended or name[:-1] != "cb")]))
                if name == "mod":
                    sp.wait_ge(s_const, 80)
                if name[:-1] != "u":
                    barrier(sp, "sp")
        for n in range(len(phases)):
            if n:
                nc.all_engine_barrier(sems_to_clear=range(shared[0].num, shared[-1].num + 1))
            with nc.Block() as block:
                @block.sync
                def _(sp):
                    run_sync(sp, n)

                @block.gpsimd
                def _(pool):
                    run_phase(pool, "pool", n)

                @block.scalar
                def _(act):
                    run_phase(act, "act", n)

                @block.tensor
                def _(pe):
                    run_phase(pe, "pe", n)

                @block.vector
                def _(dve):
                    run_phase(dve, "dve", n)


_INS = ["x", "c", "ctx", "c_ctx", "w_ada", "b_ada", "w_in", "mla_q_norm", "mla_kv_norm", "w_uq", "w_ukv",
        "dn_conv", "dn_a_log", "dn_dt_bias", "dn_norm", "gqa_sink", "w_o_mla", "w_o_dn", "w_o_gqa", "w_out",
        "ln1_g", "ln1_b", "w_router", "router_bias", "w_exp_gate", "w_exp_up", "w_exp_down",
        "w_sh_gate", "w_sh_up", "w_sh_down", "ln2_g", "ln2_b"]


def kernel(**inputs):
    import numpy as _np
    import concourse.bacc as _bacc
    from concourse import mybir as _mybir
    from concourse.bass_utils import run_bass_kernel_spmd as _run

    nc = _bacc.Bacc("TRN2", target_bir_lowering=False, num_devices=1)
    arrays, aps = {}, {}
    for name in _INS:
        v = _np.ascontiguousarray(inputs[name])
        arrays[f"in_{name}"] = v
        aps[name] = nc.dram_tensor(f"in_{name}", v.shape, _mybir.dt.from_np(v.dtype), kind="ExternalInput").ap()
    arrays["in_const"] = CONST
    aps["const"] = nc.dram_tensor("in_const", CONST.shape, F32, kind="ExternalInput").ap()
    out = nc.dram_tensor("out_0", (1, SEG, D), F32, kind="ExternalOutput").ap()
    trunk(nc, aps, out)
    r = _run(nc, [arrays], core_ids=[0])
    return r.results[0]["out_0"]
```
